# Optimizing a Trainium2 kernel written in Bass

```python
import math
import jax, jax.numpy as jnp
from jax import lax
import numpy as np

D_MODEL = 1024
BATCH = 1
SEQ = 4096
DEPTH = 1

CHUNK = 64
D_MIX = D_MODEL
D_RNN = D_MIX // 2
N_RNN_BLOCKS = 8
RNN_BLOCK = D_RNN // N_RNN_BLOCKS
CONV_WIDTH = 4
LRU_C = 8.0
D_ATTN = D_MIX - D_RNN
HEAD_DIM = 64
N_Q_HEADS = D_ATTN // HEAD_DIM
N_KV_HEADS = 2
KV_DIM = N_KV_HEADS * HEAD_DIM
WINDOW = 128
WIN_CHUNKS = WINDOW // CHUNK
N_GROUPS = 4
EXPERTS_PER_GROUP = 8
N_EXPERTS = N_GROUPS * EXPERTS_PER_GROUP
TOP_K = 2
D_EXPERT = 256
MOE_BLOCK = 128
EPS = 1e-6
D_IN = 2 * D_RNN + D_ATTN + 2 * KV_DIM
SPLITS = [D_RNN, 2 * D_RNN, 2 * D_RNN + D_ATTN, 2 * D_RNN + D_ATTN + KV_DIM]

kernel_name = "hymba_rglru_swa_sink_hiermoe"

def rms_norm(x, g):
    xf = x.astype(jnp.float32)
    y = xf * lax.rsqrt(jnp.mean(xf * xf, axis=-1, keepdims=True) + EPS)
    return (y * g.astype(jnp.float32)).astype(x.dtype)

def causal_depthwise_conv(u, w, b):
    S = u.shape[1]
    up = jnp.pad(u, ((0, 0), (CONV_WIDTH - 1, 0), (0, 0)))
    out = b
    for k in range(CONV_WIDTH):
        out = out + up[:, k:k + S, :] * w[k]
    return out

def rg_lru(u, w_rg, b_rg, w_ig, b_ig, lam):
    B, S, _ = u.shape
    f32 = jnp.float32
    uf = u.astype(f32)
    ub = uf.reshape(B, S, N_RNN_BLOCKS, RNN_BLOCK)
    r = jax.nn.sigmoid(jnp.einsum('bsnc,ncd->bsnd', ub, w_rg.astype(f32)).reshape(B, S, D_RNN) + b_rg.astype(f32))
    i = jax.nn.sigmoid(jnp.einsum('bsnc,ncd->bsnd', ub, w_ig.astype(f32)).reshape(B, S, D_RNN) + b_ig.astype(f32))
    log_a = -LRU_C * r * jax.nn.softplus(-lam.astype(f32))
    a = jnp.exp(log_a)
    gated = jnp.sqrt(-jnp.expm1(2.0 * log_a)) * (i * uf)

    def combine(left, right):
        a1, b1 = left
        a2, b2 = right
        return a1 * a2, a2 * b1 + b2

    _, h = lax.associative_scan(combine, (a, gated), axis=1)
    return h

def sliding_window_attention(q, k, v, sinks):
    B, S, _ = q.shape
    nC = S // CHUNK
    G = N_Q_HEADS // N_KV_HEADS
    f32 = jnp.float32
    qc = q.astype(f32).reshape(B, nC, CHUNK, N_KV_HEADS, G, HEAD_DIM)

    def band(t):
        tc = t.astype(f32).reshape(B, nC, CHUNK, N_KV_HEADS, HEAD_DIM)
        tp = jnp.pad(tc, ((0, 0), (WIN_CHUNKS - 1, 0), (0, 0), (0, 0), (0, 0)))
        return jnp.concatenate([tp[:, j:j + nC] for j in range(WIN_CHUNKS)], axis=2)

    kb, vb = band(k), band(v)
    s = jnp.einsum('bnqhgd,bnkhd->bnhgqk', qc, kb) * (1.0 / math.sqrt(HEAD_DIM))
    slopes = 2.0 ** (-8.0 * jnp.arange(1, N_Q_HEADS + 1, dtype=f32) / N_Q_HEADS)
    qi = jnp.arange(CHUNK)
    kj = jnp.arange(WIN_CHUNKS * CHUNK)
    dist = jnp.abs(qi[:, None] - kj[None, :] + (WIN_CHUNKS - 1) * CHUNK).astype(f32)
    bias = -slopes.reshape(N_KV_HEADS, G)[:, :, None, None] * dist
    key_chunk = jnp.arange(nC)[:, None] - (WIN_CHUNKS - 1) + kj[None, :] // CHUNK
    valid = key_chunk >= 0
    s = jnp.where(valid[None, :, None, None, None, :], s + bias, -jnp.inf)
    sink = sinks.astype(f32).reshape(N_KV_HEADS, G)[None, None, :, :, None, None]
    m = jnp.maximum(jnp.max(s, axis=-1, keepdims=True), sink)
    p = jnp.exp(s - m)
    p = p / (jnp.sum(p, axis=-1, keepdims=True) + jnp.exp(sink - m))
    o = jnp.einsum('bnhgqk,bnkhd->bnqhgd', p, vb)
    return o.reshape(B, S, N_Q_HEADS * HEAD_DIM)

def hierarchical_moe(xt, w_group_router, w_expert_router, w_gate, w_up, w_down):
    T, D = xt.shape
    f32 = jnp.float32
    xf = xt.astype(f32)
    g_prob = jax.nn.softmax(xf @ w_group_router.astype(f32), axis=-1)
    g_w, g_idx = lax.top_k(g_prob, 1)
    e_logits = (xf @ w_expert_router.astype(f32)).reshape(T, N_GROUPS, EXPERTS_PER_GROUP)
    e_sel = jnp.take_along_axis(e_logits, g_idx[:, :, None], axis=1)[:, 0]
    e_w, e_idx = lax.top_k(jax.nn.softmax(e_sel, axis=-1), TOP_K)
    e_w = e_w / jnp.sum(e_w, axis=-1, keepdims=True)
    weights = (g_w * e_w).reshape(-1)
    experts = (g_idx * EXPERTS_PER_GROUP + e_idx).reshape(-1)
    tokens = jnp.repeat(jnp.arange(T, dtype=jnp.int32), TOP_K)
    TK = T * TOP_K
    order = jnp.argsort(experts)
    e_s, t_s, w_s = experts[order], tokens[order], weights[order]
    counts = jnp.bincount(experts, length=N_EXPERTS)
    starts = jnp.cumsum(counts) - counts
    padded = (counts + MOE_BLOCK - 1) // MOE_BLOCK * MOE_BLOCK
    pad_end = jnp.cumsum(padded)
    pad_start = pad_end - padded
    dest = pad_start[e_s] + jnp.arange(TK) - starts[e_s]
    P = ((TK + MOE_BLOCK - 1) // MOE_BLOCK) * MOE_BLOCK + N_EXPERTS * MOE_BLOCK
    n_blocks = P // MOE_BLOCK
    row_tok = jnp.zeros((P,), jnp.int32).at[dest].set(t_s)
    row_w = jnp.zeros((P,), f32).at[dest].set(w_s)
    block_start = jnp.arange(n_blocks) * MOE_BLOCK
    block_exp = jnp.minimum(jnp.searchsorted(pad_end, block_start, side='right'), N_EXPERTS - 1)
    xb = xt[row_tok].reshape(n_blocks, MOE_BLOCK, D)

    def expert_block(args):
        xblk, e = args
        hid = jax.nn.silu(xblk @ w_gate[e]) * (xblk @ w_up[e])
        return hid @ w_down[e]

    yb = lax.map(expert_block, (xb, block_exp))
    y = yb.reshape(P, D) * row_w[:, None].astype(xt.dtype)
    return jnp.zeros_like(xt).at[row_tok].add(y)

def setup_inputs(seed: int = 0) -> dict:
    key = jax.random.key(seed)
    ks = jax.random.split(key, 24)
    f32 = jnp.float32
    L = DEPTH

    def nrm(k, shape, scale):
        return jax.random.normal(k, shape, f32) * scale

    v = jax.random.uniform(ks[9], (L, D_RNN), f32, 0.9, 0.999)
    s_lam = v ** (1.0 / LRU_C)
    lru_lambda = jnp.log(s_lam) - jnp.log1p(-s_lam)
    return {
        "x": nrm(ks[0], (BATCH, SEQ, D_MODEL), 1.0),
        "norm1_g": 1.0 + nrm(ks[1], (L, D_MODEL), 0.02),
        "w_in": nrm(ks[2], (L, D_MODEL, D_IN), D_MODEL ** -0.5),
        "conv_w": nrm(ks[3], (L, CONV_WIDTH, D_RNN), CONV_WIDTH ** -0.5),
        "conv_b": nrm(ks[4], (L, D_RNN), 0.01),
        "w_rg": nrm(ks[5], (L, N_RNN_BLOCKS, RNN_BLOCK, RNN_BLOCK), RNN_BLOCK ** -0.5),
        "b_rg": nrm(ks[6], (L, D_RNN), 0.01),
        "w_ig": nrm(ks[7], (L, N_RNN_BLOCKS, RNN_BLOCK, RNN_BLOCK), RNN_BLOCK ** -0.5),
        "b_ig": nrm(ks[8], (L, D_RNN), 0.01),
        "lru_lambda": lru_lambda,
        "attn_sinks": nrm(ks[10], (L, N_Q_HEADS), 0.5),
        "rnn_out_g": 1.0 + nrm(ks[11], (L, D_RNN), 0.02),
        "attn_out_g": 1.0 + nrm(ks[12], (L, D_ATTN), 0.02),
        "w_out": nrm(ks[13], (L, D_MIX, D_MODEL), D_MIX ** -0.5),
        "norm2_g": 1.0 + nrm(ks[14], (L, D_MODEL), 0.02),
        "w_group_router": nrm(ks[15], (L, D_MODEL, N_GROUPS), D_MODEL ** -0.5),
        "w_expert_router": nrm(ks[16], (L, D_MODEL, N_EXPERTS), D_MODEL ** -0.5),
        "w_gate": nrm(ks[17], (L, N_EXPERTS, D_MODEL, D_EXPERT), D_MODEL ** -0.5),
        "w_up": nrm(ks[18], (L, N_EXPERTS, D_MODEL, D_EXPERT), D_MODEL ** -0.5),
        "w_down": nrm(ks[19], (L, N_EXPERTS, D_EXPERT, D_MODEL), D_EXPERT ** -0.5),
        "final_g": 1.0 + nrm(ks[20], (D_MODEL,), 0.02),
    }

def reference(x, norm1_g, w_in, conv_w, conv_b, w_rg, b_rg, w_ig, b_ig, lru_lambda,
              attn_sinks, rnn_out_g, attn_out_g, w_out, norm2_g, w_group_router,
              w_expert_router, w_gate, w_up, w_down, final_g):
    B, S, D = x.shape
    h = x
    for l in range(DEPTH):
        u = rms_norm(h, norm1_g[l])
        proj = u @ w_in[l]
        xr, yr, q, k, v = jnp.split(proj, SPLITS, axis=-1)
        xc = causal_depthwise_conv(xr, conv_w[l], conv_b[l])
        rnn = rg_lru(xc, w_rg[l], b_rg[l], w_ig[l], b_ig[l], lru_lambda[l])
        rnn = (rnn * jax.nn.gelu(yr.astype(jnp.float32))).astype(h.dtype)
        att = sliding_window_attention(q, k, v, attn_sinks[l]).astype(h.dtype)
        mix = jnp.concatenate([rms_norm(rnn, rnn_out_g[l]), rms_norm(att, attn_out_g[l])], axis=-1)
        h = h + mix @ w_out[l]
        u2 = rms_norm(h, norm2_g[l])
        y = hierarchical_moe(u2.reshape(B * S, D), w_group_router[l], w_expert_router[l],
                             w_gate[l], w_up[l], w_down[l])
        h = h + y.reshape(B, S, D)
    return rms_norm(h, final_g)


_drawn_inputs = setup_inputs


def setup_inputs(seed=0):
    import zlib

    import numpy as np

    out = dict(_drawn_inputs(seed))
    spreads = {}
    factors = {'b_rg': 27.05,
     'b_ig': 24.146,
     'rnn_out_g': 12.227,
     'attn_out_g': 12.137,
     'final_g': 8.795,
     'norm2_g': 6.341}
    for name, (base, spread) in spreads.items():
        noise = np.random.default_rng([zlib.crc32(name.encode()), seed]).standard_normal(out[name].shape)
        drawn = base * np.exp(spread * noise) if base else spread * noise
        out[name] = __import__('jax').numpy.asarray(drawn.astype(out[name].dtype))
    for name, factor in factors.items():
        out[name] = (out[name] * factor).astype(out[name].dtype)
    return out
```

```python
from contextlib import ExitStack

import numpy as np

import concourse.bass as bass
from concourse import mybir

ALU = mybir.AluOpType
ACT = mybir.ActivationFunctionType
AX = mybir.AxisListType
F32 = mybir.dt.float32
F32R = mybir.dt.float32r
BF16 = mybir.dt.bfloat16
I32 = mybir.dt.int32
U32 = mybir.dt.uint32

P = 128
D = 1024
KD = D // P
T = 4096
EPS = 1e-6
D_RNN = 512
RC = D_RNN // P
CONV = 4
LRU_C = 8.0
CHUNK = 64
HEADS, KV, HD = 8, 2, 64
G = HEADS // KV
D_ATTN = HEADS * HD
D_IN = 2 * D_RNN + D_ATTN + 2 * KV * HD
Q0, K0, V0 = 2 * D_RNN, 2 * D_RNN + D_ATTN, 2 * D_RNN + D_ATTN + KV * HD
GROUPS, EPG = 4, 8
E = GROUPS * EPG
TOP = 2
F = 256
FC = F // P
NEG = -1e30

TOK = 256
NG = T // TOK
TJ = TOK // P
NT = T // P
LIST = T + P
NB = T * TOP // P + E - 1
NBLK = NB + NB % 2
GELU_K, GELU_C = (2 / np.pi) ** 0.5, 0.044715


class Signal:

    def __init__(self, ctx, nc, name, per, base=0, step=1):
        self.sem, self.per, self.base, self.step = ctx.enter_context(nc.semaphore(name)), per, base, step

    def wait(self, eng, g, n):
        value = (g * self.per + (self.base + n)) * self.step
        if not isinstance(value, int) or value > 0:
            eng.wait_ge(self.sem, value)

    def by(self, ins):
        ins.then_inc(self.sem, self.step)


class Chain:

    def __init__(self, ctx, nc, name, per=0):
        self.sem, self.per, self.before, self.n, self.g = ctx.enter_context(nc.semaphore(name)), per, 0, 0, None

    def step(self, ins):
        ins.then_inc(self.sem, 1)
        self.n += 1

    def enter(self, g):
        self.before, self.n, self.g = self.before + self.n, 0, g

    def leave(self):
        assert self.n == self.per, (self.n, self.per)

    def wait(self, eng):
        if self.g is None:
            eng.wait_ge(self.sem, self.before + self.n)
        else:
            eng.wait_ge(self.sem, self.g * self.per + (self.before + self.n))


def product3(pe, out, w_hi, w_lo, x_hi, x_lo, first, last):
    pe.matmul(out, w_lo, x_hi, start=first, stop=False)
    pe.matmul(out, w_hi, x_lo, start=False, stop=False)
    return pe.matmul(out, w_hi, x_hi, start=False, stop=last)


def project_and_mix(nc, x, norm1_g, w_in, conv_w, conv_b, w_rg, b_rg, w_ig, b_ig, lru_lambda, attn_sinks, mixT):
    with ExitStack() as ctx:
        def sb(name, shape, dt=F32):
            return ctx.enter_context(nc.sbuf_tensor(name, shape, dt))

        def ps(name, shape):
            return ctx.enter_context(nc.psum_tensor(name, shape, F32))

        def sig(name, per, base=0, step=1):
            return Signal(ctx, nc, name, per, base, step)

        w_hi, w_lo = sb("w_hi", [P, KD, D_IN], F32R), sb("w_lo", [P, KD, D_IN], F32R)
        u_hi, u_lo = sb("u_hi", [P, KD, TOK], F32R), sb("u_lo", [P, KD, TOK], F32R)
        xt = sb("xt", [P, TJ, D])
        xr = sb("xr", [P, RC, CONV - 1 + TOK])
        yg = sb("yg", [P, RC, TOK])
        t1 = sb("t1", [P, RC, TOK])
        xc = sb("xc", [P, RC, TOK])
        rr = sb("rr", [P, RC, TOK])
        ig = sb("ig", [P, RC, TOK])
        qT = sb("qT", [P, G, TOK])
        kT, vT = sb("kT", [P, CHUNK + TOK]), sb("vT", [P, CHUNK + TOK])
        vb = sb("vb", [P, TOK // CHUNK, P])
        ss = sb("ss", [P, TJ, HEADS, P])
        stage = [ss[:, b].rearrange("p h n -> p (h n)")[:, 0:D_IN // 2] for b in range(2)]
        pT = sb("pT", [P, HEADS, P])
        bT = sb("bT", [P, G, TOK])
        bias = sb("bias", [P, 2, HEADS, P])
        wg = sb("wg", [P, RC, 2, P])
        ident = sb("ident", [P, P])
        g1 = sb("g1", [P, KD])
        cw, cb = sb("cw", [P, CONV, RC]), sb("cb", [P, RC])
        brg, big, lam = sb("brg", [P, RC]), sb("big", [P, RC]), sb("lam", [P, RC])
        la, lb, lc, ld, le = (sb(n, [P, RC]) for n in ("la", "lb", "lc", "ld", "le"))
        sp4 = sb("sp4", [P, RC])
        sink, neg_sink = sb("sink", [P, HEADS]), sb("neg_sink", [P, HEADS])
        carry = sb("carry", [P, RC])
        ssq, rstd = sb("ssq", [P, TJ]), sb("rstd", [P, TJ])
        eps = sb("eps", [P, 1])
        mx, nm, sd, den, rs = (sb(n, [P, HEADS]) for n in ("mx", "nm", "sd", "den", "rs"))

        bank = [ps(f"proj{b}", [P, 512]) for b in range(2)]
        tp = ps("tp", [P, KD, P])
        sc = ps("sc", [P, HEADS, P])
        gt = ps("gt", [P, 2, TOK])
        ot = ps("ot", [P, G, P])

        NCH = D_IN // P

        def w_cols(w, k, m):
            if m < 2:
                c0 = (V0, K0)[m]
            elif m < 2 + G:
                c0 = Q0 + (m - 2) * P
            else:
                c0 = (m - 2 - G) * P
            return w[:, k, c0:c0 + P]

        consts_in = sig("consts_in", 0)
        gate_w_zero, const_ready = sig("gate_w_zero", 0), sig("const_ready", 0)
        tables_ready, lambda_abs, lambda_exp = sig("tables_ready", 0), sig("lambda_abs", 0), sig("lambda_exp", 0)
        w_staged = [sig("w_staged0", 1, step=16), sig("w_staged1", 1, step=4 * 16)]
        w_hi_done, w_lo_done = sig("w_hi_done", 2), sig("w_lo_done", 2)
        x_in = [sig(f"x_in{j}", 1, 1, 16) for j in range(TJ)]
        x_squared, rms_done, x_scaled = sig("x_squared", TJ, TJ), sig("rms_done", 1, 1), sig("x_scaled", TJ, TJ)
        u_transposed = sig("u_transposed", TJ, TJ)
        u_hi_done, u_lo_done = sig("u_hi_done", TJ, TJ), sig("u_lo_done", TJ, TJ)
        v_transposed, v_taken = sig("v_transposed", 1), sig("v_taken", 1)
        p_transposed, p_taken = sig("p_transposed", TJ), sig("p_taken", TJ)
        projected, proj_taken = sig("projected", NCH), sig("proj_taken", NCH, 2)
        scored, scores_taken = sig("scored", TJ), sig("scores_taken", TJ, 1)
        smax_done, exp_done, p_ready = sig("smax_done", TJ), sig("exp_done", TJ), sig("p_ready", TJ)
        pv_done, ot_taken = sig("pv_done", TJ, 1), sig("ot_taken", TJ, 1)
        conv_done, xr_free = sig("conv_done", RC), sig("xr_free", 1, 1)
        gelu_sq, gelu_poly, gelu_sig, gelu_done = (sig(f"gelu_{n}", 1) for n in ("sq", "poly", "sig", "done"))
        gated, gates_taken = sig("gated", RC), sig("gates_taken", RC, 1)
        s_done, sqrt_done, rnn_done = sig("s_done", 1), sig("sqrt_done", 1), sig("rnn_done", 1, 1)
        a_stored, b_stored = sig("a_stored", 1, 1, 16), sig("b_stored", 1, 1, 16)
        stores_begun = sig("stores_begun", 2)
        step = Chain(ctx, nc, "dve_step", 4 * TJ + 3 * RC + 12)

        NCONST, CONST_STEPS = 6 + CONV + 4, 9
        x_tiles = x.rearrange("(t p) n -> t p n", p=P)
        mix_rows = mixT.rearrange("c p t -> p c t")
        block = ctx.enter_context(nc.Block())

        @block.sync
        def _(sp):
            w_rows = w_in[0].rearrange("(k p) n -> k p n", p=P)
            cut = D_IN // 2

            def stage_w(k, b):
                if b == 0:
                    w_staged[0].by(sp.dma_start(stage[0], w_rows[k, :, 0:cut]))
                    return
                pieces = [(stage[1][:, 0:Q0 - cut], w_rows[k, :, cut:Q0]),
                          (stage[1][:, K0 - cut:], w_rows[k, :, K0:])]
                for v in range(KV):
                    pieces.append((stage[1][:, Q0 - cut:K0 - cut].rearrange("p (c v d) -> p v c d", c=G, v=KV)[:, v],
                                   w_rows[k, :, Q0 + v * G * HD:Q0 + (v + 1) * G * HD]
                                   .rearrange("p (c d) -> p c d", c=G)))
                for dst, src in pieces:
                    sp.dma_start(dst, src).then_inc(w_staged[1].sem, 16)

            for b in range(2):
                stage_w(0, b)
            for dst, src in ((g1, norm1_g), (cb, conv_b), (brg, b_rg), (big, b_ig), (lam, lru_lambda)):
                sp.dma_start(dst[:], src[0].rearrange("(c p) -> p c", p=P),
                             allow_slow_non_contiguous=True).then_inc(consts_in.sem, 16)
            sp.dma_start(sink[:], attn_sinks[0].partition_broadcast(P)).then_inc(consts_in.sem, 16)
            for k in range(CONV):
                sp.dma_start(cw[:, k, :], conv_w[0, k].rearrange("(c p) -> p c", p=P),
                             allow_slow_non_contiguous=True).then_inc(consts_in.sem, 16)
            for j in range(TJ):
                x_in[j].by(sp.dma_start(xt[:, j], x_tiles[j]))
            sp.wait_ge(gate_w_zero.sem, 1)
            for s, w in enumerate((w_rg, w_ig)):
                for half in range(2):
                    sp.dma_start(wg[64 * half:64 * half + 64, :, s, 64 * half:64 * half + 64],
                                 w[0].rearrange("(c h) i o -> h i c o", h=2)[half]).then_inc(consts_in.sem, 16)
            with sp.Fori(1, KD) as k:
                for b in range(2):
                    w_lo_done.wait(sp, k, b - 1)
                    stage_w(k, b)
            sp.sem_inc(a_stored.sem, 16)
            sp.sem_inc(b_stored.sem, 16)
            with sp.Fori(0, NG) as g:
                nxt = sp.snap((g + 1) % NG)
                for j in range(TJ):
                    u_transposed.wait(sp, g, j + 1 - TJ)
                    x_in[j].by(sp.dma_start(xt[:, j], x_tiles[nxt * TJ + j]))
                ot_taken.wait(sp, g, TJ)
                sp.sem_inc(stores_begun.sem, 1)
                b_stored.by(sp.dma_start(mix_rows[:, RC:, bass.ds(g * TOK, TOK)], bT[:]))
                rnn_done.wait(sp, g, 1)
                sp.sem_inc(stores_begun.sem, 1)
                a_stored.by(sp.dma_start(mix_rows[:, 0:RC, bass.ds(g * TOK, TOK)], yg[:]))
            for s in (x_in[0], x_in[1], a_stored, b_stored):
                sp.wait_ge(s.sem, 16 * (NG + 1))

        @block.gpsimd
        def _(pool):
            pool.memset(wg[:], 0.0).then_inc(gate_w_zero.sem, 1)
            pool.memset(ident[:], 0.0).then_inc(const_ready.sem, 1)
            pool.wait_ge(const_ready.sem, 1)
            pool.affine_select(out=ident[:], in_=ident[:], compare_op=ALU.not_equal, fill=1.0, base=0,
                               pattern=[[-1, P]], channel_multiplier=1).then_inc(const_ready.sem, 1)
            pool.memset(eps[:], EPS).then_inc(const_ready.sem, 1)
            for half in range(2):
                pool.wait_ge(const_ready.sem, 3 + half)
                pool.iota(pT[64 * half:64 * half + 64, 0, :].bitcast(I32), pattern=[[-1, P]], base=CHUNK,
                          channel_multiplier=1).then_inc(const_ready.sem, 1)
            pool.wait_ge(const_ready.sem, 5)
            for t in (xr, kT, vT, carry):
                pool.memset(t[:], 0.0).then_inc(const_ready.sem, 1)

        @block.tensor
        def _(pe):
            def transpose_u(g, j):
                x_scaled.wait(pe, g, j + 1)
                for k in range(KD):
                    ins = pe.transpose(tp[:, k], xt[:, j, k * P:(k + 1) * P], ident[:])
                u_transposed.by(ins)

            def project(g, m):
                proj_taken.wait(pe, g, m - 1)
                for k in range(KD):
                    ins = product3(pe, bank[m % 2][:, 0:TOK], w_cols(w_hi, k, m), w_cols(w_lo, k, m),
                                   u_hi[:, k], u_lo[:, k], k == 0, k == KD - 1)
                projected.by(ins)

            def transpose_v(g):
                proj_taken.wait(pe, g, 1)
                for c in range(TOK // CHUNK):
                    ins = pe.transpose(tp[:, c], vT[:, c * CHUNK:c * CHUNK + P], ident[:])
                v_transposed.by(ins)

            def score(g, j):
                for h in range(HEADS):
                    kv = slice(64 * (h // G), 64 * (h // G) + 64)
                    for half in range(2):
                        c = 2 * j + half
                        ins = pe.matmul(sc[64 * half:64 * half + 64, h], qT[kv, h % G, c * CHUNK:(c + 1) * CHUNK],
                                        kT[kv, c * CHUNK:c * CHUNK + P], start=True, stop=True)
                scored.by(ins)

            def transpose_p(g, j):
                p_ready.wait(pe, g, j + 1)
                for h in range(HEADS):
                    ins = pe.transpose(tp[:, h], ss[:, j, h], ident[:])
                p_transposed.by(ins)

            def attend(g, j):
                p_taken.wait(pe, g, j + 1)
                ot_taken.wait(pe, g, j)
                for v in range(KV):
                    for half in range(2):
                        ins = pe.matmul(ot[64 * v:64 * v + 64, :, 64 * half:64 * half + 64],
                                        vb[:, 2 * j + half, 64 * v:64 * v + 64],
                                        pT[:, G * v:G * v + G, 64 * half:64 * half + 64], start=True, stop=True)
                pv_done.by(ins)

            def gate(g, c):
                conv_done.wait(pe, g, c + 1)
                gates_taken.wait(pe, g, c)
                for s in range(2):
                    ins = pe.matmul(gt[:, s], wg[:, c, s], xc[:, c], start=True, stop=True)
                gated.by(ins)

            pe.wait_ge(const_ready.sem, CONST_STEPS)
            pe.wait_ge(consts_in.sem, 16 * NCONST)
            transpose_u(-1, 0)
            u_lo_done.wait(pe, -1, 1)
            transpose_u(-1, 1)
            pe.wait_ge(w_lo_done.sem, 2 * KD)
            pe.sem_inc(pv_done.sem, 1)
            with pe.Fori(0, NG) as g:
                u_lo_done.wait(pe, g, 0)
                for m in range(2 + G):
                    project(g, m)
                transpose_v(g)
                proj_taken.wait(pe, g, 2 + G)
                scores_taken.wait(pe, g, 0)
                project(g, 6)
                score(g, 0)
                project(g, 7)
                scores_taken.wait(pe, g, 1)
                project(g, 8)
                score(g, 1)
                project(g, 9)
                project(g, 10)
                v_taken.wait(pe, g, 1)
                transpose_p(g, 0)
                project(g, 11)
                attend(g, 0)
                project(g, 12)
                transpose_p(g, 1)
                project(g, 13)
                attend(g, 1)
                for c in range(RC):
                    gate(g, c)
                transpose_u(g, 0)
                u_lo_done.wait(pe, g, 1)
                transpose_u(g, 1)

        @block.scalar
        def _(a):
            def square_x(g, j):
                x_in[j].wait(a, g, 1)
                x_squared.by(a.activation((rr, ig)[j][:].rearrange("p c t -> p (c t)"), xt[:, j], ACT.Square,
                                          accum_out=ssq[:, j:j + 1]))

            def rms(g):
                x_squared.wait(a, g, TJ)
                rms_done.by(a.activation(ssq[:], ssq[:], ACT.Sqrt, bias=eps[:, 0:1], scale=1.0 / D))

            def take_hi(g, j):
                u_transposed.wait(a, g, j + 1)
                u_hi_done.by(a.activation(u_hi[:, :, j * P:(j + 1) * P], tp[:], ACT.Copy))

            a.wait_ge(consts_in.sem, 16 * NCONST)
            with a.Fori(0, KD) as k:
                for b in range(2):
                    w_staged[b].wait(a, k, 1)
                    w_hi_done.by(a.activation(w_hi[:, k, bass.ts(b, D_IN // 2)], stage[b], ACT.Copy,
                                              scale=g1[:, bass.ds(k, 1)]))
            a.wait_ge(lambda_abs.sem, 1)
            a.activation(lb[:], la[:], ACT.Exp, scale=-1.0).then_inc(lambda_exp.sem, 1)
            a.wait_ge(const_ready.sem, CONST_STEPS)
            for j in range(TJ):
                square_x(-1, j)
            rms(-1)
            for j in range(TJ):
                take_hi(-1, j)
            a.wait_ge(tables_ready.sem, 1)
            a.sem_inc(proj_taken.sem, 2)
            a.sem_inc(gates_taken.sem, 1)
            a.sem_inc(ot_taken.sem, 1)

            with a.Fori(0, NG) as g:
                def take(m, dst, scale=1.0):
                    projected.wait(a, g, m + 1)
                    proj_taken.by(a.activation(dst, bank[m % 2][:, 0:TOK], ACT.Copy, scale=scale))

                def exps(j):
                    smax_done.wait(a, g, j + 1)
                    for h in range(HEADS):
                        a.activation(ss[:, j, h], ss[:, j, h], ACT.Exp, bias=nm[:, h:h + 1],
                                     accum_out=den[:, h:h + 1])
                    exp_done.by(a.activation(sd[:], sd[:], ACT.Exp))

                def take_p(j):
                    p_transposed.wait(a, g, j + 1)
                    pv_done.wait(a, g, j)
                    p_taken.by(a.activation(pT[:], tp[:], ACT.Copy))

                def take_o(j):
                    pv_done.wait(a, g, j + 1)
                    ot_taken.by(a.activation(bT[:, :, j * P:(j + 1) * P], ot[:], ACT.Copy))

                take(0, vT[:, CHUNK:])
                take(1, kT[:, CHUNK:])
                for c in range(G):
                    take(2 + c, qT[:, c], scale=HD ** -0.5)
                v_transposed.wait(a, g, 1)
                v_taken.by(a.activation(vb[:], tp[:, 0:TOK // CHUNK], ACT.Copy))
                xr_free.wait(a, g, 0)
                take(6, xr[:, 0, CONV - 1:])
                take(7, xr[:, 1, CONV - 1:])
                exps(0)
                take(8, xr[:, 2, CONV - 1:])
                take(9, xr[:, 3, CONV - 1:])
                exps(1)
                a_stored.wait(a, g, 0)
                b_stored.wait(a, g, 0)
                take(10, yg[:, 0])
                take_p(0)
                take(11, yg[:, 1])
                take_o(0)
                take(12, yg[:, 2])
                take_p(1)
                take(13, yg[:, 3])
                take_o(1)
                a.activation(kT[:, 0:CHUNK], kT[:, TOK:], ACT.Copy)
                a.activation(vT[:, 0:CHUNK], vT[:, TOK:], ACT.Copy)
                proj_taken.wait(a, g, NCH)
                rnn_done.wait(a, g, 0)
                gelu_sq.by(a.activation(t1[:], yg[:], ACT.Square))
                for j in range(TJ):
                    square_x(g, j)
                rms(g)
                gelu_poly.wait(a, g, 1)
                gelu_sig.by(a.activation(t1[:], t1[:], ACT.Sigmoid, scale=2 * GELU_K * GELU_C))
                for c in range(RC):
                    gated.wait(a, g, c + 1)
                    a.activation(rr[:, c], gt[:, 0], ACT.Sigmoid, bias=brg[:, c:c + 1])
                    gates_taken.by(a.activation(ig[:, c], gt[:, 1], ACT.Sigmoid, bias=big[:, c:c + 1]))
                for j in range(TJ):
                    take_hi(g, j)
                gates_taken.wait(a, g, RC)
                for c in range(RC):
                    ins = a.activation(rr[:, c], rr[:, c], ACT.Tanh, scale=sp4[:, c:c + 1])
                s_done.by(ins)
                s_done.wait(a, g, 1)
                gelu_done.wait(a, g, 1)
                sqrt_done.by(a.activation(t1[:], rr[:], ACT.Sqrt))

        @block.vector
        def _(v):
            def chained(ins):
                step.step(ins)
                step.wait(v)

            def scale_x(g):
                rms_done.wait(v, g, 1)
                chained(v.reciprocal(rstd[:], ssq[:]))
                for j in range(TJ):
                    x_scaled.by(v.tensor_scalar(xt[:, j], xt[:, j], rstd[:, j:j + 1], None, ALU.mult))

            def take_lo(g, j):
                u_hi_done.wait(v, g, j + 1)
                u_lo_done.by(v.tensor_tensor(u_lo[:, :, j * P:(j + 1) * P], tp[:],
                                             u_hi[:, :, j * P:(j + 1) * P].bitcast(F32), ALU.subtract))

            v.wait_ge(consts_in.sem, 16 * NCONST)
            v.tensor_scalar(lc[:], lam[:], -1.0, None, ALU.mult).then_inc(step.sem, 1)
            step.n += 1
            step.wait(v)
            v.tensor_tensor(la[:], lam[:], lc[:], ALU.max).then_inc(lambda_abs.sem, 1)
            with v.Fori(0, KD) as k:
                for b in range(2):
                    w_hi_done.wait(v, k, b + 1)
                    cut = bass.ts(b, D_IN // 2)
                    w_lo_done.by(v.scalar_tensor_tensor(out=w_lo[:, k, cut], in0=stage[b],
                                                        scalar=g1[:, bass.ds(k, 1)],
                                                        in1=w_hi[:, k, cut].bitcast(F32),
                                                        op0=ALU.mult, op1=ALU.subtract))
            v.wait_ge(lambda_exp.sem, 1)
            chained(v.tensor_scalar(ld[:], lb[:], 2.0, None, ALU.add))
            chained(v.reciprocal(ld[:], ld[:]))
            chained(v.tensor_tensor(lb[:], lb[:], ld[:], ALU.mult))
            chained(v.tensor_tensor(ld[:], lb[:], lb[:], ALU.mult))
            TERMS = 9
            chained(v.tensor_scalar(le[:], ld[:], 1.0 / (2 * TERMS - 1), 1.0 / (2 * TERMS - 3), ALU.mult, ALU.add))
            for n in range(TERMS - 3, -1, -1):
                chained(v.tensor_tensor(le[:], le[:], ld[:], ALU.mult))
                chained(v.tensor_scalar(le[:], le[:], 1.0 / (2 * n + 1), None, ALU.add))
            chained(v.tensor_tensor(le[:], le[:], lb[:], ALU.mult))
            chained(v.tensor_scalar(lc[:], lc[:], 0.0, LRU_C / 2, ALU.max, ALU.mult))
            chained(v.scalar_tensor_tensor(out=sp4[:], in0=le[:], scalar=LRU_C, in1=lc[:],
                                           op0=ALU.mult, op1=ALU.add))
            chained(v.tensor_scalar(neg_sink[:], sink[:], -1.0, None, ALU.mult))
            v.wait_ge(const_ready.sem, CONST_STEPS)
            chained(v.tensor_copy(pT[:, 1], pT[:, 0].bitcast(I32)))
            chained(v.tensor_scalar(pT[:, 2], pT[:, 1], -1.0, None, ALU.mult))
            chained(v.tensor_tensor(pT[:, 3], pT[:, 1], pT[:, 2], ALU.min))
            for h in range(HEADS):
                for b in range(2):
                    chained(v.tensor_scalar(bias[:, b, h], pT[:, 3], 2.0 ** (-8.0 * (h + 1) / HEADS), None, ALU.mult))
            chained(v.memset(bias[0:CHUNK, 0, :, 0:CHUNK], NEG))
            scale_x(-1)
            for j in range(TJ):
                take_lo(-1, j)
            v.sem_inc(scores_taken.sem, 1)
            v.sem_inc(xr_free.sem, 1)
            v.sem_inc(rnn_done.sem, 1)
            v.sem_inc(tables_ready.sem, 1)

            with v.Fori(0, NG) as g:
                step.enter(g)

                def softmax_max(j):
                    scored.wait(v, g, j + 1)
                    table = (g + NG - 1) // NG if j == 0 else 1
                    scores_taken.by(v.tensor_tensor(ss[:, j], sc[:], bias[:, table], ALU.add))
                    scores_taken.wait(v, g, j + 1)
                    chained(v.tensor_reduce(mx[:], ss[:, j], AX.X, ALU.max, negate=True))
                    chained(v.tensor_tensor(nm[:], mx[:], neg_sink[:], ALU.min))
                    smax_done.by(v.tensor_tensor(sd[:], sink[:], nm[:], ALU.add))

                def softmax_scale(j):
                    exp_done.wait(v, g, j + 1)
                    chained(v.tensor_tensor(rs[:], den[:], sd[:], ALU.add))
                    chained(v.reciprocal(rs[:], rs[:]))
                    p_ready.by(v.tensor_tensor(ss[:, j], ss[:, j],
                                               rs[:].unsqueeze(2).to_broadcast([P, HEADS, P]), ALU.mult))

                def conv(c):
                    proj_taken.wait(v, g, 2 + G + c + 1)
                    chained(v.tensor_scalar(xc[:, c], xr[:, c, 0:TOK], cw[:, 0, c:c + 1], cb[:, c:c + 1],
                                            ALU.mult, ALU.add))
                    for k in range(1, CONV):
                        ins = v.scalar_tensor_tensor(out=xc[:, c], in0=xr[:, c, k:k + TOK],
                                                     scalar=cw[:, k, c:c + 1], in1=xc[:, c],
                                                     op0=ALU.mult, op1=ALU.add)
                        conv_done.by(ins) if k == CONV - 1 else chained(ins)

                softmax_max(0)
                conv(0)
                conv(1)
                softmax_scale(0)
                softmax_max(1)
                conv(2)
                conv(3)
                softmax_scale(1)
                xr_free.by(v.tensor_copy(xr[:, :, 0:CONV - 1], xr[:, :, TOK:TOK + CONV - 1]))
                gelu_sq.wait(v, g, 1)
                gelu_poly.by(v.scalar_tensor_tensor(out=t1[:].rearrange("p c t -> p (c t)"),
                                                    in0=t1[:].rearrange("p c t -> p (c t)"), scalar=1.0 / GELU_C,
                                                    in1=yg[:].rearrange("p c t -> p (c t)"),
                                                    op0=ALU.add, op1=ALU.mult))
                scale_x(g)
                gelu_sig.wait(v, g, 1)
                gelu_done.by(v.tensor_tensor(yg[:], yg[:], t1[:], ALU.mult))
                for j in range(TJ):
                    take_lo(g, j)
                sqrt_done.wait(v, g, 1)
                step.step(v.tensor_tensor(ig[:], ig[:], xc[:], ALU.mult))
                chained(v.tensor_scalar(rr[:], rr[:], 1.0, None, ALU.add))
                chained(v.reciprocal(rr[:], rr[:]))
                step.step(v.tensor_scalar(xc[:], rr[:], 2.0, -1.0, ALU.mult, ALU.add))
                chained(v.tensor_tensor(t1[:], t1[:], rr[:], ALU.mult))
                chained(v.scalar_tensor_tensor(out=ig[:].rearrange("p c t -> p (c t)"),
                                               in0=t1[:].rearrange("p c t -> p (c t)"), scalar=2.0,
                                               in1=ig[:].rearrange("p c t -> p (c t)"),
                                               op0=ALU.mult, op1=ALU.mult))
                for c in range(RC):
                    step.step(v.tensor_tensor_scan(rr[:, c], xc[:, c], ig[:, c], carry[:, c:c + 1],
                                                   ALU.mult, ALU.add))
                step.wait(v)
                chained(v.tensor_copy(carry[:], rr[:, :, TOK - 1]))
                rnn_done.by(v.tensor_tensor(yg[:], rr[:], yg[:], ALU.mult))
                step.leave()


def project_out(nc, x, mixT, rnn_out_g, attn_out_g, w_out, norm2_g, w_group_router, w_expert_router,
                h_rows, u_rows, lists, slots, seen_out):
    with ExitStack() as ctx:
        def sb(name, shape, dt=F32):
            return ctx.enter_context(nc.sbuf_tensor(name, shape, dt))

        def ps(name, shape):
            return ctx.enter_context(nc.psum_tensor(name, shape, F32))

        def sig(name, per=2, step=1):
            return Signal(ctx, nc, name, per, 0, step)

        N2 = D // 2
        R = GROUPS + E
        o_hi, o_lo = sb("o_hi", [P, KD, D], F32R), sb("o_lo", [P, KD, D], F32R)
        wst = sb("wst", [P, KD, D])
        og = sb("og", [P, KD])
        g2 = sb("g2", [P, D])
        wr = sb("wr", [P, KD, R])
        mt = sb("mt", [P, 2, KD, P])
        m_hi, m_lo = sb("m_hi", [P, 2, KD, P], F32R), sb("m_lo", [P, 2, KD, P], F32R)
        sq = sb("sq", [P, KD, P])
        xt, ht, ut = sb("x_tile", [P, 2, D]), sb("h_tile", [P, 2, D]), sb("u_tile", [P, 2, D])
        hsq = sb("hsq", [P, D])
        uT = sb("uT", [P, KD, P])
        ones, onesb = sb("ones", [P, 2]), sb("onesb", [P, P], BF16)
        before = sb("before", [P, P], BF16)
        idn = sb("idn", [P, P])
        epsc = sb("epsc", [P, 1])
        rab, rh = sb("rab", [P, 2]), sb("rh", [P, 2])
        lg, g8, e8 = sb("lg", [P, 8]), sb("g8", [P, 8]), sb("e8", [P, 8])
        gi, ei = sb("gi", [P, 8], U32), sb("ei", [P, 8], U32)
        ngm, gif, pen = sb("ngm", [P, 1]), sb("gif", [P, 1]), sb("pen", [P, GROUPS])
        pg, gsum, ex, nl = sb("pg", [P, GROUPS]), sb("gsum", [P, 1]), sb("ex", [P, 1]), sb("nl", [P, 1])
        em, hot, sel = sb("em", [P, E]), sb("hot", [P, TOP, E]), sb("sel", [P, TOP, E])
        chosen, seen = sb("chosen", [P, E], BF16), sb("seen", [P, E], BF16)
        slot = sb("slot", [P, 6])
        at = [sb(f"at{b}", [P, TOP], U32) for b in range(2)]
        tokf, toki = sb("tokf", [P, 2]), [sb(f"toki{b}", [P, 1], I32) for b in range(2)]
        iota_i, iota_e = sb("iota_i", [P, E], I32), sb("iota_e", [P, E])
        tok0 = sb("tok0", [P, 2], I32)
        zeros = sb("zeros", [P, E * LIST // P], I32)

        pa, pb = ps("pa", [P, 2, N2]), ps("pb", [P, 2, N2])
        tps = ps("tps", [P, KD, P])
        sums = ps("sums", [P, 512])
        rt = ps("rt", [P, 512])
        LOGIT, RANK = 0, 64

        consts_in, const_ready = sig("consts_in2"), sig("const_ready2")
        o_hi_done, o_lo_done = sig("o_hi_done"), sig("o_lo_done")
        lists_zero = sig("lists_zero")
        mix_in = [sig(f"mix_in{b}", 1, 32) for b in range(2)]
        m_hi_done, m_squared, m_lo_done = sig("m_hi_done"), sig("m_squared"), sig("m_lo_done")
        summed, roots, a_done, a_added = sig("summed"), sig("roots"), sig("a_done"), sig("a_added")
        b_done, b_added = sig("b_done"), sig("b_added")
        h_squared, h_root, u_ready = sig("h_squared"), sig("h_root"), sig("u_ready")
        h_stored = [sig(f"h_stored{b}", 1, 16) for b in range(2)]
        u_stored = [sig(f"u_stored{b}", 1, 16) for b in range(2)]
        u_turned, uT_done, routed = sig("u_turned"), sig("uT_done"), sig("routed")
        group_max, group_exp, expert_max, expert_exp = (sig(n) for n in ("group_max", "group_exp", "expert_max",
                                                                        "expert_exp"))
        chosen_done, ranked, slots_done = sig("chosen_done"), sig("ranked"), sig("slots_done")
        scattered = [sig(f"scattered{b}", 1, 32) for b in range(2)]
        at_free = Signal(ctx, nc, "at_free", 2, 2)
        sp_begun, pool_begun, settled, ranks_end = (sig(n) for n in ("sp_begun", "pool_begun", "settled", "ranks_end"))
        ROUTE_STEPS, RANK_STEPS, NORM_STEPS = 14, 6, 2
        step = Chain(ctx, nc, "dve_step2", 2 * (ROUTE_STEPS + RANK_STEPS + NORM_STEPS))
        NCONST, CONST_STEPS = 9, 14
        block = ctx.enter_context(nc.Block())
        x_tiles, h_tiles, u_tiles = (t.rearrange("(t p) n -> t p n", p=P) for t in (x, h_rows, u_rows))
        mix_cols = mixT.rearrange("c p t -> p c t")

        @block.sync
        def _(sp):
            def load(i, b):
                mix_t = mix_cols[:, :, bass.ds(i * P, P)]
                sp.dma_start(mt[:, b], mix_t).then_inc(mix_in[b].sem, 16)
                sp.dma_start(xt[:, b], x_tiles[i]).then_inc(mix_in[b].sem, 16)

            pieces = [(wst[:, 0:RC], w_out[0, 0:D_RNN].rearrange("(c p) n -> p c n", p=P)),
                      (og[:, 0:RC], rnn_out_g[0].rearrange("(c p) -> p c", p=P))]
            for v in range(KV):
                half = slice(64 * v, 64 * v + 64)
                pieces.append((wst[half, RC:],
                               w_out[0, D_RNN:].rearrange("(v c d) n -> v d c n", v=KV, c=G)[v]))
                pieces.append((og[half, RC:], attn_out_g[0].rearrange("(v c d) -> v d c", v=KV, c=G)[v]))
            pieces.append((g2[:], norm2_g[0].partition_broadcast(P)))
            for dst, src in pieces:
                sp.dma_start(dst, src, allow_slow_non_contiguous=True).then_inc(consts_in.sem, 16)
            for b in range(2):
                load(b, b)
            sp.dma_start(wr[:, :, 0:GROUPS], w_group_router[0].rearrange("(k p) e -> p k e", p=P),
                         allow_slow_non_contiguous=True).then_inc(consts_in.sem, 16)
            sp.dma_start(wr[:, :, GROUPS:], w_expert_router[0].rearrange("(k p) e -> p k e", p=P),
                         allow_slow_non_contiguous=True).then_inc(consts_in.sem, 16)
            sp.wait_ge(const_ready.sem, CONST_STEPS)
            sp.dma_start(lists.rearrange("(p n) one -> p (n one)", p=P), zeros[:]).then_inc(lists_zero.sem, 16)

            def tile(g, b):
                m_lo_done.wait(sp, g, b + 1)
                m_squared.wait(sp, g, b + 1)
                a_added.wait(sp, g, b + 1)
                sp.sem_inc(sp_begun.sem, 1)
                if isinstance(g, int):
                    load((2 * g + b + 2) % NT, b)
                else:
                    load(sp.snap((g * 2 + (b + 2)) % NT), b)
                b_added.wait(sp, g, b + 1)
                sp.sem_inc(sp_begun.sem, 1)
                h_stored[b].by(sp.dma_start(h_tiles[g * 2 + b], ht[:, b]))
                u_ready.wait(sp, g, b + 1)
                sp.sem_inc(sp_begun.sem, 1)
                u_stored[b].by(sp.dma_start(u_tiles[g * 2 + b], ut[:, b]))

            for b in range(2):
                tile(0, b)
            with sp.Fori(1, NT // 2) as g:
                for b in range(2):
                    tile(g, b)
            sp.wait_ge(lists_zero.sem, 16)
            for b in range(2):
                sp.wait_ge(h_stored[b].sem, 16 * (NT // 2))
                sp.wait_ge(u_stored[b].sem, 16 * (NT // 2))
                sp.wait_ge(mix_in[b].sem, 32 * (NT // 2 + 1))

        @block.gpsimd
        def _(pool):
            made = 0

            def then(ins):
                nonlocal made
                made += 1
                ins.then_inc(const_ready.sem, 1)
                pool.wait_ge(const_ready.sem, made)

            then(pool.memset(zeros[:], 0))
            then(pool.memset(idn[:], 0.0))
            then(pool.affine_select(out=idn[:], in_=idn[:], compare_op=ALU.not_equal, fill=1.0, base=0,
                                    pattern=[[-1, P]], channel_multiplier=1))
            then(pool.memset(before[:], 1.0))
            then(pool.affine_select(out=before[:], in_=before[:], compare_op=ALU.is_gt, fill=0.0, base=0,
                                    pattern=[[1, P]], channel_multiplier=-1))
            then(pool.memset(onesb[:], 1.0))
            then(pool.memset(ones[:], 1.0))
            then(pool.memset(epsc[:], EPS))
            then(pool.memset(lg[:], NEG))
            then(pool.memset(seen[:], 0.0))
            then(pool.memset(hsq[:], 0.0))
            then(pool.iota(iota_i[:], pattern=[[1, E]], base=0, channel_multiplier=0))
            then(pool.iota(tok0[:], pattern=[[P, 2]], base=0, channel_multiplier=1))
            then(pool.memset(sq[:], 0.0))
            assert made == CONST_STEPS
            pool.wait_ge(lists_zero.sem, 16)
            pool.sem_inc(at_free.sem, 2)

            def scatter(g, b):
                slots_done.wait(pool, g, b + 1)
                pool.sem_inc(pool_begun.sem, 1)
                for k in range(TOP):
                    pool.indirect_dma_start(lists, bass.IndirectOffsetOnAxis(ap=at[b][:, k:k + 1], axis=0),
                                            toki[b][:], None).then_inc(scattered[b].sem, 16)
                scattered[b].wait(pool, g, 1)
                pool.sem_inc(at_free.sem, 1)

            for b in range(2):
                scatter(0, b)
            with pool.Fori(1, NT // 2) as g:
                for b in range(2):
                    scatter(g, b)

        @block.tensor
        def _(pe):
            def product(dst, half, b, c0):
                for c in range(RC):
                    k = c0 + c
                    cut = bass.ts(half, N2)
                    ins = product3(pe, dst[:, half], m_hi[:, b, k], m_lo[:, b, k],
                                   o_hi[:, k, cut], o_lo[:, k, cut], c == 0, c == RC - 1)
                return ins

            def sum_squares(g, b):
                m_squared.wait(pe, g, b + 1)
                roots.wait(pe, g, b)
                for s in range(2):
                    for c in range(RC):
                        ins = pe.matmul(sums[:, 2 * s:2 * s + 2], sq[:, RC * s + c], ones[:], start=(c == 0),
                                        stop=(c == RC - 1))
                summed.by(ins)

            def rank(g, b):
                chosen_done.wait(pe, g, b + 1)
                pe.matmul(rt[:, RANK:RANK + E], before[:], chosen[:], start=True, stop=False)
                ranked.by(pe.matmul(rt[:, RANK:RANK + E], onesb[:], seen[:], start=False, stop=True))

            pe.wait_ge(const_ready.sem, CONST_STEPS)
            sum_squares(0, 0)
            pe.wait_ge(o_lo_done.sem, KD)
            m_lo_done.wait(pe, 0, 1)
            product(pa, 0, 0, 0)
            a_done.by(product(pa, 1, 0, 0))
            pe.wait_ge(consts_in.sem, 16 * NCONST)

            def tile(g, b):
                first = isinstance(g, int) and b == 0
                b_added.wait(pe, g, b)
                product(pb, 0, b, RC)
                b_done.by(product(pb, 1, b, RC))
                if not first:
                    rank(g, b - 1)
                sum_squares(g, b + 1)
                m_lo_done.wait(pe, g, b + 2)
                a_added.wait(pe, g, b + 1)
                product(pa, 0, 1 - b, 0)
                u_ready.wait(pe, g, b + 1)
                uT_done.wait(pe, g, b)
                for k in range(KD):
                    ins = pe.transpose(tps[:, k], ut[:, b, k * P:(k + 1) * P], idn[:])
                u_turned.by(ins)
                a_done.by(product(pa, 1, 1 - b, 0))
                uT_done.wait(pe, g, b + 1)
                slots_done.wait(pe, g, b)
                for k in range(KD):
                    ins = pe.matmul(rt[:, LOGIT:LOGIT + R], uT[:, k], wr[:, k], start=(k == 0), stop=(k == KD - 1))
                routed.by(ins)

            for b in range(2):
                tile(0, b)
            with pe.Fori(1, NT // 2) as g:
                for b in range(2):
                    tile(g, b)
            rank(NT // 2 - 1, 1)

        @block.scalar
        def _(a):
            def split(g, b):
                mix_in[b % 2].wait(a, g, 1 + b // 2)
                m_hi_done.by(a.activation(m_hi[:, b % 2], mt[:, b % 2], ACT.Copy))
                summed.wait(a, g, b)
                m_squared.by(a.activation(sq[:], mt[:, b % 2], ACT.Square))

            def root(g, b):
                summed.wait(a, g, b + 1)
                a_added.wait(a, g, b)
                roots.by(a.activation(rab[:], sums[:, 0:4:2], ACT.Sqrt, bias=epsc[:, 0:1], scale=1.0 / D_RNN))

            a.wait_ge(consts_in.sem, 16 * NCONST)
            for k in range(KD):
                o_hi_done.by(a.activation(o_hi[:, k], wst[:, k], ACT.Copy, scale=og[:, k:k + 1]))
            a.wait_ge(const_ready.sem, CONST_STEPS)
            split(0, 0)
            root(0, 0)

            def tile(g, b):
                b_done.wait(a, g, b)
                split(g, b + 1)
                b_added.wait(a, g, b + 1)
                u_ready.wait(a, g, b)
                h_squared.by(a.activation(hsq[:], ht[:, b], ACT.Square, accum_out=rh[:, 0:1]))
                h_squared.wait(a, g, b + 1)
                h_root.by(a.activation(rh[:, 1:2], rh[:, 0:1], ACT.Sqrt, bias=epsc[:, 0:1], scale=1.0 / D))
                root(g, b + 1)
                u_turned.wait(a, g, b + 1)
                uT_done.by(a.activation(uT[:], tps[:], ACT.Copy))
                group_max.wait(a, g, b + 1)
                group_exp.by(a.activation(pg[:], lg[:, 0:GROUPS], ACT.Exp, bias=ngm[:, 0:1], accum_out=gsum[:, 0:1]))
                expert_max.wait(a, g, b + 1)
                expert_exp.by(a.activation(ex[:], e8[:, 1:2], ACT.Exp, bias=nl[:, 0:1]))

            for b in range(2):
                tile(0, b)
            with a.Fori(1, NT // 2) as g:
                for b in range(2):
                    tile(g, b)

        @block.vector
        def _(v):
            def chained(ins):
                step.step(ins)
                step.wait(v)

            def lower(g, b):
                m_hi_done.wait(v, g, b + 1)
                m_lo_done.by(v.tensor_tensor(m_lo[:, b % 2], mt[:, b % 2], m_hi[:, b % 2].bitcast(F32),
                                             ALU.subtract))

            def add_a(g, b):
                a_done.wait(v, g, b + 1)
                h_stored[b % 2].wait(v, g, b // 2)
                a_added.by(v.scalar_tensor_tensor(out=ht[:, b % 2], in0=pa[:].rearrange("p a n -> p (a n)"),
                                                  scalar=rab[:, 0:1], in1=xt[:, b % 2], op0=ALU.mult, op1=ALU.add))

            def place(g, b):
                ranked.wait(v, g, b + 1)
                at_free.wait(v, g, b - 1)
                step.step(v.tensor_tensor(sel[:], hot[:], rt[:, RANK:RANK + E].unsqueeze(1)
                                          .to_broadcast([P, TOP, E]), ALU.mult))
                chained(v.tensor_tensor(seen[:], seen[:], chosen[:], ALU.add))
                chained(v.tensor_reduce(slot[:, 2:4], sel[:], AX.X, ALU.add))
                chained(v.tensor_copy(slots[:, bass.ds(g * 2 + b, 1)].rearrange("p one n -> p (one n)"), slot[:])
                        if not isinstance(g, int) else v.tensor_copy(slots[:, 2 * g + b], slot[:]))
                chained(v.tensor_copy(toki[b][:], tokf[:, b:b + 1]))
                step.step(v.tensor_scalar(tokf[:, b:b + 1], tokf[:, b:b + 1], 2.0 * P, None, ALU.add))
                slots_done.by(v.scalar_tensor_tensor(out=at[b][:], in0=slot[:, 0:2], scalar=float(LIST),
                                                     in1=slot[:, 2:4], op0=ALU.mult, op1=ALU.add))

            v.wait_ge(consts_in.sem, 16 * NCONST)
            for k in range(KD):
                o_hi_done.wait(v, 0, k + 1)
                o_lo_done.by(v.scalar_tensor_tensor(out=o_lo[:, k], in0=wst[:, k], scalar=og[:, k:k + 1],
                                                    in1=o_hi[:, k].bitcast(F32), op0=ALU.mult, op1=ALU.subtract))
            v.wait_ge(const_ready.sem, CONST_STEPS)
            chained(v.tensor_copy(iota_e[:], iota_i[:]))
            chained(v.tensor_copy(tokf[:], tok0[:]))
            lower(0, 0)
            roots.wait(v, 0, 1)
            chained(v.reciprocal(rab[:], rab[:]))
            add_a(0, 0)

            def tile(g, b):
                first = isinstance(g, int) and b == 0
                lower(g, b + 1)
                if not first:
                    if b == 1:
                        place(g, 0)
                    else:
                        place(g - 1, 1)
                b_done.wait(v, g, b + 1)
                a_added.wait(v, g, b + 1)
                b_added.by(v.scalar_tensor_tensor(out=ht[:, b], in0=pb[:].rearrange("p a n -> p (a n)"),
                                                  scalar=rab[:, 1:2], in1=ht[:, b], op0=ALU.mult, op1=ALU.add))
                h_root.wait(v, g, b + 1)
                chained(v.reciprocal(rh[:, 1:2], rh[:, 1:2]))
                u_stored[b].wait(v, g, 0)
                u_ready.by(v.scalar_tensor_tensor(out=ut[:, b], in0=ht[:, b], scalar=rh[:, 1:2], in1=g2[:],
                                                  op0=ALU.mult, op1=ALU.mult))
                roots.wait(v, g, b + 2)
                chained(v.reciprocal(rab[:], rab[:]))
                add_a(g, b + 1)
                routed.wait(v, g, b + 1)
                chained(v.tensor_copy(lg[:, 0:GROUPS], rt[:, LOGIT:LOGIT + GROUPS]))
                v.sem_inc(settled.sem, 1)
                chained(v.max(g8[:], lg[:]))
                v.sem_inc(settled.sem, 1)
                step.step(v.max_index(gi[:], g8[:], lg[:]))
                group_max.by(v.tensor_scalar(ngm[:], g8[:, 0:1], -1.0, None, ALU.mult))
                step.wait(v)
                chained(v.tensor_copy(gif[:], gi[:, 0:1]))
                chained(v.tensor_scalar(pen[:], iota_e[:, 0:GROUPS], gif[:, 0:1], -NEG, ALU.is_equal, ALU.mult))
                chained(v.scalar_tensor_tensor(out=em[:].rearrange("p (g e) -> p g e", e=EPG),
                                               in0=pen[:].unsqueeze(2).to_broadcast([P, GROUPS, EPG]), scalar=NEG,
                                               in1=rt[:, LOGIT + GROUPS:LOGIT + R].rearrange("p (g e) -> p g e", e=EPG),
                                               op0=ALU.add, op1=ALU.add))
                v.sem_inc(settled.sem, 1)
                chained(v.max(e8[:], em[:]))
                v.sem_inc(settled.sem, 1)
                step.step(v.max_index(ei[:], e8[:], em[:]))
                expert_max.by(v.tensor_scalar(nl[:], e8[:, 0:1], -1.0, None, ALU.mult))
                step.wait(v)
                chained(v.tensor_copy(slot[:, 0:TOP], ei[:, 0:TOP]))
                step.step(v.tensor_scalar(hot[:, 0], iota_e[:], slot[:, 0:1], None, ALU.is_equal))
                chained(v.tensor_scalar(hot[:, 1], iota_e[:], slot[:, 1:2], None, ALU.is_equal))
                chosen_done.by(v.tensor_tensor(chosen[:], hot[:, 0], hot[:, 1], ALU.add))
                group_exp.wait(v, g, b + 1)
                expert_exp.wait(v, g, b + 1)
                chained(v.tensor_scalar(slot[:, 4:5], ex[:], 1.0, gsum[:, 0:1], ALU.add, ALU.mult))
                chained(v.reciprocal(slot[:, 4:5], slot[:, 4:5]))
                chained(v.tensor_tensor(slot[:, 5:6], slot[:, 4:5], ex[:], ALU.mult))

            step.enter(0)
            for b in range(2):
                tile(0, b)
            step.before, step.n = step.before + step.n, 0
            with v.Fori(1, NT // 2) as g:
                step.g = g - 1
                for b in range(2):
                    tile(g, b)
                step.leave()
            step.g, step.before, step.n = None, step.before + (NT // 2 - 1) * step.per, 0
            place(NT // 2 - 1, 1)
            step.wait(v)
            ranks_end.by(v.tensor_copy(seen_out[:], seen[:]))


def plan_blocks(nc, seen, slots, plan_dram, plan, dest):
    with ExitStack() as ctx:
        def sb(name, shape, dt=F32):
            return ctx.enter_context(nc.sbuf_tensor(name, shape, dt))

        ones = sb("ones_p", [P, P], BF16)
        zero = sb("zero_p", [P, E])
        cnt_i, nb_i = sb("cnt_i", [P, E], I32), sb("nb_i", [P, E], I32)
        nb, end, start = sb("nb", [P, E]), sb("end", [P, E]), sb("start", [P, E])
        ie, io = sb("ie", [P, E], I32), sb("io", [P, E])
        ib, block_no = sb("ib", [P, 1], I32), sb("block_no", [P, 1])
        ends, past, hot, tmp = (sb(n, [P, E]) for n in ("ends", "past", "hot_p", "tmp"))
        col = sb("col", [P, 8])
        f = sb("f", [P, 8])
        need_i = sb("need_i", [P, 2], I32)
        fi, one_i = sb("fi", [P, 2], I32), sb("one_i", [P, 2], I32)
        tab = sb("tab", [P, 8], I32)
        big = sb("big_p", [P, NT * TOP, E])
        row = sb("row", [P, NT * TOP])
        count = ctx.enter_context(nc.psum_tensor("count", [P, E], F32))
        const_ready, counted, planned = (Signal(ctx, nc, n, 0) for n in ("const_ready3", "counted", "planned"))
        out, back = Signal(ctx, nc, "plan_out", 0), Signal(ctx, nc, "plan_back", 0)
        step = Chain(ctx, nc, "dve_step3")
        block = ctx.enter_context(nc.Block())

        @block.gpsimd
        def _(pool):
            made = 0
            for make in (lambda: pool.memset(ones[:], 1.0), lambda: pool.memset(zero[:], 0.0),
                         lambda: pool.iota(ie[:], pattern=[[1, E]], base=0, channel_multiplier=0),
                         lambda: pool.iota(ib[:], pattern=[[1, 1]], base=0, channel_multiplier=1),
                         lambda: pool.memset(one_i[:], 1), lambda: pool.memset(col[:], 0.0)):
                make().then_inc(const_ready.sem, 1)
                made += 1
                pool.wait_ge(const_ready.sem, made)

        @block.tensor
        def _(pe):
            pe.wait_ge(const_ready.sem, 6)
            pe.matmul(count[:], ones[:], seen[:], start=True, stop=True).then_inc(counted.sem, 1)

        @block.vector
        def _(v):
            def chained(ins):
                step.step(ins)
                step.wait(v)

            def total(dst, src):
                chained(v.tensor_reduce(dst, src, AX.X, ALU.add))

            v.wait_ge(const_ready.sem, 6)
            step.step(v.tensor_copy(io[:], ie[:]))
            step.step(v.tensor_copy(block_no[:], ib[:]))
            v.wait_ge(counted.sem, 1)
            chained(v.tensor_scalar(cnt_i[:], count[:], float(P - 1), None, ALU.add))
            chained(v.tensor_scalar(nb_i[:], cnt_i[:], 7, None, ALU.arith_shift_right))
            chained(v.tensor_copy(nb[:], nb_i[:]))
            chained(v.tensor_tensor_scan(end[:], nb[:], zero[:], 0.0, ALU.add, ALU.add))
            chained(v.tensor_tensor(start[:], end[:], nb[:], ALU.subtract))
            chained(v.tensor_scalar(ends[:], end[:], block_no[:, 0:1], None, ALU.is_le))
            total(f[:, 0:1], ends[:])
            chained(v.tensor_scalar(col[:, 0:1], f[:, 0:1], float(E - 1), None, ALU.min))
            chained(v.tensor_scalar(hot[:], io[:], col[:, 0:1], None, ALU.is_equal))
            chained(v.tensor_tensor(tmp[:], hot[:], start[:], ALU.mult))
            total(f[:, 1:2], tmp[:])
            chained(v.tensor_tensor(tmp[:], hot[:], end[:], ALU.mult))
            total(f[:, 2:3], tmp[:])
            chained(v.tensor_scalar(past[:], end[:], f[:, 2:3], None, ALU.is_le))
            total(f[:, 3:4], past[:])
            chained(v.tensor_scalar(col[:, 1:2], f[:, 3:4], float(E - 1), None, ALU.min))
            chained(v.tensor_tensor(f[:, 4:5], block_no[:], f[:, 1:2], ALU.is_equal))
            chained(v.tensor_tensor(f[:, 5:6], block_no[:], end[:, E - 1:E], ALU.is_lt))
            chained(v.tensor_tensor(f[:, 4:5], f[:, 4:5], f[:, 5:6], ALU.mult))
            chained(v.tensor_scalar(f[:, 5:6], f[:, 3:4], float(E), None, ALU.is_lt))
            chained(v.tensor_tensor(col[:, 2:3], f[:, 4:5], f[:, 5:6], ALU.mult))
            chained(v.tensor_tensor(f[:, 6:7], block_no[:], f[:, 1:2], ALU.subtract))
            chained(v.tensor_scalar(f[:, 6:7], f[:, 6:7], float(T // P), float(P), ALU.min, ALU.mult))
            chained(v.scalar_tensor_tensor(out=col[:, 3:4], in0=col[:, 0:1], scalar=float(LIST), in1=f[:, 6:7],
                                           op0=ALU.mult, op1=ALU.add))
            chained(v.tensor_scalar(tmp[:], nb[:], 0.0, None, ALU.is_gt))
            chained(v.tensor_tensor(tmp[:], tmp[:], ends[:], ALU.mult))
            total(f[:, 7:8], tmp[:])
            chained(v.tensor_copy(fi[:, 0:1], f[:, 7:8]))
            chained(v.tensor_tensor(fi[:, 1:2], fi[:, 0:1], one_i[:, 0:1], ALU.bitwise_and))
            chained(v.tensor_copy(col[:, 4:5], fi[:, 1:2]))
            chained(v.tensor_scalar(past[:], start[:], 1.0, None, ALU.add))
            chained(v.tensor_tensor(tmp[:], tmp[:], past[:], ALU.mult))
            chained(v.tensor_tensor(past[:], end[:], f[:, 1:2].to_broadcast([P, E]), ALU.is_le))
            chained(v.tensor_tensor(tmp[:], tmp[:], past[:], ALU.mult))
            chained(v.tensor_reduce(f[:, 0:1], tmp[:], AX.X, ALU.max))
            chained(v.tensor_scalar(f[:, 1:2], f[:, 0:1], 1.0, None, ALU.add))
            chained(v.tensor_copy(need_i[:], f[:, 0:2]))
            chained(v.tensor_scalar(need_i[:], need_i[:], 1, None, ALU.arith_shift_right))
            chained(v.tensor_copy(f[:, 0:2], need_i[:]))
            chained(v.tensor_scalar(col[:, 5:6], f[:, 1:2], 48.0, 48.0, ALU.mult, ALU.add))
            chained(v.tensor_scalar(col[:, 6:7], f[:, 0:1], 48.0, 48.0, ALU.mult, ALU.add))
            planned.by(v.tensor_copy(tab[:], col[:]))
            sl = slots[:].rearrange("p t (s k) -> p t s k", k=TOP)
            chained(v.tensor_copy(row[:].rearrange("p (t k) -> p t k", k=TOP), sl[:, :, 0]))
            chained(v.tensor_tensor(big[:], row[:].unsqueeze(2).to_broadcast([P, NT * TOP, E]),
                                    io[:].unsqueeze(1).to_broadcast([P, NT * TOP, E]), ALU.is_equal))
            chained(v.tensor_tensor(big[:], big[:], start[:].unsqueeze(1).to_broadcast([P, NT * TOP, E]), ALU.mult))
            chained(v.tensor_reduce(row[:], big[:], AX.X, ALU.add))
            chained(v.scalar_tensor_tensor(out=dest[:], in0=row[:].rearrange("p (t k) -> p t k", k=TOP),
                                           scalar=float(P), in1=sl[:, :, 1], op0=ALU.mult, op1=ALU.add))

        @block.sync
        def _(sp):
            sp.wait_ge(planned.sem, 1)
            sp.dma_start(plan_dram, tab[:]).then_inc(out.sem, 16)
            sp.wait_ge(out.sem, 16)
            sp.dma_start(plan[0:1, :], plan_dram.rearrange("(a b) c -> a (b c)", a=1)).then_inc(back.sem, 16)
            sp.wait_ge(back.sem, 16)


def run_experts(nc, plan, lists, u_rows, w_gate, w_up, w_down, y_rows):
    with ExitStack() as ctx:
        def sb(name, shape, dt=F32):
            return ctx.enter_context(nc.sbuf_tensor(name, shape, dt))

        def ps(name, shape):
            return ctx.enter_context(nc.psum_tensor(name, shape, F32))

        U = 4
        NI = NBLK // U

        def sig(name, per=U, base=0, step=1):
            return Signal(ctx, nc, name, per, base, step)

        wgu = sb("wgu", [P, 2, KD, 2 * F])
        wdn = sb("wdn", [P, 2, FC, D])
        idx = [sb(f"idx{b}", [P, 1], I32) for b in range(U)]
        xg = [sb(f"xg{b}", [P, D]) for b in range(U)]
        xT = sb("xT", [P, 2, KD, P])
        act_g, hid = sb("act_g", [P, F]), sb("hid", [P, F])
        hT = sb("hT", [P, FC, P])
        ys = sb("ys", [P, U, D])
        idn = sb("idn_m", [P, P])
        tps = ps("tps_m", [P, KD, P])
        gu = [ps(f"gu{b}", [P, 2 * F]) for b in range(2)]
        hp = ps("hp", [P, FC, P])
        yp = [ps(f"yp{n}", [P, D // 2]) for n in range(2)]

        const_ready = sig("const_ready4", 0)
        w_first = sig("w_first", 0)
        w_in = [sig(f"w_in{b}", U // 2, 2 - b, 48) for b in range(2)]
        idx_in = [sig(f"idx_in{b}", 1, 1, 16) for b in range(U)]
        gathered = [sig(f"gathered{b}", 1, 1, 16) for b in range(U)]
        turned, xT_done = sig("turned", U, 1), sig("xT_done", U, 1)
        gated, silu_done, hid_done = sig("gated_m", U, 1), sig("silu_done"), sig("hid_done")
        h_turned, hT_done, down_done = sig("h_turned"), sig("hT_done"), sig("down_done", 2 * U)
        y_taken = [sig(f"y_taken{n}", U, 1) for n in range(2)]
        y_stored = [sig(f"y_stored{b}", 1, 1, 16) for b in range(U)]
        begun, pool_begun = sig("begun_m", 0), sig("pool_begun_m", 0)
        block = ctx.enter_context(nc.Block())
        plan_rows = plan[0:1, :].rearrange("a (b c) -> a b c", c=8)
        y_blocks = y_rows.rearrange("(b p) n -> b p n", p=P)
        wg_rows, wu_rows = (w[0].rearrange("e (k p) n -> e p k n", p=P) for w in (w_gate, w_up))
        wd_rows = w_down[0].rearrange("e (c p) n -> e p c n", p=P)

        def planned(eng, blk, c, top, low=0):
            at = bass.ds(blk, 1) if not isinstance(blk, int) else slice(blk, blk + 1)
            return eng.value_load(plan_rows[:, at, c], min_val=low, max_val=top)

        @block.sync
        def _(sp):
            def load_index(blk, b):
                row = planned(sp, blk, 3, E * LIST - P)
                idx_in[b].by(sp.dma_start(idx[b][:], lists[bass.ds(row, P), :]))

            def load_weights(g, b):
                nxt, load, buf = (planned(sp, g * U + b, c, top) for c, top in ((1, E - 1), (2, 1), (4, 1)))
                other = sp.snap(1 - buf, min_val=0, max_val=1)
                w_in[b % 2].wait(sp, g, (b - 1) // 2)
                sp.sem_inc(begun.sem, 1)
                for dst, src in ((wgu[:, bass.ds(other, 1), :, 0:F], wg_rows),
                                 (wgu[:, bass.ds(other, 1), :, F:], wu_rows),
                                 (wdn[:, bass.ds(other, 1)], wd_rows)):
                    sp.dma_start(dst.rearrange("p one k n -> p (one k) n"), src[nxt],
                                 cond=load).then_inc(w_in[b % 2].sem, 16)

            sp.sem_inc(w_in[0].sem, 48)
            sp.sem_inc(w_in[1].sem, 48)
            for b in range(2):
                load_index(b, b)
            e0 = planned(sp, 0, 0, E - 1)
            for dst, src in ((wgu[:, 0, :, 0:F], wg_rows), (wgu[:, 0, :, F:], wu_rows), (wdn[:, 0], wd_rows)):
                sp.dma_start(dst, src[e0]).then_inc(w_first.sem, 16)
            for b in range(2, U):
                load_index(b, b)
            load_weights(0, 0)
            for b in range(U):
                sp.sem_inc(y_stored[b].sem, 16)
            with sp.Fori(0, NI) as g:
                for b in range(U):
                    gathered[b].wait(sp, g, 0)
                    sp.sem_inc(begun.sem, 1)
                    load_index(g * U + (b + U), b)
                    down_done.wait(sp, g, 2 * b + 2)
                    sp.sem_inc(begun.sem, 1)
                    load_weights(g, b + 1)
                    for n in range(2):
                        y_taken[n].wait(sp, g, b + 1)
                    sp.sem_inc(begun.sem, 1)
                    y_stored[b].by(sp.dma_start(y_blocks[g * U + b], ys[:, b]))
            for b in range(U):
                sp.wait_ge(y_stored[b].sem, 16 * (NI + 1))
                sp.wait_ge(idx_in[b].sem, 16 * (NI + 1))
            sp.wait_ge(w_in[0].sem, 48 * (NBLK // 2 + 2))
            sp.wait_ge(w_in[1].sem, 48 * (NBLK // 2 + 1))

        @block.gpsimd
        def _(pool):
            pool.memset(idn[:], 0.0).then_inc(const_ready.sem, 1)
            pool.wait_ge(const_ready.sem, 1)
            pool.affine_select(out=idn[:], in_=idn[:], compare_op=ALU.not_equal, fill=1.0, base=0,
                               pattern=[[-1, P]], channel_multiplier=1).then_inc(const_ready.sem, 1)

            def gather(b):
                pool.sem_inc(pool_begun.sem, 1)
                gathered[b].by(pool.indirect_dma_start(xg[b][:], None, u_rows,
                                                       bass.IndirectOffsetOnAxis(ap=idx[b][:, 0:1], axis=0)))

            for b in range(U):
                idx_in[b].wait(pool, -1, 1)
                gather(b)
            with pool.Fori(0, NI) as g:
                for b in range(U):
                    idx_in[b].wait(pool, g, 1)
                    turned.wait(pool, g, b)
                    gather(b)
            for b in range(U):
                pool.wait_ge(gathered[b].sem, 16 * (NI + 1))

        @block.tensor
        def _(pe):
            def turn(g, b):
                gathered[b % U].wait(pe, g, b // U)
                xT_done.wait(pe, g, b - 1)
                for k in range(KD):
                    ins = pe.transpose(tps[:, k], xg[b % U][:, k * P:(k + 1) * P], idn[:])
                turned.by(ins)

            def gate_up(g, b, buf, k0):
                for k in range(k0, k0 + KD // 2):
                    ins = pe.matmul(gu[b % 2][:], xT[:, b % 2, k],
                                    wgu[:, bass.ds(buf, 1), k].rearrange("p one n -> p (one n)"),
                                    start=(k == 0), stop=(k == KD - 1))
                return ins

            pe.wait_ge(const_ready.sem, 2)
            turn(0, 0)
            pe.wait_ge(w_first.sem, 48)
            xT_done.wait(pe, 0, 0)
            gate_up(0, 0, 0, 0)
            gated.by(gate_up(0, 0, 0, KD // 2))
            with pe.Fori(0, NI) as g:
                for b in range(U):
                    if b == 0:
                        buf = planned(pe, g * U, 4, 1)
                    nbuf, even, odd = (planned(pe, g * U + (b + 1), c, top, low) for c, top, low in
                                       ((4, 1, 0), (5, 24 * NBLK + 96, 48), (6, 24 * NBLK + 96, 48)))
                    turn(g, b + 1)
                    pe.wait_ge(w_in[0].sem, even)
                    pe.wait_ge(w_in[1].sem, odd)
                    xT_done.wait(pe, g, b + 1)
                    gate_up(g, b + 1, nbuf, 0)
                    hid_done.wait(pe, g, b + 1)
                    for c in range(FC):
                        ins = pe.transpose(hp[:, c], hid[:, c * P:(c + 1) * P], idn[:])
                    h_turned.by(ins)
                    gated.by(gate_up(g, b + 1, nbuf, KD // 2))
                    hT_done.wait(pe, g, b + 1)
                    for n in range(2):
                        y_taken[n].wait(pe, g, b)
                        for c in range(FC):
                            ins = pe.matmul(yp[n][:], hT[:, c],
                                            wdn[:, bass.ds(buf, 1), c, n * (D // 2):(n + 1) * (D // 2)]
                                            .rearrange("p one n -> p (one n)"), start=(c == 0), stop=(c == FC - 1))
                        down_done.by(ins)
                    buf = nbuf

        @block.scalar
        def _(a):
            def take_x(g, b):
                turned.wait(a, g, b)
                xT_done.by(a.activation(xT[:, b % 2], tps[:], ACT.Copy))

            take_x(0, 0)
            a.sem_inc(y_taken[0].sem, 1)
            with a.Fori(0, NI) as g:
                for b in range(U):
                    gated.wait(a, g, b)
                    silu_done.by(a.activation(act_g[:], gu[b % 2][:, 0:F], ACT.Silu))
                    take_x(g, b + 1)
                    h_turned.wait(a, g, b + 1)
                    hT_done.by(a.activation(hT[:], hp[:], ACT.Copy))
                    down_done.wait(a, g, 2 * b + 1)
                    y_stored[b].wait(a, g, 0)
                    y_taken[0].by(a.activation(ys[:, b, 0:D // 2], yp[0][:], ACT.Copy))

        @block.vector
        def _(v):
            v.sem_inc(y_taken[1].sem, 1)
            with v.Fori(0, NI) as g:
                for b in range(U):
                    silu_done.wait(v, g, b + 1)
                    hid_done.by(v.tensor_tensor(hid[:], act_g[:], gu[b % 2][:, F:], ALU.mult))
                    down_done.wait(v, g, 2 * b + 2)
                    y_stored[b].wait(v, g, 0)
                    y_taken[1].by(v.tensor_copy(ys[:, b, D // 2:], yp[1][:]))


def combine(nc, h_rows, y_rows, slots, dest, final_g, out):
    with ExitStack() as ctx:
        def sb(name, shape, dt=F32):
            return ctx.enter_context(nc.sbuf_tensor(name, shape, dt))

        def sig(name, per=2, base=0, step=1):
            return Signal(ctx, nc, name, per, base, step)

        NBUF = 4
        fg, eps = sb("fg", [P, D]), sb("eps_f", [P, 1])
        ht = [sb(f"hf{b}", [P, D]) for b in range(NBUF)]
        y = [[sb(f"y{k}_{b}", [P, D]) for k in range(TOP)] for b in range(NBUF)]
        at = [sb(f"at_f{b}", [P, TOP], U32) for b in range(NBUF)]
        sq = [sb(f"sq_f{b}", [P, D]) for b in range(2)]
        wt = sb("wt_f", [P, NBUF, TOP])
        r = sb("r_f", [P, NBUF])
        consts_in, const_ready = sig("consts_in5", 0), sig("const_ready5", 0)
        h_in = [sig(f"hf_in{b}", 1, 0, 16) for b in range(NBUF)]
        y_in = [sig(f"yf_in{b}", 1, 0, 32) for b in range(NBUF)]
        index_done = [sig(f"index_done{b}", 1, 0, 1) for b in range(NBUF)]
        squared, rooted = sig("squared_f", NBUF), sig("rooted_f", NBUF)
        summed, scaled = sig("summed_f", NBUF), sig("scaled_f", NBUF, NBUF)
        stored = [sig(f"stored_f{b}", 1, 1, 16) for b in range(NBUF)]
        begun, pool_begun = sig("begun_f", 0), sig("pool_begun_f", 0)
        STEPS = 3
        step = Chain(ctx, nc, "dve_step5", NBUF * STEPS)
        block = ctx.enter_context(nc.Block())
        h_tiles, out_tiles = (t.rearrange("(t p) n -> t p n", p=P) for t in (h_rows, out))
        NI = NT // NBUF

        @block.sync
        def _(sp):
            sp.dma_start(fg[:], final_g.partition_broadcast(P)).then_inc(consts_in.sem, 16)
            for b in range(NBUF):
                sp.sem_inc(stored[b].sem, 16)
            with sp.Fori(0, NI) as g:
                for b in range(NBUF):
                    stored[b].wait(sp, g, 0)
                    sp.sem_inc(begun.sem, 1)
                    h_in[b].by(sp.dma_start(ht[b][:], h_tiles[g * NBUF + b]))
            for b in range(NBUF):
                sp.wait_ge(stored[b].sem, 16 * (NI + 1))

        @block.gpsimd
        def _(pool):
            pool.memset(eps[:], EPS).then_inc(const_ready.sem, 1)
            with pool.Fori(0, NI) as g:
                for b in range(NBUF):
                    scaled.wait(pool, g, b + 1 - NBUF)
                    index_done[b].by(pool.tensor_copy(at[b][:], dest[:, bass.ds(g * NBUF + b, 1)]
                                                      .rearrange("p one k -> p (one k)")))
                    index_done[b].wait(pool, g, 1)
                    pool.sem_inc(pool_begun.sem, 1)
                    for k in range(TOP):
                        pool.indirect_dma_start(y[b][k][:], None, y_rows,
                                                bass.IndirectOffsetOnAxis(ap=at[b][:, k:k + 1], axis=0)
                                                ).then_inc(y_in[b].sem, 16)

        @block.scalar
        def _(a):
            a.wait_ge(const_ready.sem, 1)
            with a.Fori(0, NI) as g:
                for b in range(NBUF):
                    summed.wait(a, g, b + 1)
                    squared.by(a.activation(sq[b % 2][:], ht[b][:], ACT.Square, accum_out=r[:, b:b + 1]))
                    squared.wait(a, g, b + 1)
                    rooted.by(a.activation(r[:, b:b + 1], r[:, b:b + 1], ACT.Sqrt, bias=eps[:, 0:1], scale=1.0 / D))
                    if b > 0:
                        scaled.wait(a, g, b)
                        stored[b - 1].by(a.dma_start(out_tiles[g * NBUF + (b - 1)], ht[b - 1][:]))
                scaled.wait(a, g, NBUF)
                stored[NBUF - 1].by(a.dma_start(out_tiles[g * NBUF + (NBUF - 1)], ht[NBUF - 1][:]))

        @block.vector
        def _(v):
            def chained(ins):
                step.step(ins)
                step.wait(v)

            v.wait_ge(consts_in.sem, 16)
            v.sem_inc(scaled.sem, NBUF)
            with v.Fori(0, NI) as g:
                step.enter(g)

                def add(b):
                    h_in[b].wait(v, g, 1)
                    y_in[b].wait(v, g, 1)
                    chained(v.tensor_copy(wt[:, b], slots[:, bass.ds(g * NBUF + b, 1), 4:6]
                                          .rearrange("p one k -> p (one k)")))
                    chained(v.scalar_tensor_tensor(out=ht[b][:], in0=y[b][0][:], scalar=wt[:, b, 0:1],
                                                   in1=ht[b][:], op0=ALU.mult, op1=ALU.add))
                    summed.by(v.scalar_tensor_tensor(out=ht[b][:], in0=y[b][1][:], scalar=wt[:, b, 1:2],
                                                     in1=ht[b][:], op0=ALU.mult, op1=ALU.add))

                def scale(b):
                    rooted.wait(v, g, b + 1)
                    chained(v.reciprocal(r[:, b:b + 1], r[:, b:b + 1]))
                    scaled.by(v.scalar_tensor_tensor(out=ht[b][:], in0=ht[b][:], scalar=r[:, b:b + 1], in1=fg[:],
                                                     op0=ALU.mult, op1=ALU.mult))

                for b in range(NBUF):
                    add(b)
                    if b > 0:
                        scale(b - 1)
                scale(NBUF - 1)
                step.leave()


def build(nc, x, out, norm1_g, w_in, conv_w, conv_b, w_rg, b_rg, w_ig, b_ig, lru_lambda, attn_sinks,
          rnn_out_g, attn_out_g, w_out, norm2_g, w_group_router, w_expert_router, w_gate, w_up, w_down, final_g):
    def dram(name, shape, dt=F32):
        return nc.dram_tensor(name, shape, dt).ap()

    mixT = dram("mixT", (2 * RC, P, T))
    h_rows, u_rows = dram("h_rows", (T, D)), dram("u_rows", (T, D))
    lists = dram("lists", (E * LIST, 1), I32)
    plan_dram = dram("plan_dram", (P, 8), I32)
    y_rows = dram("y_rows", (NBLK * P, D))
    xr, outr = x[0], out[0]
    project_and_mix(nc, xr, norm1_g, w_in, conv_w, conv_b, w_rg, b_rg, w_ig, b_ig, lru_lambda, attn_sinks, mixT)
    with (nc.sbuf_tensor("slots", [P, NT, 3 * TOP], F32) as slots,
          nc.sbuf_tensor("dest", [P, NT, TOP], U32) as dest):
        with (nc.sbuf_tensor("seen_out", [P, E], BF16) as seen,
              nc.sbuf_tensor("plan", [1, P * 8], I32) as plan):
            project_out(nc, xr, mixT, rnn_out_g, attn_out_g, w_out, norm2_g, w_group_router, w_expert_router,
                        h_rows, u_rows, lists, slots, seen)
            plan_blocks(nc, seen, slots, plan_dram, plan, dest)
            run_experts(nc, plan, lists, u_rows, w_gate, w_up, w_down, y_rows)
        combine(nc, h_rows, y_rows, slots, dest, final_g, outr)


_INS = ['x', 'norm1_g', 'w_in', 'conv_w', 'conv_b', 'w_rg', 'b_rg', 'w_ig', 'b_ig', 'lru_lambda', 'attn_sinks',
        'rnn_out_g', 'attn_out_g', 'w_out', 'norm2_g', 'w_group_router', 'w_expert_router', 'w_gate', 'w_up',
        'w_down', 'final_g']


def kernel(**inputs):
    import concourse.bacc as _bacc
    from concourse.bass_utils import run_bass_kernel_spmd as _run

    nc = _bacc.Bacc("TRN2", target_bir_lowering=False, num_devices=1)
    arrays, aps = {}, {}
    for name in _INS:
        a = np.ascontiguousarray(inputs[name])
        arrays[f"in_{name}"] = a
        aps[name] = nc.dram_tensor(f"in_{name}", a.shape, mybir.dt.from_np(a.dtype), kind="ExternalInput").ap()
    x = aps.pop("x")
    out = nc.dram_tensor("out_dram", (1, T, D), F32, kind="ExternalOutput").ap()
    build(nc, x, out, **aps)
    r = _run(nc, [arrays], core_ids=[0])
    return r.results[0]["out_dram"]
```

```python
from contextlib import ExitStack

import numpy as np

import concourse.bass as bass
from concourse import mybir

ALU = mybir.AluOpType
ACT = mybir.ActivationFunctionType
AX = mybir.AxisListType
F32 = mybir.dt.float32
F32R = mybir.dt.float32r
BF16 = mybir.dt.bfloat16
I32 = mybir.dt.int32
U32 = mybir.dt.uint32

P = 128
D = 1024
KD = D // P
T = 4096
EPS = 1e-6
D_RNN = 512
RC = D_RNN // P
CONV = 4
LRU_C = 8.0
CHUNK = 64
HEADS, KV, HD = 8, 2, 64
G = HEADS // KV
D_ATTN = HEADS * HD
D_IN = 2 * D_RNN + D_ATTN + 2 * KV * HD
Q0, K0, V0 = 2 * D_RNN, 2 * D_RNN + D_ATTN, 2 * D_RNN + D_ATTN + KV * HD
GROUPS, EPG = 4, 8
E = GROUPS * EPG
TOP = 2
F = 256
FC = F // P
NEG = -1e30

TOK = 256
NG = T // TOK
TJ = TOK // P
NT = T // P
LIST = T + P
NB = T * TOP // P + E - 1
NBLK = NB + NB % 2
GELU_K, GELU_C = (2 / np.pi) ** 0.5, 0.044715


class Signal:

    def __init__(self, ctx, nc, name, per, base=0, step=1):
        self.sem, self.per, self.base, self.step = ctx.enter_context(nc.semaphore(name)), per, base, step

    def wait(self, eng, g, n):
        value = (g * self.per + (self.base + n)) * self.step
        if not isinstance(value, int) or value > 0:
            eng.wait_ge(self.sem, value)

    def by(self, ins):
        ins.then_inc(self.sem, self.step)


class Chain:

    def __init__(self, ctx, nc, name, per=0):
        self.sem, self.per, self.before, self.n, self.g = ctx.enter_context(nc.semaphore(name)), per, 0, 0, None

    def step(self, ins):
        ins.then_inc(self.sem, 1)
        self.n += 1

    def enter(self, g):
        self.before, self.n, self.g = self.before + self.n, 0, g

    def leave(self):
        assert self.n == self.per, (self.n, self.per)

    def wait(self, eng):
        if self.g is None:
            eng.wait_ge(self.sem, self.before + self.n)
        else:
            eng.wait_ge(self.sem, self.g * self.per + (self.before + self.n))


def product3(pe, out, w_hi, w_lo, x_hi, x_lo, first, last):
    pe.matmul(out, w_lo, x_hi, start=first, stop=False)
    pe.matmul(out, w_hi, x_lo, start=False, stop=False)
    return pe.matmul(out, w_hi, x_hi, start=False, stop=last)


def project_and_mix(nc, x, norm1_g, w_in, conv_w, conv_b, w_rg, b_rg, w_ig, b_ig, lru_lambda, attn_sinks, mixT):
    with ExitStack() as ctx:
        def sb(name, shape, dt=F32):
            return ctx.enter_context(nc.sbuf_tensor(name, shape, dt))

        def ps(name, shape):
            return ctx.enter_context(nc.psum_tensor(name, shape, F32))

        def sig(name, per, base=0, step=1):
            return Signal(ctx, nc, name, per, base, step)

        w_hi, w_lo = sb("w_hi", [P, KD, D_IN], F32R), sb("w_lo", [P, KD, D_IN], F32R)
        u_hi, u_lo = sb("u_hi", [P, KD, TOK], F32R), sb("u_lo", [P, KD, TOK], F32R)
        xt = sb("xt", [P, TJ, D])
        xr = sb("xr", [P, RC, CONV - 1 + TOK])
        yg = sb("yg", [P, RC, TOK])
        ao = sb("ao", [P, RC, TOK])
        t1 = sb("t1", [P, RC, TOK])
        xc = sb("xc", [P, RC, TOK])
        rr = sb("rr", [P, RC, TOK])
        ig = sb("ig", [P, RC, TOK])
        qT = sb("qT", [P, G, TOK])
        kT, vT = sb("kT", [P, CHUNK + TOK]), sb("vT", [P, CHUNK + TOK])
        vb = sb("vb", [P, TOK // CHUNK, P])
        ss = sb("ss", [P, TJ, HEADS, P])
        stage = [t[:].rearrange("p c t -> p (c t)")[:, 0:D_IN // 2] for t in (rr, ig, t1, xc)]
        pT = sb("pT", [P, HEADS, P])
        bT = sb("bT", [P, G, TOK])
        bias = sb("bias", [P, 2, HEADS, P])
        wg = sb("wg", [P, RC, 2, P])
        ident = sb("ident", [P, P])
        g1 = sb("g1", [P, KD])
        cw, cb = sb("cw", [P, CONV, RC]), sb("cb", [P, RC])
        brg, big, lam = sb("brg", [P, RC]), sb("big", [P, RC]), sb("lam", [P, RC])
        la, lb, lc, ld, le = (sb(n, [P, RC]) for n in ("la", "lb", "lc", "ld", "le"))
        sp4 = sb("sp4", [P, RC])
        sink, neg_sink = sb("sink", [P, HEADS]), sb("neg_sink", [P, HEADS])
        carry = sb("carry", [P, RC])
        ssq, rstd = sb("ssq", [P, TJ]), sb("rstd", [P, TJ])
        eps = sb("eps", [P, 1])
        mx, nm, sd, den, rs = (sb(n, [P, HEADS]) for n in ("mx", "nm", "sd", "den", "rs"))

        bank = [ps(f"proj{b}", [P, 512]) for b in range(2)]
        tp = ps("tp", [P, KD, P])
        sc = ps("sc", [P, HEADS, P])
        gt = ps("gt", [P, 2, TOK])
        ot = ps("ot", [P, G, P])

        NCH = D_IN // P

        def w_cols(w, k, m):
            if m < 2:
                c0 = (V0, K0)[m]
            elif m < 2 + G:
                c0 = Q0 + (m - 2) * P
            else:
                c0 = (m - 2 - G) * P
            return w[:, k, c0:c0 + P]

        consts_in = sig("consts_in", 0)
        gate_w_zero, const_ready = sig("gate_w_zero", 0), sig("const_ready", 0)
        tables_ready, lambda_abs, lambda_exp = sig("tables_ready", 0), sig("lambda_abs", 0), sig("lambda_exp", 0)
        w_staged = [sig(f"w_staged{b}", 1, step=(16, 4 * 16)[b % 2]) for b in range(4)]
        w_hi_done, w_lo_done = sig("w_hi_done", 4), sig("w_lo_done", 4)
        x_in = [sig(f"x_in{j}", 1, 1, 16) for j in range(TJ)]
        x_squared, rms_done, x_scaled = sig("x_squared", TJ, TJ), sig("rms_done", 1, 1), sig("x_scaled", TJ, TJ)
        u_transposed = sig("u_transposed", TJ, TJ)
        u_hi_done, u_lo_done = sig("u_hi_done", TJ, TJ), sig("u_lo_done", TJ, TJ)
        v_transposed, v_taken = sig("v_transposed", 1), sig("v_taken", 1)
        p_transposed, p_taken = sig("p_transposed", TJ), sig("p_taken", TJ)
        projected, proj_taken = sig("projected", NCH), sig("proj_taken", NCH, 2)
        scored, scores_taken = sig("scored", TJ), sig("scores_taken", TJ, 1)
        smax_done, exp_done, p_ready = sig("smax_done", TJ), sig("exp_done", TJ), sig("p_ready", TJ)
        pv_done, ot_taken = sig("pv_done", TJ, 1), sig("ot_taken", TJ, 1)
        conv_done, xr_free = sig("conv_done", RC), sig("xr_free", 1, 1)
        gelu_sq, gelu_poly, gelu_sig, gelu_done = (sig(f"gelu_{n}", 1) for n in ("sq", "poly", "sig", "done"))
        gated, gates_taken = sig("gated", RC), sig("gates_taken", RC, 1)
        s_done, sqrt_done, rnn_done = sig("s_done", 1), sig("sqrt_done", 1), sig("rnn_done", 1, 1)
        a_stored, b_stored = sig("a_stored", 1, 1, 16), sig("b_stored", 1, 1, 16)
        stores_begun = sig("stores_begun", 2)
        step = Chain(ctx, nc, "dve_step", 4 * TJ + 3 * RC + 12)

        NCONST, CONST_STEPS = 6 + CONV + 4, 9
        x_tiles = x.rearrange("(t p) n -> t p n", p=P)
        mix_rows = mixT.rearrange("c p t -> p c t")
        block = ctx.enter_context(nc.Block())

        @block.sync
        def _(sp):
            w_rows = w_in[0].rearrange("(k p) n -> k p n", p=P)
            cut = D_IN // 2

            def stage_w(k, b):
                if b % 2 == 0:
                    w_staged[b].by(sp.dma_start(stage[b], w_rows[k, :, 0:cut]))
                    return
                pieces = [(stage[b][:, 0:Q0 - cut], w_rows[k, :, cut:Q0]),
                          (stage[b][:, K0 - cut:], w_rows[k, :, K0:])]
                for v in range(KV):
                    pieces.append((stage[b][:, Q0 - cut:K0 - cut].rearrange("p (c v d) -> p v c d", c=G, v=KV)[:, v],
                                   w_rows[k, :, Q0 + v * G * HD:Q0 + (v + 1) * G * HD]
                                   .rearrange("p (c d) -> p c d", c=G)))
                for dst, src in pieces:
                    sp.dma_start(dst, src).then_inc(w_staged[b].sem, 16)

            for b in range(4):
                stage_w(b // 2, b)
            for dst, src in ((g1, norm1_g), (cb, conv_b), (brg, b_rg), (big, b_ig), (lam, lru_lambda)):
                sp.dma_start(dst[:], src[0].rearrange("(c p) -> p c", p=P),
                             allow_slow_non_contiguous=True).then_inc(consts_in.sem, 16)
            sp.dma_start(sink[:], attn_sinks[0].partition_broadcast(P)).then_inc(consts_in.sem, 16)
            for k in range(CONV):
                sp.dma_start(cw[:, k, :], conv_w[0, k].rearrange("(c p) -> p c", p=P),
                             allow_slow_non_contiguous=True).then_inc(consts_in.sem, 16)
            for j in range(TJ):
                x_in[j].by(sp.dma_start(xt[:, j], x_tiles[j]))
            sp.wait_ge(gate_w_zero.sem, 1)
            for s, w in enumerate((w_rg, w_ig)):
                for half in range(2):
                    sp.dma_start(wg[64 * half:64 * half + 64, :, s, 64 * half:64 * half + 64],
                                 w[0].rearrange("(c h) i o -> h i c o", h=2)[half]).then_inc(consts_in.sem, 16)
            with sp.Fori(1, KD // 2) as k:
                for b in range(4):
                    w_lo_done.wait(sp, k, b - 3)
                    sp.sem_inc(stores_begun.sem, 1)
                    stage_w(k * 2 + b // 2, b)
            sp.sem_inc(a_stored.sem, 16)
            sp.sem_inc(b_stored.sem, 16)

            def load_x(nxt, g):
                for j in range(TJ):
                    u_transposed.wait(sp, g, j + 1 - TJ)
                    x_in[j].by(sp.dma_start(xt[:, j], x_tiles[nxt * TJ + j]))

            def store_a(g):
                rnn_done.wait(sp, g, 1)
                sp.sem_inc(stores_begun.sem, 1)
                a_stored.by(sp.dma_start(mix_rows[:, 0:RC, bass.ds(g * TOK, TOK)], ao[:]))

            def store_b(g):
                ot_taken.wait(sp, g, TJ)
                sp.sem_inc(stores_begun.sem, 1)
                b_stored.by(sp.dma_start(mix_rows[:, RC:, bass.ds(g * TOK, TOK)], bT[:]))

            load_x(1, 0)
            store_b(0)
            with sp.Fori(1, NG) as g:
                load_x(sp.snap((g + 1) % NG), g)
                store_a(g - 1)
                store_b(g)
            store_a(NG - 1)
            for s in (x_in[0], x_in[1], a_stored, b_stored):
                sp.wait_ge(s.sem, 16 * (NG + 1))

        @block.gpsimd
        def _(pool):
            pool.memset(wg[:], 0.0).then_inc(gate_w_zero.sem, 1)
            pool.memset(ident[:], 0.0).then_inc(const_ready.sem, 1)
            pool.wait_ge(const_ready.sem, 1)
            pool.affine_select(out=ident[:], in_=ident[:], compare_op=ALU.not_equal, fill=1.0, base=0,
                               pattern=[[-1, P]], channel_multiplier=1).then_inc(const_ready.sem, 1)
            pool.memset(eps[:], EPS).then_inc(const_ready.sem, 1)
            for half in range(2):
                pool.wait_ge(const_ready.sem, 3 + half)
                pool.iota(pT[64 * half:64 * half + 64, 0, :].bitcast(I32), pattern=[[-1, P]], base=CHUNK,
                          channel_multiplier=1).then_inc(const_ready.sem, 1)
            pool.wait_ge(const_ready.sem, 5)
            for t in (xr, kT, vT, carry):
                pool.memset(t[:], 0.0).then_inc(const_ready.sem, 1)

        @block.tensor
        def _(pe):
            def transpose_u(g, j):
                x_scaled.wait(pe, g, j + 1)
                for k in range(KD):
                    ins = pe.transpose((tp, sc)[j][:, k], xt[:, j, k * P:(k + 1) * P], ident[:])
                u_transposed.by(ins)

            def project(g, m):
                proj_taken.wait(pe, g, m - 1)
                for k in range(KD):
                    ins = product3(pe, bank[m % 2][:, 0:TOK], w_cols(w_hi, k, m), w_cols(w_lo, k, m),
                                   u_hi[:, k], u_lo[:, k], k == 0, k == KD - 1)
                projected.by(ins)

            def transpose_v(g):
                proj_taken.wait(pe, g, 1)
                for c in range(TOK // CHUNK):
                    ins = pe.transpose(tp[:, c], vT[:, c * CHUNK:c * CHUNK + P], ident[:])
                v_transposed.by(ins)

            def score(g, j):
                for h in range(HEADS):
                    kv = slice(64 * (h // G), 64 * (h // G) + 64)
                    for half in range(2):
                        c = 2 * j + half
                        ins = pe.matmul(sc[64 * half:64 * half + 64, h], qT[kv, h % G, c * CHUNK:(c + 1) * CHUNK],
                                        kT[kv, c * CHUNK:c * CHUNK + P], start=True, stop=True)
                scored.by(ins)

            def transpose_p(g, j):
                p_ready.wait(pe, g, j + 1)
                for h in range(HEADS):
                    ins = pe.transpose(tp[:, h], ss[:, j, h], ident[:])
                p_transposed.by(ins)

            def attend(g, j):
                p_taken.wait(pe, g, j + 1)
                ot_taken.wait(pe, g, j)
                for v in range(KV):
                    for half in range(2):
                        ins = pe.matmul(ot[64 * v:64 * v + 64, :, 64 * half:64 * half + 64],
                                        vb[:, 2 * j + half, 64 * v:64 * v + 64],
                                        pT[:, G * v:G * v + G, 64 * half:64 * half + 64], start=True, stop=True)
                pv_done.by(ins)

            def gate(g, c):
                conv_done.wait(pe, g, c + 1)
                gates_taken.wait(pe, g, c)
                for s in range(2):
                    ins = pe.matmul(gt[:, s], wg[:, c, s], xc[:, c], start=True, stop=True)
                gated.by(ins)

            pe.wait_ge(const_ready.sem, CONST_STEPS)
            pe.wait_ge(consts_in.sem, 16 * NCONST)
            for j in range(TJ):
                transpose_u(-1, j)
            pe.wait_ge(w_lo_done.sem, 2 * KD)
            pe.sem_inc(pv_done.sem, 1)

            def group(g):
                u_lo_done.wait(pe, g, 0)
                for m in range(2 + G):
                    project(g, m)
                transpose_v(g)
                proj_taken.wait(pe, g, 2 + G)
                project(g, 6)
                score(g, 0)
                project(g, 7)
                scores_taken.wait(pe, g, 1)
                project(g, 8)
                score(g, 1)
                project(g, 9)
                project(g, 10)
                v_taken.wait(pe, g, 1)
                transpose_p(g, 0)
                gate(g, 0)
                project(g, 11)
                attend(g, 0)
                gate(g, 1)
                project(g, 12)
                transpose_p(g, 1)
                gate(g, 2)
                project(g, 13)
                p_taken.wait(pe, g, 2)
                transpose_u(g, 0)
                scores_taken.wait(pe, g, 2)
                transpose_u(g, 1)
                gate(g, 3)
                attend(g, 1)

            group(0)
            with pe.Fori(1, NG) as g:
                group(g)
        @block.scalar
        def _(a):
            def square_x(g, j):
                x_in[j].wait(a, g, 1)
                x_squared.by(a.activation(ss[:, j].rearrange("p h n -> p (h n)"), xt[:, j], ACT.Square,
                                          accum_out=ssq[:, j:j + 1]))

            def rms(g):
                x_squared.wait(a, g, TJ)
                rms_done.by(a.activation(ssq[:], ssq[:], ACT.Sqrt, bias=eps[:, 0:1], scale=1.0 / D))

            def take_hi(g, j):
                u_transposed.wait(a, g, j + 1)
                u_hi_done.by(a.activation(u_hi[:, :, j * P:(j + 1) * P], (tp, sc)[j][:], ACT.Copy))

            a.wait_ge(consts_in.sem, 16 * NCONST)
            with a.Fori(0, KD // 2) as k:
                for b in range(4):
                    kk = k * 2 + b // 2
                    w_staged[b].wait(a, k, 1)
                    w_hi_done.by(a.activation(w_hi[:, bass.ds(kk, 1), bass.ts(b % 2, D_IN // 2)]
                                              .rearrange("p one n -> p (one n)"), stage[b], ACT.Copy,
                                              scale=g1[:, bass.ds(kk, 1)]))
            a.wait_ge(lambda_abs.sem, 1)
            a.activation(lb[:], la[:], ACT.Exp, scale=-1.0).then_inc(lambda_exp.sem, 1)
            a.wait_ge(const_ready.sem, CONST_STEPS)
            for j in range(TJ):
                square_x(-1, j)
            rms(-1)
            for j in range(TJ):
                take_hi(-1, j)
            a.wait_ge(tables_ready.sem, 1)
            a.sem_inc(proj_taken.sem, 2)
            a.sem_inc(gates_taken.sem, 1)
            a.sem_inc(ot_taken.sem, 1)

            def take(g, m, dst, scale=1.0):
                projected.wait(a, g, m + 1)
                proj_taken.by(a.activation(dst, bank[m % 2][:, 0:TOK], ACT.Copy, scale=scale))

            def exps(g, j):
                smax_done.wait(a, g, j + 1)
                for h in range(HEADS):
                    a.activation(ss[:, j, h], ss[:, j, h], ACT.Exp, bias=nm[:, h:h + 1],
                                 accum_out=den[:, h:h + 1])
                exp_done.by(a.activation(sd[:], sd[:], ACT.Exp))

            def take_p(g, j):
                p_transposed.wait(a, g, j + 1)
                pv_done.wait(a, g, j)
                p_taken.by(a.activation(pT[:], tp[:], ACT.Copy))

            def take_o(g, j):
                pv_done.wait(a, g, j + 1)
                ot_taken.by(a.activation(bT[:, :, j * P:(j + 1) * P], ot[:], ACT.Copy))

            def take_gates(g, c):
                gated.wait(a, g, c + 1)
                a.activation(rr[:, c], gt[:, 0], ACT.Sigmoid, bias=brg[:, c:c + 1])
                gates_taken.by(a.activation(ig[:, c], gt[:, 1], ACT.Sigmoid, bias=big[:, c:c + 1]))

            def gelu_sigmoid(g):
                gelu_poly.wait(a, g, 1)
                gelu_sig.by(a.activation(t1[:], t1[:], ACT.Sigmoid, scale=2 * GELU_K * GELU_C))

            def decay(g):
                gates_taken.wait(a, g, RC)
                for c in range(RC):
                    ins = a.activation(rr[:, c], rr[:, c], ACT.Tanh, scale=sp4[:, c:c + 1])
                s_done.by(ins)

            def decay_root(g):
                s_done.wait(a, g, 1)
                gelu_done.wait(a, g, 1)
                sqrt_done.by(a.activation(t1[:], rr[:], ACT.Sqrt))

            def group(g):
                first = isinstance(g, int)
                take(g, 0, vT[:, CHUNK:])
                if not first:
                    gelu_sigmoid(g - 1)
                take(g, 1, kT[:, CHUNK:])
                if not first:
                    decay_root(g - 1)
                take(g, 2, qT[:, 0], scale=HD ** -0.5)
                for j in range(TJ):
                    square_x(g, j)
                    take(g, 3 + j, qT[:, 1 + j], scale=HD ** -0.5)
                rms(g)
                take(g, 5, qT[:, 3], scale=HD ** -0.5)
                v_transposed.wait(a, g, 1)
                v_taken.by(a.activation(vb[:], tp[:, 0:TOK // CHUNK], ACT.Copy))
                xr_free.wait(a, g, 0)
                take(g, 6, xr[:, 0, CONV - 1:])
                take(g, 7, xr[:, 1, CONV - 1:])
                exps(g, 0)
                take(g, 8, xr[:, 2, CONV - 1:])
                take(g, 9, xr[:, 3, CONV - 1:])
                exps(g, 1)
                rnn_done.wait(a, g, 0)
                b_stored.wait(a, g, 0)
                take(g, 10, yg[:, 0])
                take_p(g, 0)
                take_gates(g, 0)
                take(g, 11, yg[:, 1])
                take_o(g, 0)
                take_gates(g, 1)
                take(g, 12, yg[:, 2])
                take_p(g, 1)
                take_gates(g, 2)
                a.activation(kT[:, 0:CHUNK], kT[:, TOK:], ACT.Copy)
                a.activation(vT[:, 0:CHUNK], vT[:, TOK:], ACT.Copy)
                take(g, 13, yg[:, 3])
                for j in range(TJ):
                    take_hi(g, j)
                proj_taken.wait(a, g, NCH)
                gelu_sq.by(a.activation(t1[:], yg[:], ACT.Square))
                take_gates(g, 3)
                take_o(g, 1)
                decay(g)

            group(0)
            with a.Fori(1, NG) as g:
                group(g)
            gelu_sigmoid(NG - 1)
            decay_root(NG - 1)

        @block.vector
        def _(v):
            def chained(ins):
                step.step(ins)
                step.wait(v)

            def scale_x(g):
                rms_done.wait(v, g, 1)
                chained(v.reciprocal(rstd[:], ssq[:]))
                for j in range(TJ):
                    x_scaled.by(v.tensor_scalar(xt[:, j], xt[:, j], rstd[:, j:j + 1], None, ALU.mult))

            def take_lo(g, j):
                u_hi_done.wait(v, g, j + 1)
                u_lo_done.by(v.tensor_tensor(u_lo[:, :, j * P:(j + 1) * P], (tp, sc)[j][:],
                                             u_hi[:, :, j * P:(j + 1) * P].bitcast(F32), ALU.subtract))

            v.wait_ge(consts_in.sem, 16 * NCONST)
            v.tensor_scalar(lc[:], lam[:], -1.0, None, ALU.mult).then_inc(step.sem, 1)
            step.n += 1
            step.wait(v)
            v.tensor_tensor(la[:], lam[:], lc[:], ALU.max).then_inc(lambda_abs.sem, 1)
            with v.Fori(0, KD // 2) as k:
                for b in range(4):
                    kk = k * 2 + b // 2
                    w_hi_done.wait(v, k, b + 1)
                    hi, lo = (w[:, bass.ds(kk, 1), bass.ts(b % 2, D_IN // 2)].rearrange("p one n -> p (one n)")
                              for w in (w_hi, w_lo))
                    w_lo_done.by(v.scalar_tensor_tensor(out=lo, in0=stage[b], scalar=g1[:, bass.ds(kk, 1)],
                                                        in1=hi.bitcast(F32), op0=ALU.mult, op1=ALU.subtract))
            v.wait_ge(lambda_exp.sem, 1)
            chained(v.tensor_scalar(ld[:], lb[:], 2.0, None, ALU.add))
            chained(v.reciprocal(ld[:], ld[:]))
            chained(v.tensor_tensor(lb[:], lb[:], ld[:], ALU.mult))
            chained(v.tensor_tensor(ld[:], lb[:], lb[:], ALU.mult))
            TERMS = 9
            chained(v.tensor_scalar(le[:], ld[:], 1.0 / (2 * TERMS - 1), 1.0 / (2 * TERMS - 3), ALU.mult, ALU.add))
            for n in range(TERMS - 3, -1, -1):
                chained(v.tensor_tensor(le[:], le[:], ld[:], ALU.mult))
                chained(v.tensor_scalar(le[:], le[:], 1.0 / (2 * n + 1), None, ALU.add))
            chained(v.tensor_tensor(le[:], le[:], lb[:], ALU.mult))
            chained(v.tensor_scalar(lc[:], lc[:], 0.0, LRU_C / 2, ALU.max, ALU.mult))
            chained(v.scalar_tensor_tensor(out=sp4[:], in0=le[:], scalar=LRU_C, in1=lc[:],
                                           op0=ALU.mult, op1=ALU.add))
            chained(v.tensor_scalar(neg_sink[:], sink[:], -1.0, None, ALU.mult))
            v.wait_ge(const_ready.sem, CONST_STEPS)
            chained(v.tensor_copy(pT[:, 1], pT[:, 0].bitcast(I32)))
            chained(v.tensor_scalar(pT[:, 2], pT[:, 1], -1.0, None, ALU.mult))
            chained(v.tensor_tensor(pT[:, 3], pT[:, 1], pT[:, 2], ALU.min))
            for h in range(HEADS):
                for b in range(2):
                    chained(v.tensor_scalar(bias[:, b, h], pT[:, 3], 2.0 ** (-8.0 * (h + 1) / HEADS), None, ALU.mult))
            chained(v.memset(bias[0:CHUNK, 0, :, 0:CHUNK], NEG))
            scale_x(-1)
            for j in range(TJ):
                take_lo(-1, j)
            v.sem_inc(scores_taken.sem, 1)
            v.sem_inc(xr_free.sem, 1)
            v.sem_inc(rnn_done.sem, 1)
            v.sem_inc(tables_ready.sem, 1)

            def softmax_max(g, j):
                scored.wait(v, g, j + 1)
                table = 0 if isinstance(g, int) and j == 0 else 1
                scores_taken.by(v.tensor_tensor(ss[:, j], sc[:], bias[:, table], ALU.add))
                scores_taken.wait(v, g, j + 1)
                chained(v.tensor_reduce(mx[:], ss[:, j], AX.X, ALU.max, negate=True))
                chained(v.tensor_tensor(nm[:], mx[:], neg_sink[:], ALU.min))
                smax_done.by(v.tensor_tensor(sd[:], sink[:], nm[:], ALU.add))

            def softmax_scale(g, j):
                exp_done.wait(v, g, j + 1)
                chained(v.tensor_tensor(rs[:], den[:], sd[:], ALU.add))
                chained(v.reciprocal(rs[:], rs[:]))
                p_ready.by(v.tensor_tensor(ss[:, j], ss[:, j],
                                           rs[:].unsqueeze(2).to_broadcast([P, HEADS, P]), ALU.mult))

            def conv(g, c):
                proj_taken.wait(v, g, 2 + G + c + 1)
                chained(v.tensor_scalar(xc[:, c], xr[:, c, 0:TOK], cw[:, 0, c:c + 1], cb[:, c:c + 1],
                                        ALU.mult, ALU.add))
                for k in range(1, CONV):
                    ins = v.scalar_tensor_tensor(out=xc[:, c], in0=xr[:, c, k:k + TOK],
                                                 scalar=cw[:, k, c:c + 1], in1=xc[:, c],
                                                 op0=ALU.mult, op1=ALU.add)
                    conv_done.by(ins) if k == CONV - 1 else chained(ins)

            def recur(g):
                gelu_sig.wait(v, g, 1)
                gelu_done.by(v.tensor_tensor(yg[:], yg[:], t1[:], ALU.mult))
                gates_taken.wait(v, g, RC)
                step.step(v.tensor_tensor(ig[:], ig[:], xc[:], ALU.mult))
                sqrt_done.wait(v, g, 1)
                chained(v.tensor_scalar(rr[:], rr[:], 1.0, None, ALU.add))
                chained(v.reciprocal(rr[:], rr[:]))
                step.step(v.tensor_scalar(xc[:], rr[:], 2.0, -1.0, ALU.mult, ALU.add))
                chained(v.tensor_tensor(t1[:], t1[:], rr[:], ALU.mult))
                chained(v.scalar_tensor_tensor(out=ig[:].rearrange("p c t -> p (c t)"),
                                               in0=t1[:].rearrange("p c t -> p (c t)"), scalar=2.0,
                                               in1=ig[:].rearrange("p c t -> p (c t)"),
                                               op0=ALU.mult, op1=ALU.mult))
                for c in range(RC):
                    step.step(v.tensor_tensor_scan(rr[:, c], xc[:, c], ig[:, c], carry[:, c:c + 1],
                                                   ALU.mult, ALU.add))
                step.wait(v)
                chained(v.tensor_copy(carry[:], rr[:, :, TOK - 1]))
                gelu_done.wait(v, g, 1)
                a_stored.wait(v, g, 0)
                rnn_done.by(v.tensor_tensor(ao[:], rr[:], yg[:], ALU.mult))

            def group(g):
                if not isinstance(g, int):
                    recur(g - 1)
                scale_x(g)
                softmax_max(g, 0)
                conv(g, 0)
                conv(g, 1)
                softmax_scale(g, 0)
                softmax_max(g, 1)
                conv(g, 2)
                conv(g, 3)
                softmax_scale(g, 1)
                xr_free.by(v.tensor_copy(xr[:, :, 0:CONV - 1], xr[:, :, TOK:TOK + CONV - 1]))
                for j in range(TJ):
                    take_lo(g, j)
                gelu_sq.wait(v, g, 1)
                gelu_poly.by(v.scalar_tensor_tensor(out=t1[:].rearrange("p c t -> p (c t)"),
                                                    in0=t1[:].rearrange("p c t -> p (c t)"), scalar=1.0 / GELU_C,
                                                    in1=yg[:].rearrange("p c t -> p (c t)"),
                                                    op0=ALU.add, op1=ALU.mult))

            group(0)
            step.before, step.n = step.before + step.n, 0
            with v.Fori(1, NG) as g:
                step.g = g - 1
                group(g)
                step.leave()
            step.g, step.before, step.n = None, step.before + (NG - 1) * step.per, 0
            recur(NG - 1)

def project_out(nc, x, mixT, rnn_out_g, attn_out_g, w_out, norm2_g, w_group_router, w_expert_router,
                h_rows, u_rows, lists, slots, seen_out):
    with ExitStack() as ctx:
        def sb(name, shape, dt=F32):
            return ctx.enter_context(nc.sbuf_tensor(name, shape, dt))

        def ps(name, shape):
            return ctx.enter_context(nc.psum_tensor(name, shape, F32))

        def sig(name, per=2, step=1):
            return Signal(ctx, nc, name, per, 0, step)

        N2 = D // 2
        R = GROUPS + E
        o_hi, o_lo = sb("o_hi", [P, KD, D], F32R), sb("o_lo", [P, KD, D], F32R)
        wst = sb("wst", [P, KD, D])
        og = sb("og", [P, KD])
        g2 = sb("g2", [P, D])
        wr = sb("wr", [P, KD, R])
        mt = sb("mt", [P, 2, KD, P])
        m_hi, m_lo = sb("m_hi", [P, 2, KD, P], F32R), sb("m_lo", [P, 2, KD, P], F32R)
        sq = sb("sq", [P, KD, P])
        xt, ht, ut = sb("x_tile", [P, 2, D]), sb("h_tile", [P, 2, D]), sb("u_tile", [P, 2, D])
        hsq = sb("hsq", [P, D])
        uT = sb("uT", [P, KD, P])
        ones, onesb = sb("ones", [P, 2]), sb("onesb", [P, P], BF16)
        before = sb("before", [P, P], BF16)
        idn = sb("idn", [P, P])
        epsc = sb("epsc", [P, 1])
        rab, rh = sb("rab", [P, 2, 2]), sb("rh", [P, 2])
        lg, g8, e8 = sb("lg", [P, 8]), sb("g8", [P, 8]), sb("e8", [P, 8])
        gi, ei = sb("gi", [P, 8], U32), sb("ei", [P, 8], U32)
        ngm, gif, pen = sb("ngm", [P, 1]), sb("gif", [P, 1]), sb("pen", [P, GROUPS])
        pg, gsum, ex, nl = sb("pg", [P, GROUPS]), sb("gsum", [P, 1]), sb("ex", [P, 1]), sb("nl", [P, 1])
        em, hot, sel = sb("em", [P, E]), sb("hot", [P, TOP, E]), sb("sel", [P, TOP, E])
        chosen, seen = sb("chosen", [P, E], BF16), sb("seen", [P, E], BF16)
        slot = sb("slot", [P, 6])
        at = [sb(f"at{b}", [P, TOP], U32) for b in range(2)]
        tokf, toki = sb("tokf", [P, 2]), [sb(f"toki{b}", [P, 1], I32) for b in range(2)]
        iota_i, iota_e = sb("iota_i", [P, E], I32), sb("iota_e", [P, E])
        tok0 = sb("tok0", [P, 2], I32)
        zeros = sb("zeros", [P, E * LIST // P], I32)

        pa, pb = ps("pa", [P, 2, N2]), ps("pb", [P, 2, N2])
        tps = ps("tps", [P, KD, P])
        sums = ps("sums", [P, 512])
        rt = ps("rt", [P, 512])
        LOGIT, RANK = 0, 64

        consts_in, const_ready = sig("consts_in2"), sig("const_ready2")
        w_half_in = [sig(f"w_half_in{s}") for s in range(2)]
        o_hi_done, o_lo_done = sig("o_hi_done"), sig("o_lo_done")
        lists_zero = sig("lists_zero")
        mix_in = [sig(f"mix_in{b}", 1, 32) for b in range(2)]
        m_hi_done, m_squared, m_lo_done = sig("m_hi_done"), sig("m_squared"), sig("m_lo_done")
        summed, roots, a_done, a_added = sig("summed"), sig("roots"), sig("a_done"), sig("a_added")
        b_done, b_added = sig("b_done"), sig("b_added")
        h_squared, h_root, u_ready = sig("h_squared"), sig("h_root"), sig("u_ready")
        h_stored = [sig(f"h_stored{b}", 1, 16) for b in range(2)]
        u_stored = [sig(f"u_stored{b}", 1, 16) for b in range(2)]
        u_turned, uT_done, routed = sig("u_turned"), sig("uT_done"), sig("routed")
        group_max, group_exp, expert_max, expert_exp = (sig(n) for n in ("group_max", "group_exp", "expert_max",
                                                                        "expert_exp"))
        chosen_done, ranked, slots_done = sig("chosen_done"), sig("ranked"), sig("slots_done")
        scattered = [sig(f"scattered{b}", 1, 32) for b in range(2)]
        at_free = Signal(ctx, nc, "at_free", 2, 2)
        sp_begun, pool_begun, settled, ranks_end = (sig(n) for n in ("sp_begun", "pool_begun", "settled", "ranks_end"))
        ROUTE_STEPS, RANK_STEPS, NORM_STEPS = 14, 6, 2
        step = Chain(ctx, nc, "dve_step2", 2 * (ROUTE_STEPS + RANK_STEPS + NORM_STEPS))
        NCONST, CONST_STEPS = 3, 14
        block = ctx.enter_context(nc.Block())
        x_tiles, h_tiles, u_tiles = (t.rearrange("(t p) n -> t p n", p=P) for t in (x, h_rows, u_rows))
        mix_cols = mixT.rearrange("c p t -> p c t")

        @block.sync
        def _(sp):
            def load(i, b):
                mix_t = mix_cols[:, :, bass.ds(i * P, P)]
                sp.dma_start(mt[:, b], mix_t).then_inc(mix_in[b].sem, 16)
                sp.dma_start(xt[:, b], x_tiles[i]).then_inc(mix_in[b].sem, 16)

            pieces = [[(og[:, 0:RC], rnn_out_g[0].rearrange("(c p) -> p c", p=P))], []]
            for v in range(KV):
                half = slice(64 * v, 64 * v + 64)
                pieces[1].append((og[half, RC:], attn_out_g[0].rearrange("(v c d) -> v d c", v=KV, c=G)[v]))
            for c in range(RC):
                pieces[0].append((wst[:, c], w_out[0, c * P:(c + 1) * P]))
            for v in range(KV):
                pieces[1].append((wst[64 * v:64 * v + 64, RC:],
                                  w_out[0, D_RNN:].rearrange("(v c d) n -> v d c n", v=KV, c=G)[v]))
            for s in range(2):
                for dst, src in pieces[s]:
                    sp.dma_start(dst, src, allow_slow_non_contiguous=True).then_inc(w_half_in[s].sem, 16)
                if s == 0:
                    load(0, 0)
            load(1, 1)
            sp.dma_start(g2[:], norm2_g[0].partition_broadcast(P)).then_inc(consts_in.sem, 16)
            sp.dma_start(wr[:, :, 0:GROUPS], w_group_router[0].rearrange("(k p) e -> p k e", p=P),
                         allow_slow_non_contiguous=True).then_inc(consts_in.sem, 16)
            sp.dma_start(wr[:, :, GROUPS:], w_expert_router[0].rearrange("(k p) e -> p k e", p=P),
                         allow_slow_non_contiguous=True).then_inc(consts_in.sem, 16)
            sp.wait_ge(const_ready.sem, CONST_STEPS)
            sp.dma_start(lists.rearrange("(p n) one -> p (n one)", p=P), zeros[:]).then_inc(lists_zero.sem, 16)

            def tile(g, b):
                m_lo_done.wait(sp, g, b + 1)
                m_squared.wait(sp, g, b + 1)
                a_added.wait(sp, g, b + 1)
                sp.sem_inc(sp_begun.sem, 1)
                if isinstance(g, int):
                    load((2 * g + b + 2) % NT, b)
                else:
                    load(sp.snap((g * 2 + (b + 2)) % NT), b)
                b_added.wait(sp, g, b + 1)
                sp.sem_inc(sp_begun.sem, 1)
                h_stored[b].by(sp.dma_start(h_tiles[g * 2 + b], ht[:, b]))
                u_ready.wait(sp, g, b + 1)
                sp.sem_inc(sp_begun.sem, 1)
                u_stored[b].by(sp.dma_start(u_tiles[g * 2 + b], ut[:, b]))

            for b in range(2):
                tile(0, b)
            with sp.Fori(1, NT // 2) as g:
                for b in range(2):
                    tile(g, b)
            sp.wait_ge(lists_zero.sem, 16)
            for b in range(2):
                sp.wait_ge(h_stored[b].sem, 16 * (NT // 2))
                sp.wait_ge(u_stored[b].sem, 16 * (NT // 2))
                sp.wait_ge(mix_in[b].sem, 32 * (NT // 2 + 1))

        @block.gpsimd
        def _(pool):
            made = 0

            def then(ins):
                nonlocal made
                made += 1
                ins.then_inc(const_ready.sem, 1)
                pool.wait_ge(const_ready.sem, made)

            then(pool.memset(zeros[:], 0))
            then(pool.memset(idn[:], 0.0))
            then(pool.affine_select(out=idn[:], in_=idn[:], compare_op=ALU.not_equal, fill=1.0, base=0,
                                    pattern=[[-1, P]], channel_multiplier=1))
            then(pool.memset(before[:], 1.0))
            then(pool.affine_select(out=before[:], in_=before[:], compare_op=ALU.is_gt, fill=0.0, base=0,
                                    pattern=[[1, P]], channel_multiplier=-1))
            then(pool.memset(onesb[:], 1.0))
            then(pool.memset(ones[:], 1.0))
            then(pool.memset(epsc[:], EPS))
            then(pool.memset(lg[:], NEG))
            then(pool.memset(seen[:], 0.0))
            then(pool.memset(hsq[:], 0.0))
            then(pool.iota(iota_i[:], pattern=[[1, E]], base=0, channel_multiplier=0))
            then(pool.iota(tok0[:], pattern=[[P, 2]], base=0, channel_multiplier=1))
            then(pool.memset(sq[:], 0.0))
            assert made == CONST_STEPS
            pool.wait_ge(lists_zero.sem, 16)
            pool.sem_inc(at_free.sem, 2)

            def scatter(g, b):
                slots_done.wait(pool, g, b + 1)
                pool.sem_inc(pool_begun.sem, 1)
                for k in range(TOP):
                    pool.indirect_dma_start(lists, bass.IndirectOffsetOnAxis(ap=at[b][:, k:k + 1], axis=0),
                                            toki[b][:], None).then_inc(scattered[b].sem, 16)
                scattered[b].wait(pool, g, 1)
                pool.sem_inc(at_free.sem, 1)

            for b in range(2):
                scatter(0, b)
            with pool.Fori(1, NT // 2) as g:
                for b in range(2):
                    scatter(g, b)

        @block.tensor
        def _(pe):
            def product(dst, half, b, c0):
                for c in range(RC):
                    k = c0 + c
                    cut = bass.ts(half, N2)
                    ins = product3(pe, dst[:, half], m_hi[:, b, k], m_lo[:, b, k],
                                   o_hi[:, k, cut], o_lo[:, k, cut], c == 0, c == RC - 1)
                return ins

            def sum_squares(g, b):
                m_squared.wait(pe, g, b + 1)
                roots.wait(pe, g, b)
                for s in range(2):
                    for c in range(RC):
                        ins = pe.matmul(sums[:, 2 * s:2 * s + 2], sq[:, RC * s + c], ones[:], start=(c == 0),
                                        stop=(c == RC - 1))
                summed.by(ins)

            def rank(g, b):
                chosen_done.wait(pe, g, b + 1)
                pe.matmul(rt[:, RANK:RANK + E], before[:], chosen[:], start=True, stop=False)
                ranked.by(pe.matmul(rt[:, RANK:RANK + E], onesb[:], seen[:], start=False, stop=True))

            def turn_u(g, b):
                u_ready.wait(pe, g, b + 1)
                uT_done.wait(pe, g, b)
                for k in range(KD):
                    ins = pe.transpose(tps[:, k], ut[:, b, k * P:(k + 1) * P], idn[:])
                u_turned.by(ins)

            def route(g, b):
                uT_done.wait(pe, g, b + 1)
                slots_done.wait(pe, g, b)
                for k in range(KD):
                    ins = pe.matmul(rt[:, LOGIT:LOGIT + R], uT[:, k], wr[:, k], start=(k == 0), stop=(k == KD - 1))
                routed.by(ins)

            pe.wait_ge(const_ready.sem, CONST_STEPS)
            sum_squares(0, 0)
            pe.wait_ge(o_lo_done.sem, RC)
            m_lo_done.wait(pe, 0, 1)
            product(pa, 0, 0, 0)
            a_done.by(product(pa, 1, 0, 0))
            pe.wait_ge(o_lo_done.sem, KD)
            pe.wait_ge(consts_in.sem, 16 * NCONST)

            def tile(g, b):
                first = isinstance(g, int) and b == 0
                b_added.wait(pe, g, b)
                product(pb, 0, b, RC)
                if not first:
                    route(g, b - 1)
                sum_squares(g, b + 1)
                b_done.by(product(pb, 1, b, RC))
                m_lo_done.wait(pe, g, b + 2)
                a_added.wait(pe, g, b + 1)
                product(pa, 0, 1 - b, 0)
                a_done.by(product(pa, 1, 1 - b, 0))
                if not first:
                    rank(g, b - 1)
                turn_u(g, b)

            for b in range(2):
                tile(0, b)
            with pe.Fori(1, NT // 2) as g:
                for b in range(2):
                    tile(g, b)
            route(NT // 2 - 1, 1)
            rank(NT // 2 - 1, 1)

        @block.scalar
        def _(a):
            def split(g, b):
                mix_in[b % 2].wait(a, g, 1 + b // 2)
                m_hi_done.by(a.activation(m_hi[:, b % 2], mt[:, b % 2], ACT.Copy))
                summed.wait(a, g, b)
                m_squared.by(a.activation(sq[:], mt[:, b % 2], ACT.Square))

            def root(g, b):
                summed.wait(a, g, b + 1)
                b_added.wait(a, g, b - 1)
                roots.by(a.activation(rab[:, b % 2], sums[:, 0:4:2], ACT.Sqrt, bias=epsc[:, 0:1], scale=1.0 / D_RNN))

            for k in range(KD):
                if k % RC == 0:
                    a.wait_ge(w_half_in[k // RC].sem, 16 * (5, 4)[k // RC])
                o_hi_done.by(a.activation(o_hi[:, k], wst[:, k], ACT.Copy, scale=og[:, k:k + 1]))
            a.wait_ge(const_ready.sem, CONST_STEPS)
            split(0, 0)
            root(0, 0)

            def exps(g, b):
                group_max.wait(a, g, b + 1)
                group_exp.by(a.activation(pg[:], lg[:, 0:GROUPS], ACT.Exp, bias=ngm[:, 0:1], accum_out=gsum[:, 0:1]))
                expert_max.wait(a, g, b + 1)
                expert_exp.by(a.activation(ex[:], e8[:, 1:2], ACT.Exp, bias=nl[:, 0:1]))

            def tile(g, b):
                first = isinstance(g, int) and b == 0
                b_done.wait(a, g, b)
                split(g, b + 1)
                root(g, b + 1)
                b_added.wait(a, g, b + 1)
                u_ready.wait(a, g, b)
                h_squared.by(a.activation(hsq[:], ht[:, b], ACT.Square, accum_out=rh[:, 0:1]))
                h_squared.wait(a, g, b + 1)
                h_root.by(a.activation(rh[:, 1:2], rh[:, 0:1], ACT.Sqrt, bias=epsc[:, 0:1], scale=1.0 / D))
                if not first:
                    exps(g, b - 1)
                u_turned.wait(a, g, b + 1)
                uT_done.by(a.activation(uT[:], tps[:], ACT.Copy))

            for b in range(2):
                tile(0, b)
            with a.Fori(1, NT // 2) as g:
                for b in range(2):
                    tile(g, b)
            exps(NT // 2 - 1, 1)

        @block.vector
        def _(v):
            def chained(ins):
                step.step(ins)
                step.wait(v)

            def lower(g, b):
                m_hi_done.wait(v, g, b + 1)
                m_lo_done.by(v.tensor_tensor(m_lo[:, b % 2], mt[:, b % 2], m_hi[:, b % 2].bitcast(F32),
                                             ALU.subtract))

            def add_a(g, b):
                a_done.wait(v, g, b + 1)
                h_stored[b % 2].wait(v, g, b // 2)
                a_added.by(v.scalar_tensor_tensor(out=ht[:, b % 2], in0=pa[:].rearrange("p a n -> p (a n)"),
                                                  scalar=rab[:, b % 2, 0:1], in1=xt[:, b % 2], op0=ALU.mult, op1=ALU.add))

            def choose(g, b):
                routed.wait(v, g, b + 1)
                chained(v.tensor_copy(lg[:, 0:GROUPS], rt[:, LOGIT:LOGIT + GROUPS]))
                v.sem_inc(settled.sem, 1)
                chained(v.max(g8[:], lg[:]))
                v.sem_inc(settled.sem, 1)
                step.step(v.max_index(gi[:], g8[:], lg[:]))
                group_max.by(v.tensor_scalar(ngm[:], g8[:, 0:1], -1.0, None, ALU.mult))
                step.wait(v)
                chained(v.tensor_copy(gif[:], gi[:, 0:1]))
                chained(v.tensor_scalar(pen[:], iota_e[:, 0:GROUPS], gif[:, 0:1], -NEG, ALU.is_equal, ALU.mult))
                chained(v.scalar_tensor_tensor(out=em[:].rearrange("p (g e) -> p g e", e=EPG),
                                               in0=pen[:].unsqueeze(2).to_broadcast([P, GROUPS, EPG]), scalar=NEG,
                                               in1=rt[:, LOGIT + GROUPS:LOGIT + R].rearrange("p (g e) -> p g e", e=EPG),
                                               op0=ALU.add, op1=ALU.add))
                v.sem_inc(settled.sem, 1)
                chained(v.max(e8[:], em[:]))
                v.sem_inc(settled.sem, 1)
                step.step(v.max_index(ei[:], e8[:], em[:]))
                expert_max.by(v.tensor_scalar(nl[:], e8[:, 0:1], -1.0, None, ALU.mult))
                step.wait(v)
                chained(v.tensor_copy(slot[:, 0:TOP], ei[:, 0:TOP]))
                step.step(v.tensor_scalar(hot[:, 0], iota_e[:], slot[:, 0:1], None, ALU.is_equal))
                chained(v.tensor_scalar(hot[:, 1], iota_e[:], slot[:, 1:2], None, ALU.is_equal))
                chosen_done.by(v.tensor_tensor(chosen[:], hot[:, 0], hot[:, 1], ALU.add))

            def place(g, b):
                group_exp.wait(v, g, b + 1)
                expert_exp.wait(v, g, b + 1)
                chained(v.tensor_scalar(slot[:, 4:5], ex[:], 1.0, gsum[:, 0:1], ALU.add, ALU.mult))
                chained(v.reciprocal(slot[:, 4:5], slot[:, 4:5]))
                step.step(v.tensor_tensor(slot[:, 5:6], slot[:, 4:5], ex[:], ALU.mult))
                ranked.wait(v, g, b + 1)
                at_free.wait(v, g, b - 1)
                step.step(v.tensor_tensor(sel[:], hot[:], rt[:, RANK:RANK + E].unsqueeze(1)
                                          .to_broadcast([P, TOP, E]), ALU.mult))
                chained(v.tensor_tensor(seen[:], seen[:], chosen[:], ALU.add))
                chained(v.tensor_reduce(slot[:, 2:4], sel[:], AX.X, ALU.add))
                par = b % 2
                chained(v.tensor_copy(slots[:, bass.ds(g * 2 + b, 1)].rearrange("p one n -> p (one n)"), slot[:])
                        if not isinstance(g, int) else v.tensor_copy(slots[:, 2 * g + b], slot[:]))
                chained(v.tensor_copy(toki[par][:], tokf[:, par:par + 1]))
                step.step(v.tensor_scalar(tokf[:, par:par + 1], tokf[:, par:par + 1], 2.0 * P, None, ALU.add))
                slots_done.by(v.scalar_tensor_tensor(out=at[par][:], in0=slot[:, 0:2], scalar=float(LIST),
                                                     in1=slot[:, 2:4], op0=ALU.mult, op1=ALU.add))

            for k in range(KD):
                o_hi_done.wait(v, 0, k + 1)
                o_lo_done.by(v.scalar_tensor_tensor(out=o_lo[:, k], in0=wst[:, k], scalar=og[:, k:k + 1],
                                                    in1=o_hi[:, k].bitcast(F32), op0=ALU.mult, op1=ALU.subtract))
            v.wait_ge(const_ready.sem, CONST_STEPS)
            chained(v.tensor_copy(iota_e[:], iota_i[:]))
            chained(v.tensor_copy(tokf[:], tok0[:]))
            lower(0, 0)
            roots.wait(v, 0, 1)
            chained(v.reciprocal(rab[:, 0], rab[:, 0]))
            add_a(0, 0)
            v.wait_ge(consts_in.sem, 16 * NCONST)

            def tile(g, b):
                first = isinstance(g, int) and b == 0
                lower(g, b + 1)
                roots.wait(v, g, b + 2)
                chained(v.reciprocal(rab[:, 1 - b], rab[:, 1 - b]))
                if not first:
                    choose(g, b - 1)
                b_done.wait(v, g, b + 1)
                a_added.wait(v, g, b + 1)
                b_added.by(v.scalar_tensor_tensor(out=ht[:, b], in0=pb[:].rearrange("p a n -> p (a n)"),
                                                  scalar=rab[:, b, 1:2], in1=ht[:, b], op0=ALU.mult, op1=ALU.add))
                h_root.wait(v, g, b + 1)
                chained(v.reciprocal(rh[:, 1:2], rh[:, 1:2]))
                u_stored[b].wait(v, g, 0)
                u_ready.by(v.scalar_tensor_tensor(out=ut[:, b], in0=ht[:, b], scalar=rh[:, 1:2], in1=g2[:],
                                                  op0=ALU.mult, op1=ALU.mult))
                add_a(g, b + 1)
                if not first:
                    place(g, b - 1)

            step.enter(0)
            for b in range(2):
                tile(0, b)
            step.before, step.n = step.before + step.n, 0
            with v.Fori(1, NT // 2) as g:
                step.g = g - 1
                for b in range(2):
                    tile(g, b)
                step.leave()
            step.g, step.before, step.n = None, step.before + (NT // 2 - 1) * step.per, 0
            choose(NT // 2 - 1, 1)
            place(NT // 2 - 1, 1)
            step.wait(v)
            ranks_end.by(v.tensor_copy(seen_out[:], seen[:]))


def plan_blocks(nc, seen, slots, plan_dram, plan, dest):
    with ExitStack() as ctx:
        def sb(name, shape, dt=F32):
            return ctx.enter_context(nc.sbuf_tensor(name, shape, dt))

        ones = sb("ones_p", [P, P], BF16)
        zero = sb("zero_p", [P, E])
        cnt_i, nb_i = sb("cnt_i", [P, E], I32), sb("nb_i", [P, E], I32)
        nb, end, start = sb("nb", [P, E]), sb("end", [P, E]), sb("start", [P, E])
        ie, io = sb("ie", [P, E], I32), sb("io", [P, E])
        ib, block_no = sb("ib", [P, 1], I32), sb("block_no", [P, 1])
        ends, past, hot, tmp = (sb(n, [P, E]) for n in ("ends", "past", "hot_p", "tmp"))
        col = sb("col", [P, 8])
        f = sb("f", [P, 8])
        need_i = sb("need_i", [P, 2], I32)
        fi, one_i = sb("fi", [P, 2], I32), sb("one_i", [P, 2], I32)
        tab = sb("tab", [P, 8], I32)
        big = sb("big_p", [P, NT * TOP, E])
        row = sb("row", [P, NT * TOP])
        count = ctx.enter_context(nc.psum_tensor("count", [P, E], F32))
        const_ready, counted, planned = (Signal(ctx, nc, n, 0) for n in ("const_ready3", "counted", "planned"))
        out, back = Signal(ctx, nc, "plan_out", 0), Signal(ctx, nc, "plan_back", 0)
        step = Chain(ctx, nc, "dve_step3")
        block = ctx.enter_context(nc.Block())

        @block.gpsimd
        def _(pool):
            made = 0
            for make in (lambda: pool.memset(ones[:], 1.0), lambda: pool.memset(zero[:], 0.0),
                         lambda: pool.iota(ie[:], pattern=[[1, E]], base=0, channel_multiplier=0),
                         lambda: pool.iota(ib[:], pattern=[[1, 1]], base=0, channel_multiplier=1),
                         lambda: pool.memset(one_i[:], 1), lambda: pool.memset(col[:], 0.0)):
                make().then_inc(const_ready.sem, 1)
                made += 1
                pool.wait_ge(const_ready.sem, made)

        @block.tensor
        def _(pe):
            pe.wait_ge(const_ready.sem, 6)
            pe.matmul(count[:], ones[:], seen[:], start=True, stop=True).then_inc(counted.sem, 1)

        @block.vector
        def _(v):
            def chained(ins):
                step.step(ins)
                step.wait(v)

            def total(dst, src):
                chained(v.tensor_reduce(dst, src, AX.X, ALU.add))

            v.wait_ge(const_ready.sem, 6)
            step.step(v.tensor_copy(io[:], ie[:]))
            step.step(v.tensor_copy(block_no[:], ib[:]))
            v.wait_ge(counted.sem, 1)
            chained(v.tensor_scalar(cnt_i[:], count[:], float(P - 1), None, ALU.add))
            chained(v.tensor_scalar(nb_i[:], cnt_i[:], 7, None, ALU.arith_shift_right))
            chained(v.tensor_copy(nb[:], nb_i[:]))
            chained(v.tensor_tensor_scan(end[:], nb[:], zero[:], 0.0, ALU.add, ALU.add))
            chained(v.tensor_tensor(start[:], end[:], nb[:], ALU.subtract))
            chained(v.tensor_scalar(ends[:], end[:], block_no[:, 0:1], None, ALU.is_le))
            total(f[:, 0:1], ends[:])
            chained(v.tensor_scalar(col[:, 0:1], f[:, 0:1], float(E - 1), None, ALU.min))
            chained(v.tensor_scalar(hot[:], io[:], col[:, 0:1], None, ALU.is_equal))
            chained(v.tensor_tensor(tmp[:], hot[:], start[:], ALU.mult))
            total(f[:, 1:2], tmp[:])
            chained(v.tensor_tensor(tmp[:], hot[:], end[:], ALU.mult))
            total(f[:, 2:3], tmp[:])
            chained(v.tensor_scalar(past[:], end[:], f[:, 2:3], None, ALU.is_le))
            total(f[:, 3:4], past[:])
            chained(v.tensor_scalar(col[:, 1:2], f[:, 3:4], float(E - 1), None, ALU.min))
            chained(v.tensor_tensor(f[:, 4:5], block_no[:], f[:, 1:2], ALU.is_equal))
            chained(v.tensor_tensor(f[:, 5:6], block_no[:], end[:, E - 1:E], ALU.is_lt))
            chained(v.tensor_tensor(f[:, 4:5], f[:, 4:5], f[:, 5:6], ALU.mult))
            chained(v.tensor_scalar(f[:, 5:6], f[:, 3:4], float(E), None, ALU.is_lt))
            chained(v.tensor_tensor(col[:, 2:3], f[:, 4:5], f[:, 5:6], ALU.mult))
            chained(v.tensor_tensor(f[:, 6:7], block_no[:], f[:, 1:2], ALU.subtract))
            chained(v.tensor_scalar(f[:, 6:7], f[:, 6:7], float(T // P), float(P), ALU.min, ALU.mult))
            chained(v.scalar_tensor_tensor(out=col[:, 3:4], in0=col[:, 0:1], scalar=float(LIST), in1=f[:, 6:7],
                                           op0=ALU.mult, op1=ALU.add))
            chained(v.tensor_scalar(tmp[:], nb[:], 0.0, None, ALU.is_gt))
            chained(v.tensor_tensor(tmp[:], tmp[:], ends[:], ALU.mult))
            total(f[:, 7:8], tmp[:])
            chained(v.tensor_copy(fi[:, 0:1], f[:, 7:8]))
            chained(v.tensor_tensor(fi[:, 1:2], fi[:, 0:1], one_i[:, 0:1], ALU.bitwise_and))
            chained(v.tensor_copy(col[:, 4:5], fi[:, 1:2]))
            chained(v.tensor_scalar(past[:], start[:], 1.0, None, ALU.add))
            chained(v.tensor_tensor(tmp[:], tmp[:], past[:], ALU.mult))
            chained(v.tensor_tensor(past[:], end[:], f[:, 1:2].to_broadcast([P, E]), ALU.is_le))
            chained(v.tensor_tensor(tmp[:], tmp[:], past[:], ALU.mult))
            chained(v.tensor_reduce(f[:, 0:1], tmp[:], AX.X, ALU.max))
            chained(v.tensor_scalar(f[:, 1:2], f[:, 0:1], 1.0, None, ALU.add))
            chained(v.tensor_copy(need_i[:], f[:, 0:2]))
            chained(v.tensor_scalar(need_i[:], need_i[:], 1, None, ALU.arith_shift_right))
            chained(v.tensor_copy(f[:, 0:2], need_i[:]))
            chained(v.tensor_scalar(col[:, 5:6], f[:, 1:2], 48.0, 48.0, ALU.mult, ALU.add))
            chained(v.tensor_scalar(col[:, 6:7], f[:, 0:1], 48.0, 48.0, ALU.mult, ALU.add))
            planned.by(v.tensor_copy(tab[:], col[:]))
            sl = slots[:].rearrange("p t (s k) -> p t s k", k=TOP)
            chained(v.tensor_copy(row[:].rearrange("p (t k) -> p t k", k=TOP), sl[:, :, 0]))
            chained(v.tensor_tensor(big[:], row[:].unsqueeze(2).to_broadcast([P, NT * TOP, E]),
                                    io[:].unsqueeze(1).to_broadcast([P, NT * TOP, E]), ALU.is_equal))
            chained(v.tensor_tensor(big[:], big[:], start[:].unsqueeze(1).to_broadcast([P, NT * TOP, E]), ALU.mult))
            chained(v.tensor_reduce(row[:], big[:], AX.X, ALU.add))
            chained(v.scalar_tensor_tensor(out=dest[:], in0=row[:].rearrange("p (t k) -> p t k", k=TOP),
                                           scalar=float(P), in1=sl[:, :, 1], op0=ALU.mult, op1=ALU.add))

        @block.sync
        def _(sp):
            sp.wait_ge(planned.sem, 1)
            sp.dma_start(plan_dram, tab[:]).then_inc(out.sem, 16)
            sp.wait_ge(out.sem, 16)
            sp.dma_start(plan[0:1, :], plan_dram.rearrange("(a b) c -> a (b c)", a=1)).then_inc(back.sem, 16)
            sp.wait_ge(back.sem, 16)


def run_experts(nc, plan, lists, u_rows, w_gate, w_up, w_down, y_rows):
    with ExitStack() as ctx:
        def sb(name, shape, dt=F32):
            return ctx.enter_context(nc.sbuf_tensor(name, shape, dt))

        def ps(name, shape):
            return ctx.enter_context(nc.psum_tensor(name, shape, F32))

        U = 4
        NI = NBLK // U

        def sig(name, per=U, base=0, step=1):
            return Signal(ctx, nc, name, per, base, step)

        wgu = sb("wgu", [P, 2, KD, 2 * F])
        wdn = sb("wdn", [P, 2, FC, D])
        idx = [sb(f"idx{b}", [P, 1], I32) for b in range(U)]
        xg = [sb(f"xg{b}", [P, D]) for b in range(U)]
        xT = sb("xT", [P, 2, KD, P])
        act_g, hid = sb("act_g", [P, F]), sb("hid", [P, F])
        hT = sb("hT", [P, FC, P])
        ys = sb("ys", [P, U, D])
        idn = sb("idn_m", [P, P])
        tps = ps("tps_m", [P, KD, P])
        gu = [ps(f"gu{b}", [P, 2 * F]) for b in range(2)]
        hp = ps("hp", [P, FC, P])
        yp = [ps(f"yp{n}", [P, D // 2]) for n in range(2)]

        const_ready = sig("const_ready4", 0)
        w_first = sig("w_first", 0)
        w_in = [sig(f"w_in{b}", U // 2, 2 - b, 48) for b in range(2)]
        idx_in = [sig(f"idx_in{b}", 1, 1, 16) for b in range(U)]
        gathered = [sig(f"gathered{b}", 1, 1, 16) for b in range(U)]
        turned, xT_done = sig("turned", U, 1), sig("xT_done", U, 1)
        gated, silu_done, hid_done = sig("gated_m", U, 1), sig("silu_done"), sig("hid_done")
        h_turned, hT_done, down_done = sig("h_turned"), sig("hT_done"), sig("down_done", 2 * U)
        y_taken = [sig(f"y_taken{n}", U, 1) for n in range(2)]
        y_stored = [sig(f"y_stored{b}", 1, 1, 16) for b in range(U)]
        begun, pool_begun = sig("begun_m", 0), sig("pool_begun_m", 0)
        block = ctx.enter_context(nc.Block())
        plan_rows = plan[0:1, :].rearrange("a (b c) -> a b c", c=8)
        y_blocks = y_rows.rearrange("(b p) n -> b p n", p=P)
        wg_rows, wu_rows = (w[0].rearrange("e (k p) n -> e p k n", p=P) for w in (w_gate, w_up))
        wd_rows = w_down[0].rearrange("e (c p) n -> e p c n", p=P)

        def planned(eng, blk, c, top, low=0):
            at = bass.ds(blk, 1) if not isinstance(blk, int) else slice(blk, blk + 1)
            return eng.value_load(plan_rows[:, at, c], min_val=low, max_val=top)

        @block.sync
        def _(sp):
            def load_index(blk, b):
                row = planned(sp, blk, 3, E * LIST - P)
                idx_in[b].by(sp.dma_start(idx[b][:], lists[bass.ds(row, P), :]))

            def load_weights(g, b):
                nxt, load, buf = (planned(sp, g * U + b, c, top) for c, top in ((1, E - 1), (2, 1), (4, 1)))
                other = sp.snap(1 - buf, min_val=0, max_val=1)
                w_in[b % 2].wait(sp, g, (b - 1) // 2)
                sp.sem_inc(begun.sem, 1)
                for dst, src in ((wgu[:, bass.ds(other, 1), :, 0:F], wg_rows),
                                 (wgu[:, bass.ds(other, 1), :, F:], wu_rows),
                                 (wdn[:, bass.ds(other, 1)], wd_rows)):
                    sp.dma_start(dst.rearrange("p one k n -> p (one k) n"), src[nxt],
                                 cond=load).then_inc(w_in[b % 2].sem, 16)

            sp.sem_inc(w_in[0].sem, 48)
            sp.sem_inc(w_in[1].sem, 48)
            for b in range(2):
                load_index(b, b)
            e0 = planned(sp, 0, 0, E - 1)
            for dst, src in ((wgu[:, 0, :, 0:F], wg_rows), (wgu[:, 0, :, F:], wu_rows), (wdn[:, 0], wd_rows)):
                sp.dma_start(dst, src[e0]).then_inc(w_first.sem, 16)
            for b in range(2, U):
                load_index(b, b)
            load_weights(0, 0)
            for b in range(U):
                sp.sem_inc(y_stored[b].sem, 16)
            with sp.Fori(0, NI) as g:
                for b in range(U):
                    gathered[b].wait(sp, g, 0)
                    sp.sem_inc(begun.sem, 1)
                    load_index(g * U + (b + U), b)
                    down_done.wait(sp, g, 2 * b + 2)
                    sp.sem_inc(begun.sem, 1)
                    load_weights(g, b + 1)
                    for n in range(2):
                        y_taken[n].wait(sp, g, b + 1)
                    sp.sem_inc(begun.sem, 1)
                    y_stored[b].by(sp.dma_start(y_blocks[g * U + b], ys[:, b]))
            for b in range(U):
                sp.wait_ge(y_stored[b].sem, 16 * (NI + 1))
                sp.wait_ge(idx_in[b].sem, 16 * (NI + 1))
            sp.wait_ge(w_in[0].sem, 48 * (NBLK // 2 + 2))
            sp.wait_ge(w_in[1].sem, 48 * (NBLK // 2 + 1))

        @block.gpsimd
        def _(pool):
            pool.memset(idn[:], 0.0).then_inc(const_ready.sem, 1)
            pool.wait_ge(const_ready.sem, 1)
            pool.affine_select(out=idn[:], in_=idn[:], compare_op=ALU.not_equal, fill=1.0, base=0,
                               pattern=[[-1, P]], channel_multiplier=1).then_inc(const_ready.sem, 1)

            def gather(b):
                pool.sem_inc(pool_begun.sem, 1)
                gathered[b].by(pool.indirect_dma_start(xg[b][:], None, u_rows,
                                                       bass.IndirectOffsetOnAxis(ap=idx[b][:, 0:1], axis=0)))

            for b in range(U):
                idx_in[b].wait(pool, -1, 1)
                gather(b)
            with pool.Fori(0, NI) as g:
                for b in range(U):
                    idx_in[b].wait(pool, g, 1)
                    turned.wait(pool, g, b)
                    gather(b)
            for b in range(U):
                pool.wait_ge(gathered[b].sem, 16 * (NI + 1))

        @block.tensor
        def _(pe):
            def turn(g, b):
                gathered[b % U].wait(pe, g, b // U)
                xT_done.wait(pe, g, b - 1)
                for k in range(KD):
                    ins = pe.transpose(tps[:, k], xg[b % U][:, k * P:(k + 1) * P], idn[:])
                turned.by(ins)

            def gate_up(g, b, buf, k0):
                for k in range(k0, k0 + KD // 2):
                    ins = pe.matmul(gu[b % 2][:], xT[:, b % 2, k],
                                    wgu[:, bass.ds(buf, 1), k].rearrange("p one n -> p (one n)"),
                                    start=(k == 0), stop=(k == KD - 1))
                return ins

            pe.wait_ge(const_ready.sem, 2)
            turn(0, 0)
            pe.wait_ge(w_first.sem, 48)
            xT_done.wait(pe, 0, 0)
            gate_up(0, 0, 0, 0)
            gated.by(gate_up(0, 0, 0, KD // 2))
            with pe.Fori(0, NI) as g:
                for b in range(U):
                    if b == 0:
                        buf = planned(pe, g * U, 4, 1)
                    nbuf, even, odd = (planned(pe, g * U + (b + 1), c, top, low) for c, top, low in
                                       ((4, 1, 0), (5, 24 * NBLK + 96, 48), (6, 24 * NBLK + 96, 48)))
                    turn(g, b + 1)
                    pe.wait_ge(w_in[0].sem, even)
                    pe.wait_ge(w_in[1].sem, odd)
                    xT_done.wait(pe, g, b + 1)
                    gate_up(g, b + 1, nbuf, 0)
                    hid_done.wait(pe, g, b + 1)
                    for c in range(FC):
                        ins = pe.transpose(hp[:, c], hid[:, c * P:(c + 1) * P], idn[:])
                    h_turned.by(ins)
                    gated.by(gate_up(g, b + 1, nbuf, KD // 2))
                    hT_done.wait(pe, g, b + 1)
                    for n in range(2):
                        y_taken[n].wait(pe, g, b)
                        for c in range(FC):
                            ins = pe.matmul(yp[n][:], hT[:, c],
                                            wdn[:, bass.ds(buf, 1), c, n * (D // 2):(n + 1) * (D // 2)]
                                            .rearrange("p one n -> p (one n)"), start=(c == 0), stop=(c == FC - 1))
                        down_done.by(ins)
                    buf = nbuf

        @block.scalar
        def _(a):
            def take_x(g, b):
                turned.wait(a, g, b)
                xT_done.by(a.activation(xT[:, b % 2], tps[:], ACT.Copy))

            take_x(0, 0)
            a.sem_inc(y_taken[0].sem, 1)
            with a.Fori(0, NI) as g:
                for b in range(U):
                    gated.wait(a, g, b)
                    silu_done.by(a.activation(act_g[:], gu[b % 2][:, 0:F], ACT.Silu))
                    take_x(g, b + 1)
                    h_turned.wait(a, g, b + 1)
                    hT_done.by(a.activation(hT[:], hp[:], ACT.Copy))
                    down_done.wait(a, g, 2 * b + 1)
                    y_stored[b].wait(a, g, 0)
                    y_taken[0].by(a.activation(ys[:, b, 0:D // 2], yp[0][:], ACT.Copy))

        @block.vector
        def _(v):
            v.sem_inc(y_taken[1].sem, 1)
            with v.Fori(0, NI) as g:
                for b in range(U):
                    silu_done.wait(v, g, b + 1)
                    hid_done.by(v.tensor_tensor(hid[:], act_g[:], gu[b % 2][:, F:], ALU.mult))
                    down_done.wait(v, g, 2 * b + 2)
                    y_stored[b].wait(v, g, 0)
                    y_taken[1].by(v.tensor_copy(ys[:, b, D // 2:], yp[1][:]))


def combine(nc, h_rows, y_rows, slots, dest, final_g, out):
    with ExitStack() as ctx:
        def sb(name, shape, dt=F32):
            return ctx.enter_context(nc.sbuf_tensor(name, shape, dt))

        def sig(name, per=2, base=0, step=1):
            return Signal(ctx, nc, name, per, base, step)

        NBUF = 4
        fg, eps = sb("fg", [P, D]), sb("eps_f", [P, 1])
        ht = [sb(f"hf{b}", [P, D]) for b in range(NBUF)]
        y = [[sb(f"y{k}_{b}", [P, D]) for k in range(TOP)] for b in range(NBUF)]
        at = [sb(f"at_f{b}", [P, TOP], U32) for b in range(NBUF)]
        sq = [sb(f"sq_f{b}", [P, D]) for b in range(2)]
        wt = sb("wt_f", [P, NBUF, TOP])
        r = sb("r_f", [P, NBUF])
        consts_in, const_ready = sig("consts_in5", 0), sig("const_ready5", 0)
        h_in = [sig(f"hf_in{b}", 1, 0, 16) for b in range(NBUF)]
        y_in = [sig(f"yf_in{b}", 1, 0, 32) for b in range(NBUF)]
        index_done = [sig(f"index_done{b}", 1, 0, 1) for b in range(NBUF)]
        squared, rooted = sig("squared_f", NBUF), sig("rooted_f", NBUF)
        summed, scaled = sig("summed_f", NBUF), sig("scaled_f", NBUF, NBUF)
        stored = [sig(f"stored_f{b}", 1, 1, 16) for b in range(NBUF)]
        begun, pool_begun = sig("begun_f", 0), sig("pool_begun_f", 0)
        STEPS = 3
        step = Chain(ctx, nc, "dve_step5", NBUF * STEPS)
        block = ctx.enter_context(nc.Block())
        h_tiles, out_tiles = (t.rearrange("(t p) n -> t p n", p=P) for t in (h_rows, out))
        NI = NT // NBUF

        @block.sync
        def _(sp):
            sp.dma_start(fg[:], final_g.partition_broadcast(P)).then_inc(consts_in.sem, 16)
            for b in range(NBUF):
                sp.sem_inc(stored[b].sem, 16)
            with sp.Fori(0, NI) as g:
                for b in range(NBUF):
                    stored[b].wait(sp, g, 0)
                    sp.sem_inc(begun.sem, 1)
                    h_in[b].by(sp.dma_start(ht[b][:], h_tiles[g * NBUF + b]))
            for b in range(NBUF):
                sp.wait_ge(stored[b].sem, 16 * (NI + 1))

        @block.gpsimd
        def _(pool):
            pool.memset(eps[:], EPS).then_inc(const_ready.sem, 1)
            with pool.Fori(0, NI) as g:
                for b in range(NBUF):
                    scaled.wait(pool, g, b + 1 - NBUF)
                    index_done[b].by(pool.tensor_copy(at[b][:], dest[:, bass.ds(g * NBUF + b, 1)]
                                                      .rearrange("p one k -> p (one k)")))
                    index_done[b].wait(pool, g, 1)
                    pool.sem_inc(pool_begun.sem, 1)
                    for k in range(TOP):
                        pool.indirect_dma_start(y[b][k][:], None, y_rows,
                                                bass.IndirectOffsetOnAxis(ap=at[b][:, k:k + 1], axis=0)
                                                ).then_inc(y_in[b].sem, 16)

        @block.scalar
        def _(a):
            a.wait_ge(const_ready.sem, 1)
            with a.Fori(0, NI) as g:
                for b in range(NBUF):
                    summed.wait(a, g, b + 1)
                    squared.by(a.activation(sq[b % 2][:], ht[b][:], ACT.Square, accum_out=r[:, b:b + 1]))
                    squared.wait(a, g, b + 1)
                    rooted.by(a.activation(r[:, b:b + 1], r[:, b:b + 1], ACT.Sqrt, bias=eps[:, 0:1], scale=1.0 / D))
                    if b > 0:
                        scaled.wait(a, g, b)
                        stored[b - 1].by(a.dma_start(out_tiles[g * NBUF + (b - 1)], ht[b - 1][:]))
                scaled.wait(a, g, NBUF)
                stored[NBUF - 1].by(a.dma_start(out_tiles[g * NBUF + (NBUF - 1)], ht[NBUF - 1][:]))

        @block.vector
        def _(v):
            def chained(ins):
                step.step(ins)
                step.wait(v)

            v.wait_ge(consts_in.sem, 16)
            v.sem_inc(scaled.sem, NBUF)
            with v.Fori(0, NI) as g:
                step.enter(g)

                def add(b):
                    h_in[b].wait(v, g, 1)
                    y_in[b].wait(v, g, 1)
                    chained(v.tensor_copy(wt[:, b], slots[:, bass.ds(g * NBUF + b, 1), 4:6]
                                          .rearrange("p one k -> p (one k)")))
                    chained(v.scalar_tensor_tensor(out=ht[b][:], in0=y[b][0][:], scalar=wt[:, b, 0:1],
                                                   in1=ht[b][:], op0=ALU.mult, op1=ALU.add))
                    summed.by(v.scalar_tensor_tensor(out=ht[b][:], in0=y[b][1][:], scalar=wt[:, b, 1:2],
                                                     in1=ht[b][:], op0=ALU.mult, op1=ALU.add))

                def scale(b):
                    rooted.wait(v, g, b + 1)
                    chained(v.reciprocal(r[:, b:b + 1], r[:, b:b + 1]))
                    scaled.by(v.scalar_tensor_tensor(out=ht[b][:], in0=ht[b][:], scalar=r[:, b:b + 1], in1=fg[:],
                                                     op0=ALU.mult, op1=ALU.mult))

                for b in range(NBUF):
                    add(b)
                    if b > 0:
                        scale(b - 1)
                scale(NBUF - 1)
                step.leave()


def build(nc, x, out, norm1_g, w_in, conv_w, conv_b, w_rg, b_rg, w_ig, b_ig, lru_lambda, attn_sinks,
          rnn_out_g, attn_out_g, w_out, norm2_g, w_group_router, w_expert_router, w_gate, w_up, w_down, final_g):
    def dram(name, shape, dt=F32):
        return nc.dram_tensor(name, shape, dt).ap()

    mixT = dram("mixT", (2 * RC, P, T))
    h_rows, u_rows = dram("h_rows", (T, D)), dram("u_rows", (T, D))
    lists = dram("lists", (E * LIST, 1), I32)
    plan_dram = dram("plan_dram", (P, 8), I32)
    y_rows = dram("y_rows", (NBLK * P, D))
    xr, outr = x[0], out[0]
    project_and_mix(nc, xr, norm1_g, w_in, conv_w, conv_b, w_rg, b_rg, w_ig, b_ig, lru_lambda, attn_sinks, mixT)
    with (nc.sbuf_tensor("slots", [P, NT, 3 * TOP], F32) as slots,
          nc.sbuf_tensor("dest", [P, NT, TOP], U32) as dest):
        with (nc.sbuf_tensor("seen_out", [P, E], BF16) as seen,
              nc.sbuf_tensor("plan", [1, P * 8], I32) as plan):
            project_out(nc, xr, mixT, rnn_out_g, attn_out_g, w_out, norm2_g, w_group_router, w_expert_router,
                        h_rows, u_rows, lists, slots, seen)
            plan_blocks(nc, seen, slots, plan_dram, plan, dest)
            run_experts(nc, plan, lists, u_rows, w_gate, w_up, w_down, y_rows)
        combine(nc, h_rows, y_rows, slots, dest, final_g, outr)


_INS = ['x', 'norm1_g', 'w_in', 'conv_w', 'conv_b', 'w_rg', 'b_rg', 'w_ig', 'b_ig', 'lru_lambda', 'attn_sinks',
        'rnn_out_g', 'attn_out_g', 'w_out', 'norm2_g', 'w_group_router', 'w_expert_router', 'w_gate', 'w_up',
        'w_down', 'final_g']


def kernel(**inputs):
    import concourse.bacc as _bacc
    from concourse.bass_utils import run_bass_kernel_spmd as _run

    nc = _bacc.Bacc("TRN2", target_bir_lowering=False, num_devices=1)
    arrays, aps = {}, {}
    for name in _INS:
        a = np.ascontiguousarray(inputs[name])
        arrays[f"in_{name}"] = a
        aps[name] = nc.dram_tensor(f"in_{name}", a.shape, mybir.dt.from_np(a.dtype), kind="ExternalInput").ap()
    x = aps.pop("x")
    out = nc.dram_tensor("out_dram", (1, T, D), F32, kind="ExternalOutput").ap()
    build(nc, x, out, **aps)
    r = _run(nc, [arrays], core_ids=[0])
    return r.results[0]["out_dram"]
```

```python
from contextlib import ExitStack

import numpy as np

import concourse.bass as bass
from concourse import mybir

ALU = mybir.AluOpType
ACT = mybir.ActivationFunctionType
AX = mybir.AxisListType
F32 = mybir.dt.float32
F32R = mybir.dt.float32r
BF16 = mybir.dt.bfloat16
I32 = mybir.dt.int32
U32 = mybir.dt.uint32

P = 128
D = 1024
KD = D // P
T = 4096
EPS = 1e-6
D_RNN = 512
RC = D_RNN // P
CONV = 4
LRU_C = 8.0
CHUNK = 64
HEADS, KV, HD = 8, 2, 64
G = HEADS // KV
D_ATTN = HEADS * HD
D_IN = 2 * D_RNN + D_ATTN + 2 * KV * HD
Q0, K0, V0 = 2 * D_RNN, 2 * D_RNN + D_ATTN, 2 * D_RNN + D_ATTN + KV * HD
GROUPS, EPG = 4, 8
E = GROUPS * EPG
TOP = 2
F = 256
FC = F // P
NEG = -1e30

TOK = 256
NG = T // TOK
TJ = TOK // P
NT = T // P
LIST = T + P
NB = T * TOP // P + E - 1
U_SHIFT = 2
U_BLK = 1 << U_SHIFT
NBLK = -(-NB // U_BLK) * U_BLK
GELU_K, GELU_C = (2 / np.pi) ** 0.5, 0.044715


class Signal:

    def __init__(self, ctx, nc, name, per, base=0, step=1):
        self.sem, self.per, self.base, self.step = ctx.enter_context(nc.semaphore(name)), per, base, step

    def wait(self, eng, g, n):
        value = (g * self.per + (self.base + n)) * self.step
        if not isinstance(value, int) or value > 0:
            eng.wait_ge(self.sem, value)

    def by(self, ins):
        ins.then_inc(self.sem, self.step)


class Chain:

    def __init__(self, ctx, nc, name, per=0):
        self.sem, self.per, self.before, self.n, self.g = ctx.enter_context(nc.semaphore(name)), per, 0, 0, None

    def step(self, ins):
        ins.then_inc(self.sem, 1)
        self.n += 1

    def enter(self, g):
        self.before, self.n, self.g = self.before + self.n, 0, g

    def leave(self):
        assert self.n == self.per, (self.n, self.per)

    def wait(self, eng):
        if self.g is None:
            eng.wait_ge(self.sem, self.before + self.n)
        else:
            eng.wait_ge(self.sem, self.g * self.per + (self.before + self.n))


def product3(pe, out, w_hi, w_lo, x_hi, x_lo, first, last):
    pe.matmul(out, w_lo, x_hi, start=first, stop=False)
    pe.matmul(out, w_hi, x_lo, start=False, stop=False)
    return pe.matmul(out, w_hi, x_hi, start=False, stop=last)


def project_and_mix(nc, x, norm1_g, w_in, conv_w, conv_b, w_rg, b_rg, w_ig, b_ig, lru_lambda, attn_sinks, mixT):
    with ExitStack() as ctx:
        def sb(name, shape, dt=F32):
            return ctx.enter_context(nc.sbuf_tensor(name, shape, dt))

        def ps(name, shape):
            return ctx.enter_context(nc.psum_tensor(name, shape, F32))

        def sig(name, per, base=0, step=1):
            return Signal(ctx, nc, name, per, base, step)

        w_hi, w_lo = sb("w_hi", [P, KD, D_IN], F32R), sb("w_lo", [P, KD, D_IN], F32R)
        u_hi, u_lo = sb("u_hi", [P, KD, TOK], F32R), sb("u_lo", [P, KD, TOK], F32R)
        xt = sb("xt", [P, TJ, D])
        xr = sb("xr", [P, RC, CONV - 1 + TOK])
        yg = sb("yg", [P, RC, TOK])
        ao = sb("ao", [P, RC, TOK])
        t1 = sb("t1", [P, RC, TOK])
        xc = sb("xc", [P, RC, TOK])
        rr = sb("rr", [P, RC, TOK])
        ig = sb("ig", [P, RC, TOK])
        qT = sb("qT", [P, G, TOK])
        kT, vT = sb("kT", [P, CHUNK + TOK]), sb("vT", [P, CHUNK + TOK])
        vb = sb("vb", [P, TOK // CHUNK, P])
        ss = sb("ss", [P, TJ, HEADS, P])
        stage = [t[:].rearrange("p c t -> p (c t)") for t in (rr, ig, t1, xc)]
        pT = sb("pT", [P, HEADS, P])
        bT = sb("bT", [P, G, TOK])
        bias = sb("bias", [P, 2, HEADS, P])
        wg = sb("wg", [P, RC, 2, P])
        ident = sb("ident", [P, P])
        g1 = sb("g1", [P, KD])
        cw, cb = sb("cw", [P, CONV, RC]), sb("cb", [P, RC])
        brg, big, lam = sb("brg", [P, RC]), sb("big", [P, RC]), sb("lam", [P, RC])
        la, lb, lc, ld, le = (sb(n, [P, RC]) for n in ("la", "lb", "lc", "ld", "le"))
        sp4 = sb("sp4", [P, RC])
        sink, neg_sink = sb("sink", [P, HEADS]), sb("neg_sink", [P, HEADS])
        carry = sb("carry", [P, RC])
        ssq, rstd = sb("ssq", [P, TJ]), sb("rstd", [P, TJ])
        eps = sb("eps", [P, 1])
        mx, nm, sd, den, rs = (sb(n, [P, HEADS]) for n in ("mx", "nm", "sd", "den", "rs"))

        bank = [ps(f"proj{b}", [P, 512]) for b in range(2)]
        tp = ps("tp", [P, KD, P])
        sc = ps("sc", [P, HEADS, P])
        gt = ps("gt", [P, 2, TOK])
        ot = ps("ot", [P, G, P])

        NCH = D_IN // P

        FIRST, REST = slice(Q0, D_IN), slice(0, Q0)

        def w_cols(w, k, m):
            if m < 2:
                c0 = (V0, K0)[m]
            elif m < 2 + G:
                c0 = Q0 + (m - 2) * P
            else:
                c0 = (m - 2 - G) * P
            return w[:, k, c0:c0 + P]

        def pieces(w, k, b, first):
            row, nq = w[:, bass.ds(k, 1)].rearrange("p one n -> p (one n)"), K0 - Q0
            if not first:
                return [(row[:, REST], stage[b])]
            q = row[:, Q0:K0].rearrange("p (c v d) -> p v c d", c=G, v=KV)
            q_staged = stage[b][:, 0:nq].rearrange("p (v c d) -> p v c d", c=G, v=KV)
            return [(q[:, v], q_staged[:, v]) for v in range(KV)] + [(row[:, K0:], stage[b][:, nq:D_IN - Q0])]

        consts_in = sig("consts_in", 0)
        gate_w_zero, const_ready = sig("gate_w_zero", 0), sig("const_ready", 0)
        tables_ready, lambda_abs, lambda_exp = sig("tables_ready", 0), sig("lambda_abs", 0), sig("lambda_exp", 0)
        g1_in = sig("g1_in", 0)
        w_staged = [sig(f"w_staged{b}", 1, step=16) for b in range(4)]
        w_hi_done, w_lo_done = sig("w_hi_done", 4), sig("w_lo_done", 4)
        x_in = [sig(f"x_in{j}", 1, 1, 16) for j in range(TJ)]
        x_squared, rms_done, x_scaled = sig("x_squared", TJ, TJ), sig("rms_done", 1, 1), sig("x_scaled", TJ, TJ)
        u_transposed = sig("u_transposed", TJ, TJ)
        u_hi_done, u_lo_done = sig("u_hi_done", TJ, TJ), sig("u_lo_done", TJ, TJ)
        v_transposed, v_taken = sig("v_transposed", 1), sig("v_taken", 1)
        p_transposed, p_taken = sig("p_transposed", TJ), sig("p_taken", TJ)
        projected, proj_taken = sig("projected", NCH), sig("proj_taken", NCH, 2)
        scored, scores_taken = sig("scored", TJ), sig("scores_taken", TJ, 1)
        smax_done, exp_done, p_ready = sig("smax_done", TJ), sig("exp_done", TJ), sig("p_ready", TJ)
        pv_done, ot_taken = sig("pv_done", TJ, 1), sig("ot_taken", TJ, 1)
        conv_done, xr_free = sig("conv_done", RC), sig("xr_free", 1, 1)
        gelu_sq, gelu_poly, gelu_sig, gelu_done = (sig(f"gelu_{n}", 1) for n in ("sq", "poly", "sig", "done"))
        gated, gates_taken = sig("gated", RC), sig("gates_taken", RC, 1)
        s_done, sqrt_done, rnn_done = sig("s_done", 1), sig("sqrt_done", 1), sig("rnn_done", 1, 1)
        a_stored, b_stored = sig("a_stored", 1, 1, 16), sig("b_stored", 1, 1, 16)
        stores_begun = sig("stores_begun", 2)
        step = Chain(ctx, nc, "dve_step", 4 * TJ + 3 * RC + 12)

        NCONST, CONST_STEPS = 5 + CONV + 4, 9
        x_tiles = x.rearrange("(t p) n -> t p n", p=P)
        mix_rows = mixT.rearrange("c p t -> p c t")
        block = ctx.enter_context(nc.Block())

        @block.sync
        def _(sp):
            w_chunks = w_in[0].rearrange("(k p) n -> k p n", p=P)
            def stage_w(k, b, cut):
                w_staged[b].by(sp.dma_start(stage[b][:, 0:cut.stop - cut.start], w_chunks[k, :, cut]))

            for j in range(TJ):
                x_in[j].by(sp.dma_start(xt[:, j], x_tiles[j]))
            sp.dma_start(g1[:], norm1_g[0].rearrange("(c p) -> p c", p=P),
                         allow_slow_non_contiguous=True).then_inc(g1_in.sem, 16)
            for b in range(4):
                stage_w(b, b, FIRST)
            for b in range(4):
                w_lo_done.wait(sp, 0, b + 1)
                stage_w(4 + b, b, FIRST)
            with sp.Fori(2, 4) as n:
                for b in range(4):
                    w_lo_done.wait(sp, n, b - 3)
                    sp.sem_inc(stores_begun.sem, 1)
                    stage_w(n * 4 + (b - KD), b, REST)
            sp.sem_inc(a_stored.sem, 16)
            sp.sem_inc(b_stored.sem, 16)

            def load_x(nxt, g):
                for j in range(TJ):
                    u_transposed.wait(sp, g, j + 1 - TJ)
                    x_in[j].by(sp.dma_start(xt[:, j], x_tiles[nxt * TJ + j]))

            def store_a(g):
                rnn_done.wait(sp, g, 1)
                sp.sem_inc(stores_begun.sem, 1)
                a_stored.by(sp.dma_start(mix_rows[:, 0:RC, bass.ds(g * TOK, TOK)], ao[:]))

            def store_b(g):
                ot_taken.wait(sp, g, TJ)
                sp.sem_inc(stores_begun.sem, 1)
                b_stored.by(sp.dma_start(mix_rows[:, RC:, bass.ds(g * TOK, TOK)], bT[:]))

            load_x(1, 0)
            store_b(0)
            with sp.Fori(1, NG) as g:
                load_x(sp.snap((g + 1) % NG), g)
                store_a(g - 1)
                store_b(g)
            store_a(NG - 1)
            for s in (x_in[0], x_in[1], a_stored, b_stored):
                sp.wait_ge(s.sem, 16 * (NG + 1))

        @block.gpsimd
        def _(pool):
            pool.memset(wg[:], 0.0).then_inc(gate_w_zero.sem, 1)
            pool.memset(ident[:], 0.0).then_inc(const_ready.sem, 1)
            pool.wait_ge(const_ready.sem, 1)
            pool.affine_select(out=ident[:], in_=ident[:], compare_op=ALU.not_equal, fill=1.0, base=0,
                               pattern=[[-1, P]], channel_multiplier=1).then_inc(const_ready.sem, 1)
            pool.memset(eps[:], EPS).then_inc(const_ready.sem, 1)
            for half in range(2):
                pool.wait_ge(const_ready.sem, 3 + half)
                pool.iota(pT[64 * half:64 * half + 64, 0, :].bitcast(I32), pattern=[[-1, P]], base=CHUNK,
                          channel_multiplier=1).then_inc(const_ready.sem, 1)
            pool.wait_ge(const_ready.sem, 5)
            for t in (xr, kT, vT, carry):
                pool.memset(t[:], 0.0).then_inc(const_ready.sem, 1)
            for dst, src in ((cb, conv_b), (brg, b_rg), (big, b_ig), (lam, lru_lambda)):
                pool.dma_start(dst[:], src[0].rearrange("(c p) -> p c", p=P),
                            allow_slow_non_contiguous=True).then_inc(consts_in.sem, 16)
            pool.dma_start(sink[:], attn_sinks[0].partition_broadcast(P)).then_inc(consts_in.sem, 16)
            for k in range(CONV):
                pool.dma_start(cw[:, k, :], conv_w[0, k].rearrange("(c p) -> p c", p=P),
                            allow_slow_non_contiguous=True).then_inc(consts_in.sem, 16)
            pool.wait_ge(gate_w_zero.sem, 1)
            for s, w in enumerate((w_rg, w_ig)):
                for half in range(2):
                    pool.dma_start(wg[64 * half:64 * half + 64, :, s, 64 * half:64 * half + 64],
                                w[0].rearrange("(c h) i o -> h i c o", h=2)[half]).then_inc(consts_in.sem, 16)

        @block.tensor
        def _(pe):
            def transpose_u(g, j):
                x_scaled.wait(pe, g, j + 1)
                for k in range(KD):
                    ins = pe.transpose((tp, sc)[j][:, k], xt[:, j, k * P:(k + 1) * P], ident[:])
                u_transposed.by(ins)

            def project(g, m):
                proj_taken.wait(pe, g, m - 1)
                for k in range(KD):
                    ins = product3(pe, bank[m % 2][:, 0:TOK], w_cols(w_hi, k, m), w_cols(w_lo, k, m),
                                   u_hi[:, k], u_lo[:, k], k == 0, k == KD - 1)
                projected.by(ins)

            def transpose_v(g):
                proj_taken.wait(pe, g, 1)
                for c in range(TOK // CHUNK):
                    ins = pe.transpose(tp[:, c], vT[:, c * CHUNK:c * CHUNK + P], ident[:])
                v_transposed.by(ins)

            def score(g, j):
                for n in range(2 * HEADS):
                    h, half = n // 4 + G * (n % 2), (n % 2) ^ (n // 2 % 2)
                    kv = slice(64 * (h // G), 64 * (h // G) + 64)
                    c = 2 * j + half
                    ins = pe.matmul(sc[64 * half:64 * half + 64, h], qT[kv, h % G, c * CHUNK:(c + 1) * CHUNK],
                                    kT[kv, c * CHUNK:c * CHUNK + P], start=True, stop=True)
                scored.by(ins)

            def transpose_p(g, j):
                p_ready.wait(pe, g, j + 1)
                for h in range(HEADS):
                    ins = pe.transpose(tp[:, h], ss[:, j, h], ident[:])
                p_transposed.by(ins)

            def attend(g, j):
                p_taken.wait(pe, g, j + 1)
                ot_taken.wait(pe, g, j)
                for v in range(KV):
                    for half in range(2):
                        ins = pe.matmul(ot[64 * v:64 * v + 64, :, 64 * half:64 * half + 64],
                                        vb[:, 2 * j + half, 64 * v:64 * v + 64],
                                        pT[:, G * v:G * v + G, 64 * half:64 * half + 64], start=True, stop=True)
                pv_done.by(ins)

            def gate(g, c):
                conv_done.wait(pe, g, c + 1)
                gates_taken.wait(pe, g, c)
                for s in range(2):
                    ins = pe.matmul(gt[:, s], wg[:, c, s], xc[:, c], start=True, stop=True)
                gated.by(ins)

            pe.wait_ge(const_ready.sem, CONST_STEPS)
            for j in range(TJ):
                transpose_u(-1, j)
            pe.wait_ge(w_lo_done.sem, KD)
            pe.sem_inc(pv_done.sem, 1)

            def group(g):
                u_lo_done.wait(pe, g, 0)
                for m in range(2 + G):
                    project(g, m)
                transpose_v(g)
                proj_taken.wait(pe, g, 2 + G)
                if isinstance(g, int):
                    pe.wait_ge(w_lo_done.sem, 2 * KD)
                    pe.wait_ge(consts_in.sem, 16 * NCONST)
                project(g, 6)
                score(g, 0)
                project(g, 7)
                scores_taken.wait(pe, g, 1)
                project(g, 8)
                score(g, 1)
                project(g, 9)
                project(g, 10)
                v_taken.wait(pe, g, 1)
                transpose_p(g, 0)
                gate(g, 0)
                project(g, 11)
                attend(g, 0)
                gate(g, 1)
                project(g, 12)
                transpose_p(g, 1)
                gate(g, 2)
                project(g, 13)
                p_taken.wait(pe, g, 2)
                transpose_u(g, 0)
                scores_taken.wait(pe, g, 2)
                transpose_u(g, 1)
                gate(g, 3)
                attend(g, 1)

            group(0)
            with pe.Fori(1, NG) as g:
                group(g)
        @block.scalar
        def _(a):
            def square_x(g, j):
                x_in[j].wait(a, g, 1)
                x_squared.by(a.activation(ss[:, j].rearrange("p h n -> p (h n)"), xt[:, j], ACT.Square,
                                          accum_out=ssq[:, j:j + 1]))

            def rms(g):
                x_squared.wait(a, g, TJ)
                rms_done.by(a.activation(ssq[:], ssq[:], ACT.Sqrt, bias=eps[:, 0:1], scale=1.0 / D))

            def take_hi(g, j):
                u_transposed.wait(a, g, j + 1)
                u_hi_done.by(a.activation(u_hi[:, :, j * P:(j + 1) * P], (tp, sc)[j][:], ACT.Copy))

            a.wait_ge(const_ready.sem, CONST_STEPS)
            for j in range(TJ):
                square_x(-1, j)
            rms(-1)
            for j in range(TJ):
                take_hi(-1, j)
            a.wait_ge(g1_in.sem, 16)
            for part in range(2):
                with a.Fori(2 * part, 2 * part + 2) as n:
                    for b in range(4):
                        k = n * 4 + (b - KD * part)
                        w_staged[b].wait(a, n, 1)
                        for dst, src in pieces(w_hi, k, b, part == 0):
                            ins = a.activation(dst, src, ACT.Copy, scale=g1[:, bass.ds(k, 1)])
                        w_hi_done.by(ins)
            a.sem_inc(proj_taken.sem, 2)
            a.sem_inc(gates_taken.sem, 1)
            a.sem_inc(ot_taken.sem, 1)
            a.wait_ge(lambda_abs.sem, 1)
            a.activation(lb[:], la[:], ACT.Exp, scale=-1.0).then_inc(lambda_exp.sem, 1)

            def take(g, m, dst, scale=1.0):
                projected.wait(a, g, m + 1)
                proj_taken.by(a.activation(dst, bank[m % 2][:, 0:TOK], ACT.Copy, scale=scale))

            def exps(g, j):
                smax_done.wait(a, g, j + 1)
                for h in range(HEADS):
                    a.activation(ss[:, j, h], ss[:, j, h], ACT.Exp, bias=nm[:, h:h + 1],
                                 accum_out=den[:, h:h + 1])
                exp_done.by(a.activation(sd[:], sd[:], ACT.Exp))

            def take_p(g, j):
                p_transposed.wait(a, g, j + 1)
                pv_done.wait(a, g, j)
                p_taken.by(a.activation(pT[:], tp[:], ACT.Copy))

            def take_o(g, j):
                pv_done.wait(a, g, j + 1)
                ot_taken.by(a.activation(bT[:, :, j * P:(j + 1) * P], ot[:], ACT.Copy))

            def take_gates(g, c):
                gated.wait(a, g, c + 1)
                a.activation(rr[:, c], gt[:, 0], ACT.Sigmoid, bias=brg[:, c:c + 1])
                gates_taken.by(a.activation(ig[:, c], gt[:, 1], ACT.Sigmoid, bias=big[:, c:c + 1]))

            def gelu_sigmoid(g):
                gelu_poly.wait(a, g, 1)
                gelu_sig.by(a.activation(t1[:], t1[:], ACT.Sigmoid, scale=2 * GELU_K * GELU_C))

            def decay(g):
                gates_taken.wait(a, g, RC)
                for c in range(RC):
                    ins = a.activation(rr[:, c], rr[:, c], ACT.Tanh, scale=sp4[:, c:c + 1])
                s_done.by(ins)

            def decay_root(g):
                s_done.wait(a, g, 1)
                gelu_done.wait(a, g, 1)
                sqrt_done.by(a.activation(t1[:], rr[:], ACT.Sqrt))

            def group(g):
                first = isinstance(g, int)
                take(g, 0, vT[:, CHUNK:])
                if not first:
                    gelu_sigmoid(g - 1)
                take(g, 1, kT[:, CHUNK:])
                if not first:
                    decay_root(g - 1)
                take(g, 2, qT[:, 0], scale=HD ** -0.5)
                for j in range(TJ):
                    square_x(g, j)
                    take(g, 3 + j, qT[:, 1 + j], scale=HD ** -0.5)
                rms(g)
                take(g, 5, qT[:, 3], scale=HD ** -0.5)
                v_transposed.wait(a, g, 1)
                v_taken.by(a.activation(vb[:], tp[:, 0:TOK // CHUNK], ACT.Copy))
                xr_free.wait(a, g, 0)
                take(g, 6, xr[:, 0, CONV - 1:])
                take(g, 7, xr[:, 1, CONV - 1:])
                if first:
                    a.wait_ge(tables_ready.sem, 1)
                exps(g, 0)
                take(g, 8, xr[:, 2, CONV - 1:])
                take(g, 9, xr[:, 3, CONV - 1:])
                exps(g, 1)
                rnn_done.wait(a, g, 0)
                b_stored.wait(a, g, 0)
                take(g, 10, yg[:, 0])
                take_p(g, 0)
                take_gates(g, 0)
                take(g, 11, yg[:, 1])
                take_o(g, 0)
                take_gates(g, 1)
                take(g, 12, yg[:, 2])
                take_p(g, 1)
                take_gates(g, 2)
                a.activation(kT[:, 0:CHUNK], kT[:, TOK:], ACT.Copy)
                a.activation(vT[:, 0:CHUNK], vT[:, TOK:], ACT.Copy)
                take(g, 13, yg[:, 3])
                for j in range(TJ):
                    take_hi(g, j)
                proj_taken.wait(a, g, NCH)
                gelu_sq.by(a.activation(t1[:], yg[:], ACT.Square))
                take_gates(g, 3)
                take_o(g, 1)
                decay(g)

            group(0)
            with a.Fori(1, NG) as g:
                group(g)
            gelu_sigmoid(NG - 1)
            decay_root(NG - 1)

        @block.vector
        def _(v):
            def chained(ins):
                step.step(ins)
                step.wait(v)

            def scale_x(g):
                rms_done.wait(v, g, 1)
                chained(v.reciprocal(rstd[:], ssq[:]))
                for j in range(TJ):
                    x_scaled.by(v.tensor_scalar(xt[:, j], xt[:, j], rstd[:, j:j + 1], None, ALU.mult))

            def take_lo(g, j):
                u_hi_done.wait(v, g, j + 1)
                u_lo_done.by(v.tensor_tensor(u_lo[:, :, j * P:(j + 1) * P], (tp, sc)[j][:],
                                             u_hi[:, :, j * P:(j + 1) * P].bitcast(F32), ALU.subtract))

            scale_x(-1)
            for j in range(TJ):
                take_lo(-1, j)
            v.wait_ge(g1_in.sem, 16)
            for part in range(2):
                with v.Fori(2 * part, 2 * part + 2) as n:
                    for b in range(4):
                        k = n * 4 + (b - KD * part)
                        w_hi_done.wait(v, n, b + 1)
                        for (dst, src), (hi, _) in zip(pieces(w_lo, k, b, part == 0), pieces(w_hi, k, b, part == 0)):
                            ins = v.scalar_tensor_tensor(out=dst, in0=src, scalar=g1[:, bass.ds(k, 1)],
                                                         in1=hi.bitcast(F32), op0=ALU.mult, op1=ALU.subtract)
                        w_lo_done.by(ins)
            v.wait_ge(consts_in.sem, 16 * NCONST)
            chained(v.tensor_scalar(lc[:], lam[:], -1.0, None, ALU.mult))
            v.tensor_tensor(la[:], lam[:], lc[:], ALU.max).then_inc(lambda_abs.sem, 1)
            v.wait_ge(lambda_exp.sem, 1)
            chained(v.tensor_scalar(ld[:], lb[:], 2.0, None, ALU.add))
            chained(v.reciprocal(ld[:], ld[:]))
            chained(v.tensor_tensor(lb[:], lb[:], ld[:], ALU.mult))
            chained(v.tensor_tensor(ld[:], lb[:], lb[:], ALU.mult))
            TERMS = 9
            chained(v.tensor_scalar(le[:], ld[:], 1.0 / (2 * TERMS - 1), 1.0 / (2 * TERMS - 3), ALU.mult, ALU.add))
            for n in range(TERMS - 3, -1, -1):
                chained(v.tensor_tensor(le[:], le[:], ld[:], ALU.mult))
                chained(v.tensor_scalar(le[:], le[:], 1.0 / (2 * n + 1), None, ALU.add))
            chained(v.tensor_tensor(le[:], le[:], lb[:], ALU.mult))
            chained(v.tensor_scalar(lc[:], lc[:], 0.0, LRU_C / 2, ALU.max, ALU.mult))
            chained(v.scalar_tensor_tensor(out=sp4[:], in0=le[:], scalar=LRU_C, in1=lc[:],
                                           op0=ALU.mult, op1=ALU.add))
            chained(v.tensor_scalar(neg_sink[:], sink[:], -1.0, None, ALU.mult))
            v.wait_ge(const_ready.sem, CONST_STEPS)
            chained(v.tensor_copy(pT[:, 1], pT[:, 0].bitcast(I32)))
            chained(v.tensor_scalar(pT[:, 2], pT[:, 1], -1.0, None, ALU.mult))
            chained(v.tensor_tensor(pT[:, 3], pT[:, 1], pT[:, 2], ALU.min))
            for h in range(HEADS):
                for b in range(2):
                    chained(v.tensor_scalar(bias[:, b, h], pT[:, 3], 2.0 ** (-8.0 * (h + 1) / HEADS), None, ALU.mult))
            chained(v.memset(bias[0:CHUNK, 0, :, 0:CHUNK], NEG))
            v.sem_inc(scores_taken.sem, 1)
            v.sem_inc(xr_free.sem, 1)
            v.sem_inc(rnn_done.sem, 1)
            v.sem_inc(tables_ready.sem, 1)

            def softmax_max(g, j):
                scored.wait(v, g, j + 1)
                table = 0 if isinstance(g, int) and j == 0 else 1
                scores_taken.by(v.tensor_tensor(ss[:, j], sc[:], bias[:, table], ALU.add))
                scores_taken.wait(v, g, j + 1)
                chained(v.tensor_reduce(mx[:], ss[:, j], AX.X, ALU.max, negate=True))
                chained(v.tensor_tensor(nm[:], mx[:], neg_sink[:], ALU.min))
                smax_done.by(v.tensor_tensor(sd[:], sink[:], nm[:], ALU.add))

            def softmax_scale(g, j):
                exp_done.wait(v, g, j + 1)
                chained(v.tensor_tensor(rs[:], den[:], sd[:], ALU.add))
                chained(v.reciprocal(rs[:], rs[:]))
                p_ready.by(v.tensor_tensor(ss[:, j], ss[:, j],
                                           rs[:].unsqueeze(2).to_broadcast([P, HEADS, P]), ALU.mult))

            def conv(g, c):
                proj_taken.wait(v, g, 2 + G + c + 1)
                chained(v.tensor_scalar(xc[:, c], xr[:, c, 0:TOK], cw[:, 0, c:c + 1], cb[:, c:c + 1],
                                        ALU.mult, ALU.add))
                for k in range(1, CONV):
                    ins = v.scalar_tensor_tensor(out=xc[:, c], in0=xr[:, c, k:k + TOK],
                                                 scalar=cw[:, k, c:c + 1], in1=xc[:, c],
                                                 op0=ALU.mult, op1=ALU.add)
                    conv_done.by(ins) if k == CONV - 1 else chained(ins)

            def recur(g):
                gelu_sig.wait(v, g, 1)
                gelu_done.by(v.tensor_tensor(yg[:], yg[:], t1[:], ALU.mult))
                gates_taken.wait(v, g, RC)
                step.step(v.tensor_tensor(ig[:], ig[:], xc[:], ALU.mult))
                sqrt_done.wait(v, g, 1)
                chained(v.tensor_scalar(rr[:], rr[:], 1.0, None, ALU.add))
                chained(v.reciprocal(rr[:], rr[:]))
                step.step(v.tensor_scalar(xc[:], rr[:], 2.0, -1.0, ALU.mult, ALU.add))
                chained(v.tensor_tensor(t1[:], t1[:], rr[:], ALU.mult))
                chained(v.scalar_tensor_tensor(out=ig[:].rearrange("p c t -> p (c t)"),
                                               in0=t1[:].rearrange("p c t -> p (c t)"), scalar=2.0,
                                               in1=ig[:].rearrange("p c t -> p (c t)"),
                                               op0=ALU.mult, op1=ALU.mult))
                for c in range(RC):
                    step.step(v.tensor_tensor_scan(rr[:, c], xc[:, c], ig[:, c], carry[:, c:c + 1],
                                                   ALU.mult, ALU.add))
                step.wait(v)
                chained(v.tensor_copy(carry[:], rr[:, :, TOK - 1]))
                gelu_done.wait(v, g, 1)
                a_stored.wait(v, g, 0)
                rnn_done.by(v.tensor_tensor(ao[:], rr[:], yg[:], ALU.mult))

            def group(g):
                if not isinstance(g, int):
                    recur(g - 1)
                scale_x(g)
                softmax_max(g, 0)
                conv(g, 0)
                conv(g, 1)
                softmax_scale(g, 0)
                softmax_max(g, 1)
                conv(g, 2)
                conv(g, 3)
                softmax_scale(g, 1)
                xr_free.by(v.tensor_copy(xr[:, :, 0:CONV - 1], xr[:, :, TOK:TOK + CONV - 1]))
                for j in range(TJ):
                    take_lo(g, j)
                gelu_sq.wait(v, g, 1)
                gelu_poly.by(v.scalar_tensor_tensor(out=t1[:].rearrange("p c t -> p (c t)"),
                                                    in0=t1[:].rearrange("p c t -> p (c t)"), scalar=1.0 / GELU_C,
                                                    in1=yg[:].rearrange("p c t -> p (c t)"),
                                                    op0=ALU.add, op1=ALU.mult))

            group(0)
            step.before, step.n = step.before + step.n, 0
            with v.Fori(1, NG) as g:
                step.g = g - 1
                group(g)
                step.leave()
            step.g, step.before, step.n = None, step.before + (NG - 1) * step.per, 0
            recur(NG - 1)

def project_out(nc, x, mixT, rnn_out_g, attn_out_g, w_out, norm2_g, w_group_router, w_expert_router,
                h_rows, u_rows, lists, slots, seen_out):
    with ExitStack() as ctx:
        def sb(name, shape, dt=F32):
            return ctx.enter_context(nc.sbuf_tensor(name, shape, dt))

        def ps(name, shape):
            return ctx.enter_context(nc.psum_tensor(name, shape, F32))

        def sig(name, per=2, step=1):
            return Signal(ctx, nc, name, per, 0, step)

        N2 = D // 2
        R = GROUPS + E
        o_hi, o_lo = sb("o_hi", [P, KD, D], F32R), sb("o_lo", [P, KD, D], F32R)
        wst = sb("wst", [P, KD, D])
        og = sb("og", [P, KD])
        g2 = sb("g2", [P, D])
        wr = sb("wr", [P, KD, R])
        mt = sb("mt", [P, 2, KD, P])
        m_hi, m_lo = sb("m_hi", [P, 2, KD, P], F32R), sb("m_lo", [P, 2, KD, P], F32R)
        sq = sb("sq", [P, 2, RC, P])
        half_sum, sq_sum = sb("half_sum", [P, 2, RC // 2, P]), sb("sq_sum", [P, 2, P])
        xt, ht, ut = sb("x_tile", [P, 2, D]), sb("h_tile", [P, 2, D]), sb("u_tile", [P, 2, D])
        hsq = sb("hsq", [P, D])
        uT = sb("uT", [P, KD, P])
        ones, onesb = sb("ones", [P, 2]), sb("onesb", [P, P], BF16)
        before = sb("before", [P, P], BF16)
        idn = sb("idn", [P, P])
        epsc = sb("epsc", [P, 1])
        rab, rh = sb("rab", [P, 2, 2]), sb("rh", [P, 2])
        lg, g8, e8 = sb("lg", [P, 8]), sb("g8", [P, 8]), sb("e8", [P, 8])
        gi, ei = sb("gi", [P, 8], U32), sb("ei", [P, 8], U32)
        ngm, gif, pen = sb("ngm", [P, 1]), sb("gif", [P, 1]), sb("pen", [P, GROUPS])
        pg, gsum, ex, nl = sb("pg", [P, GROUPS]), sb("gsum", [P, 1]), sb("ex", [P, 1]), sb("nl", [P, 1])
        em, hot, sel = sb("em", [P, E]), sb("hot", [P, TOP, E]), sb("sel", [P, TOP, E])
        chosen, seen = sb("chosen", [P, E], BF16), sb("seen", [P, E], BF16)
        slot = sb("slot", [P, 6])
        at = [sb(f"at{b}", [P, TOP], U32) for b in range(2)]
        tokf, toki = sb("tokf", [P, 2]), [sb(f"toki{b}", [P, 1], I32) for b in range(2)]
        iota_i, iota_e = sb("iota_i", [P, E], I32), sb("iota_e", [P, E])
        tok0 = sb("tok0", [P, 2], I32)
        zeros = sb("zeros", [P, E * LIST // P], I32)

        pa, pb = ps("pa", [P, 2, N2]), ps("pb", [P, 2, N2])
        tps = ps("tps", [P, KD, P])
        sums = ps("sums", [P, 512])
        rt = ps("rt", [P, 512])
        LOGIT, RANK = 0, 64

        consts_in, const_ready = sig("consts_in2"), sig("const_ready2")
        w_half_in = [sig(f"w_half_in{s}") for s in range(2)]
        o_hi_done, o_lo_done = sig("o_hi_done"), sig("o_lo_done")
        lists_zero = sig("lists_zero")
        mix_in = [sig(f"mix_in{b}", 1, 32) for b in range(2)]
        m_hi_done, m_squared, m_lo_done = sig("m_hi_done"), sig("m_squared"), sig("m_lo_done")
        half_folded, folded = sig("half_folded"), sig("folded")
        summed, roots, a_done, a_added = sig("summed"), sig("roots"), sig("a_done"), sig("a_added")
        b_done, b_added = sig("b_done"), sig("b_added")
        h_squared, h_root, u_ready = sig("h_squared"), sig("h_root"), sig("u_ready")
        h_stored = [sig(f"h_stored{b}", 1, 16) for b in range(2)]
        u_stored = [sig(f"u_stored{b}", 1, 16) for b in range(2)]
        u_turned, uT_done, routed = sig("u_turned"), sig("uT_done"), sig("routed")
        group_max, group_exp, expert_max, expert_exp = (sig(n) for n in ("group_max", "group_exp", "expert_max",
                                                                        "expert_exp"))
        chosen_done, ranked, slots_done = sig("chosen_done"), sig("ranked"), sig("slots_done")
        scattered = [sig(f"scattered{b}", 1, 32) for b in range(2)]
        at_free = Signal(ctx, nc, "at_free", 2, 2)
        sp_begun, pool_begun, settled, ranks_end = (sig(n) for n in ("sp_begun", "pool_begun", "settled", "ranks_end"))
        ROUTE_STEPS, RANK_STEPS, NORM_STEPS = 14, 6, 2
        step = Chain(ctx, nc, "dve_step2", 2 * (ROUTE_STEPS + RANK_STEPS + NORM_STEPS))
        NCONST, CONST_STEPS = 3, 13
        block = ctx.enter_context(nc.Block())
        x_tiles, h_tiles, u_tiles = (t.rearrange("(t p) n -> t p n", p=P) for t in (x, h_rows, u_rows))
        mix_cols = mixT.rearrange("c p t -> p c t")

        @block.sync
        def _(sp):
            def load(i, b):
                mix_t = mix_cols[:, :, bass.ds(i * P, P)]
                sp.dma_start(mt[:, b], mix_t).then_inc(mix_in[b].sem, 16)
                sp.dma_start(xt[:, b], x_tiles[i]).then_inc(mix_in[b].sem, 16)

            pieces = [[(og[:, 0:RC], rnn_out_g[0].rearrange("(c p) -> p c", p=P))], []]
            for v in range(KV):
                half = slice(64 * v, 64 * v + 64)
                pieces[1].append((og[half, RC:], attn_out_g[0].rearrange("(v c d) -> v d c", v=KV, c=G)[v]))
            for c in range(RC):
                pieces[0].append((wst[:, c], w_out[0, c * P:(c + 1) * P]))
            for v in range(KV):
                pieces[1].append((wst[64 * v:64 * v + 64, RC:],
                                  w_out[0, D_RNN:].rearrange("(v c d) n -> v d c n", v=KV, c=G)[v]))
            load(0, 0)
            for s in range(2):
                for dst, src in pieces[s]:
                    sp.dma_start(dst, src, allow_slow_non_contiguous=True).then_inc(w_half_in[s].sem, 16)
            load(1, 1)
            sp.dma_start(g2[:], norm2_g[0].partition_broadcast(P)).then_inc(consts_in.sem, 16)
            sp.dma_start(wr[:, :, 0:GROUPS], w_group_router[0].rearrange("(k p) e -> p k e", p=P),
                         allow_slow_non_contiguous=True).then_inc(consts_in.sem, 16)
            sp.dma_start(wr[:, :, GROUPS:], w_expert_router[0].rearrange("(k p) e -> p k e", p=P),
                         allow_slow_non_contiguous=True).then_inc(consts_in.sem, 16)
            sp.wait_ge(const_ready.sem, CONST_STEPS)
            sp.dma_start(lists.rearrange("(p n) one -> p (n one)", p=P), zeros[:]).then_inc(lists_zero.sem, 16)

            def tile(g, b):
                m_lo_done.wait(sp, g, b + 1)
                m_squared.wait(sp, g, b + 1)
                a_added.wait(sp, g, b + 1)
                sp.sem_inc(sp_begun.sem, 1)
                if isinstance(g, int):
                    load((2 * g + b + 2) % NT, b)
                else:
                    load(sp.snap((g * 2 + (b + 2)) % NT), b)
                b_added.wait(sp, g, b + 1)
                sp.sem_inc(sp_begun.sem, 1)
                h_stored[b].by(sp.dma_start(h_tiles[g * 2 + b], ht[:, b]))
                u_ready.wait(sp, g, b + 1)
                sp.sem_inc(sp_begun.sem, 1)
                u_stored[b].by(sp.dma_start(u_tiles[g * 2 + b], ut[:, b]))

            for b in range(2):
                tile(0, b)
            with sp.Fori(1, NT // 2) as g:
                for b in range(2):
                    tile(g, b)
            sp.wait_ge(lists_zero.sem, 16)
            for b in range(2):
                sp.wait_ge(h_stored[b].sem, 16 * (NT // 2))
                sp.wait_ge(u_stored[b].sem, 16 * (NT // 2))
                sp.wait_ge(mix_in[b].sem, 32 * (NT // 2 + 1))

        @block.gpsimd
        def _(pool):
            made = 0

            def then(ins):
                nonlocal made
                made += 1
                ins.then_inc(const_ready.sem, 1)
                pool.wait_ge(const_ready.sem, made)

            then(pool.memset(zeros[:], 0))
            then(pool.memset(idn[:], 0.0))
            then(pool.affine_select(out=idn[:], in_=idn[:], compare_op=ALU.not_equal, fill=1.0, base=0,
                                    pattern=[[-1, P]], channel_multiplier=1))
            then(pool.memset(before[:], 1.0))
            then(pool.affine_select(out=before[:], in_=before[:], compare_op=ALU.is_gt, fill=0.0, base=0,
                                    pattern=[[1, P]], channel_multiplier=-1))
            then(pool.memset(onesb[:], 1.0))
            then(pool.memset(ones[:], 1.0))
            then(pool.memset(epsc[:], EPS))
            then(pool.memset(lg[:], NEG))
            then(pool.memset(seen[:], 0.0))
            then(pool.memset(hsq[:], 0.0))
            then(pool.iota(iota_i[:], pattern=[[1, E]], base=0, channel_multiplier=0))
            then(pool.iota(tok0[:], pattern=[[P, 2]], base=0, channel_multiplier=1))
            assert made == CONST_STEPS
            pool.sem_inc(at_free.sem, 2)

            def fold(g, b):
                m_squared.wait(pool, g, b + 1)
                half_folded.by(pool.tensor_tensor(half_sum[:], sq[:, :, 0:RC // 2], sq[:, :, RC // 2:], ALU.add))
                half_folded.wait(pool, g, b + 1)
                summed.wait(pool, g, b)
                folded.by(pool.tensor_tensor(sq_sum[:], half_sum[:, :, 0], half_sum[:, :, 1], ALU.add))

            def scatter(g, b):
                slots_done.wait(pool, g, b + 1)
                pool.sem_inc(pool_begun.sem, 1)
                for k in range(TOP):
                    pool.indirect_dma_start(lists, bass.IndirectOffsetOnAxis(ap=at[b % 2][:, k:k + 1], axis=0),
                                            toki[b % 2][:], None).then_inc(scattered[b % 2].sem, 16)

            def scatter_done(g, b):
                scattered[b % 2].wait(pool, g, b // 2 + 1)
                pool.sem_inc(at_free.sem, 1)

            assert RC == 4
            fold(0, 0)

            def tile(g, b):
                t = 2 * g + b if isinstance(g, int) else 2
                fold(g, b + 1)
                if t >= 2:
                    scatter_done(g, b - 2)
                if t == 1:
                    pool.wait_ge(lists_zero.sem, 16)
                if t >= 1:
                    scatter(g, b - 1)

            for b in range(2):
                tile(0, b)
            with pool.Fori(1, NT // 2) as g:
                for b in range(2):
                    tile(g, b)
            scatter_done(NT // 2 - 1, 0)
            scatter(NT // 2 - 1, 1)
            scatter_done(NT // 2 - 1, 1)

        @block.tensor
        def _(pe):
            def product(dst, half, b, c0):
                for c in range(RC):
                    k = c0 + c
                    cut = bass.ts(half, N2)
                    ins = product3(pe, dst[:, half], m_hi[:, b, k], m_lo[:, b, k],
                                   o_hi[:, k, cut], o_lo[:, k, cut], c == 0, c == RC - 1)
                return ins

            def sum_squares(g, b):
                folded.wait(pe, g, b + 1)
                roots.wait(pe, g, b)
                for s in range(2):
                    ins = pe.matmul(sums[:, 2 * s:2 * s + 2], sq_sum[:, s], ones[:], start=True, stop=True)
                summed.by(ins)

            def rank(g, b):
                chosen_done.wait(pe, g, b + 1)
                pe.matmul(rt[:, RANK:RANK + E], before[:], chosen[:], start=True, stop=False)
                ranked.by(pe.matmul(rt[:, RANK:RANK + E], onesb[:], seen[:], start=False, stop=True))

            def turn_u(g, b):
                u_ready.wait(pe, g, b + 1)
                uT_done.wait(pe, g, b)
                for k in range(KD):
                    ins = pe.transpose(tps[:, k], ut[:, b, k * P:(k + 1) * P], idn[:])
                u_turned.by(ins)

            def route(g, b):
                uT_done.wait(pe, g, b + 1)
                slots_done.wait(pe, g, b)
                for k in range(KD):
                    ins = pe.matmul(rt[:, LOGIT:LOGIT + R], uT[:, k], wr[:, k], start=(k == 0), stop=(k == KD - 1))
                routed.by(ins)

            pe.wait_ge(const_ready.sem, CONST_STEPS)
            sum_squares(0, 0)
            pe.wait_ge(o_lo_done.sem, RC)
            m_lo_done.wait(pe, 0, 1)
            product(pa, 0, 0, 0)
            a_done.by(product(pa, 1, 0, 0))
            pe.wait_ge(o_lo_done.sem, KD)
            pe.wait_ge(consts_in.sem, 16 * NCONST)

            def tile(g, b):
                first = isinstance(g, int) and b == 0
                b_added.wait(pe, g, b)
                product(pb, 0, b, RC)
                if not first:
                    route(g, b - 1)
                b_done.by(product(pb, 1, b, RC))
                sum_squares(g, b + 1)
                m_lo_done.wait(pe, g, b + 2)
                a_added.wait(pe, g, b + 1)
                product(pa, 0, 1 - b, 0)
                a_done.by(product(pa, 1, 1 - b, 0))
                if not first:
                    rank(g, b - 1)
                turn_u(g, b)

            for b in range(2):
                tile(0, b)
            with pe.Fori(1, NT // 2) as g:
                for b in range(2):
                    tile(g, b)
            route(NT // 2 - 1, 1)
            rank(NT // 2 - 1, 1)

        @block.scalar
        def _(a):
            def split(g, b):
                mix_in[b % 2].wait(a, g, 1 + b // 2)
                folded.wait(a, g, b)
                m_squared.by(a.activation(sq[:].rearrange("p s c n -> p (s c) n"), mt[:, b % 2], ACT.Square))
                m_hi_done.by(a.activation(m_hi[:, b % 2], mt[:, b % 2], ACT.Copy))

            def root(g, b):
                summed.wait(a, g, b + 1)
                b_added.wait(a, g, b - 1)
                roots.by(a.activation(rab[:, b % 2], sums[:, 0:4:2], ACT.Sqrt, bias=epsc[:, 0:1], scale=1.0 / D_RNN))

            split(0, 0)
            for k in range(KD):
                if k % RC == 0:
                    a.wait_ge(w_half_in[k // RC].sem, 16 * (5, 4)[k // RC])
                o_hi_done.by(a.activation(o_hi[:, k], wst[:, k], ACT.Copy, scale=og[:, k:k + 1]))
                if k == RC - 1:
                    a.wait_ge(const_ready.sem, CONST_STEPS)
                    root(0, 0)

            def exps(g, b):
                group_max.wait(a, g, b + 1)
                group_exp.by(a.activation(pg[:], lg[:, 0:GROUPS], ACT.Exp, bias=ngm[:, 0:1], accum_out=gsum[:, 0:1]))
                expert_max.wait(a, g, b + 1)
                expert_exp.by(a.activation(ex[:], e8[:, 1:2], ACT.Exp, bias=nl[:, 0:1]))

            def tile(g, b):
                first = isinstance(g, int) and b == 0
                b_done.wait(a, g, b)
                split(g, b + 1)
                root(g, b + 1)
                b_added.wait(a, g, b + 1)
                u_ready.wait(a, g, b)
                h_squared.by(a.activation(hsq[:], ht[:, b], ACT.Square, accum_out=rh[:, 0:1]))
                h_squared.wait(a, g, b + 1)
                h_root.by(a.activation(rh[:, 1:2], rh[:, 0:1], ACT.Sqrt, bias=epsc[:, 0:1], scale=1.0 / D))
                if not first:
                    exps(g, b - 1)
                u_turned.wait(a, g, b + 1)
                uT_done.by(a.activation(uT[:], tps[:], ACT.Copy))

            for b in range(2):
                tile(0, b)
            with a.Fori(1, NT // 2) as g:
                for b in range(2):
                    tile(g, b)
            exps(NT // 2 - 1, 1)

        @block.vector
        def _(v):
            def chained(ins):
                step.step(ins)
                step.wait(v)

            def lower(g, b):
                m_hi_done.wait(v, g, b + 1)
                m_lo_done.by(v.tensor_tensor(m_lo[:, b % 2], mt[:, b % 2], m_hi[:, b % 2].bitcast(F32),
                                             ALU.subtract))

            def add_a(g, b):
                a_done.wait(v, g, b + 1)
                h_stored[b % 2].wait(v, g, b // 2)
                a_added.by(v.scalar_tensor_tensor(out=ht[:, b % 2], in0=pa[:].rearrange("p a n -> p (a n)"),
                                                  scalar=rab[:, b % 2, 0:1], in1=xt[:, b % 2], op0=ALU.mult, op1=ALU.add))

            def choose(g, b):
                routed.wait(v, g, b + 1)
                chained(v.tensor_copy(lg[:, 0:GROUPS], rt[:, LOGIT:LOGIT + GROUPS]))
                v.sem_inc(settled.sem, 1)
                chained(v.max(g8[:], lg[:]))
                v.sem_inc(settled.sem, 1)
                step.step(v.max_index(gi[:], g8[:], lg[:]))
                group_max.by(v.tensor_scalar(ngm[:], g8[:, 0:1], -1.0, None, ALU.mult))
                step.wait(v)
                chained(v.tensor_copy(gif[:], gi[:, 0:1]))
                chained(v.tensor_scalar(pen[:], iota_e[:, 0:GROUPS], gif[:, 0:1], -NEG, ALU.is_equal, ALU.mult))
                chained(v.scalar_tensor_tensor(out=em[:].rearrange("p (g e) -> p g e", e=EPG),
                                               in0=pen[:].unsqueeze(2).to_broadcast([P, GROUPS, EPG]), scalar=NEG,
                                               in1=rt[:, LOGIT + GROUPS:LOGIT + R].rearrange("p (g e) -> p g e", e=EPG),
                                               op0=ALU.add, op1=ALU.add))
                v.sem_inc(settled.sem, 1)
                chained(v.max(e8[:], em[:]))
                v.sem_inc(settled.sem, 1)
                step.step(v.max_index(ei[:], e8[:], em[:]))
                expert_max.by(v.tensor_scalar(nl[:], e8[:, 0:1], -1.0, None, ALU.mult))
                step.wait(v)
                chained(v.tensor_copy(slot[:, 0:TOP], ei[:, 0:TOP]))
                step.step(v.tensor_scalar(hot[:, 0], iota_e[:], slot[:, 0:1], None, ALU.is_equal))
                chained(v.tensor_scalar(hot[:, 1], iota_e[:], slot[:, 1:2], None, ALU.is_equal))
                chosen_done.by(v.tensor_tensor(chosen[:], hot[:, 0], hot[:, 1], ALU.add))

            def place(g, b):
                group_exp.wait(v, g, b + 1)
                expert_exp.wait(v, g, b + 1)
                chained(v.tensor_scalar(slot[:, 4:5], ex[:], 1.0, gsum[:, 0:1], ALU.add, ALU.mult))
                chained(v.reciprocal(slot[:, 4:5], slot[:, 4:5]))
                step.step(v.tensor_tensor(slot[:, 5:6], slot[:, 4:5], ex[:], ALU.mult))
                ranked.wait(v, g, b + 1)
                at_free.wait(v, g, b - 1)
                step.step(v.tensor_tensor(sel[:], hot[:], rt[:, RANK:RANK + E].unsqueeze(1)
                                          .to_broadcast([P, TOP, E]), ALU.mult))
                chained(v.tensor_tensor(seen[:], seen[:], chosen[:], ALU.add))
                chained(v.tensor_reduce(slot[:, 2:4], sel[:], AX.X, ALU.add))
                par = b % 2
                chained(v.tensor_copy(slots[:, bass.ds(g * 2 + b, 1)].rearrange("p one n -> p (one n)"), slot[:])
                        if not isinstance(g, int) else v.tensor_copy(slots[:, 2 * g + b], slot[:]))
                chained(v.tensor_copy(toki[par][:], tokf[:, par:par + 1]))
                step.step(v.tensor_scalar(tokf[:, par:par + 1], tokf[:, par:par + 1], 2.0 * P, None, ALU.add))
                slots_done.by(v.scalar_tensor_tensor(out=at[par][:], in0=slot[:, 0:2], scalar=float(LIST),
                                                     in1=slot[:, 2:4], op0=ALU.mult, op1=ALU.add))

            lower(0, 0)
            for k in range(KD):
                o_hi_done.wait(v, 0, k + 1)
                o_lo_done.by(v.scalar_tensor_tensor(out=o_lo[:, k], in0=wst[:, k], scalar=og[:, k:k + 1],
                                                    in1=o_hi[:, k].bitcast(F32), op0=ALU.mult, op1=ALU.subtract))
            v.wait_ge(const_ready.sem, CONST_STEPS)
            chained(v.tensor_copy(iota_e[:], iota_i[:]))
            chained(v.tensor_copy(tokf[:], tok0[:]))
            roots.wait(v, 0, 1)
            chained(v.reciprocal(rab[:, 0], rab[:, 0]))
            add_a(0, 0)
            v.wait_ge(consts_in.sem, 16 * NCONST)

            def tile(g, b):
                first = isinstance(g, int) and b == 0
                lower(g, b + 1)
                if not first:
                    choose(g, b - 1)
                b_done.wait(v, g, b + 1)
                a_added.wait(v, g, b + 1)
                b_added.by(v.scalar_tensor_tensor(out=ht[:, b], in0=pb[:].rearrange("p a n -> p (a n)"),
                                                  scalar=rab[:, b, 1:2], in1=ht[:, b], op0=ALU.mult, op1=ALU.add))
                roots.wait(v, g, b + 2)
                chained(v.reciprocal(rab[:, 1 - b], rab[:, 1 - b]))
                h_root.wait(v, g, b + 1)
                chained(v.reciprocal(rh[:, 1:2], rh[:, 1:2]))
                u_stored[b].wait(v, g, 0)
                u_ready.by(v.scalar_tensor_tensor(out=ut[:, b], in0=ht[:, b], scalar=rh[:, 1:2], in1=g2[:],
                                                  op0=ALU.mult, op1=ALU.mult))
                add_a(g, b + 1)
                if not first:
                    place(g, b - 1)

            step.enter(0)
            for b in range(2):
                tile(0, b)
            step.before, step.n = step.before + step.n, 0
            with v.Fori(1, NT // 2) as g:
                step.g = g - 1
                for b in range(2):
                    tile(g, b)
                step.leave()
            step.g, step.before, step.n = None, step.before + (NT // 2 - 1) * step.per, 0
            choose(NT // 2 - 1, 1)
            place(NT // 2 - 1, 1)
            step.wait(v)
            ranks_end.by(v.tensor_copy(seen_out[:], seen[:]))


SPLIT, ROW, RUN, LOAD, NTH, ITERS, COLS = 0, 1, 2, 3, 4, 5, 8


def plan_blocks(nc, seen, slots, plan_dram, plan, dest):
    with ExitStack() as ctx:
        def sb(name, shape, dt=F32):
            return ctx.enter_context(nc.sbuf_tensor(name, shape, dt))

        ones = sb("ones_p", [P, P], BF16)
        zero = sb("zero_p", [P, E])
        cnt_i, nb_i = sb("cnt_i", [P, E], I32), sb("nb_i", [P, E], I32)
        nb, end, start = sb("nb", [P, E]), sb("end", [P, E]), sb("start", [P, E])
        ie, io = sb("ie", [P, E], I32), sb("io", [P, E])
        ib, block_no = sb("ib", [P, 1], I32), sb("block_no", [P, 1])
        ends, past, hot, tmp = (sb(n, [P, E]) for n in ("ends", "past", "hot_p", "tmp"))
        col = sb("col", [P, COLS])
        f = sb("f", [P, 12])
        iters = sb("iters", [P, 1], I32)
        tab = sb("tab", [P, COLS], I32)
        big = sb("big_p", [P, NT * TOP, E])
        row = sb("row", [P, NT * TOP])
        count = ctx.enter_context(nc.psum_tensor("count", [P, E], F32))
        const_ready, counted, planned = (Signal(ctx, nc, n, 0) for n in ("const_ready3", "counted", "planned"))
        out, back = Signal(ctx, nc, "plan_out", 0), Signal(ctx, nc, "plan_back", 0)
        step = Chain(ctx, nc, "dve_step3")
        block = ctx.enter_context(nc.Block())

        @block.gpsimd
        def _(pool):
            made = 0
            for make in (lambda: pool.memset(ones[:], 1.0), lambda: pool.memset(zero[:], 0.0),
                         lambda: pool.iota(ie[:], pattern=[[1, E]], base=0, channel_multiplier=0),
                         lambda: pool.iota(ib[:], pattern=[[1, 1]], base=0, channel_multiplier=1),
                         lambda: pool.memset(col[:], 0.0)):
                make().then_inc(const_ready.sem, 1)
                made += 1
                pool.wait_ge(const_ready.sem, made)

        @block.tensor
        def _(pe):
            pe.wait_ge(const_ready.sem, 5)
            pe.matmul(count[:], ones[:], seen[:], start=True, stop=True).then_inc(counted.sem, 1)

        @block.vector
        def _(v):
            def chained(ins):
                step.step(ins)
                step.wait(v)

            def total(dst, src):
                chained(v.tensor_reduce(dst, src, AX.X, ALU.add))

            v.wait_ge(const_ready.sem, 5)
            step.step(v.tensor_copy(io[:], ie[:]))
            step.step(v.tensor_copy(block_no[:], ib[:]))
            v.wait_ge(counted.sem, 1)
            chained(v.tensor_scalar(cnt_i[:], count[:], float(P - 1), None, ALU.add))
            chained(v.tensor_scalar(nb_i[:], cnt_i[:], 7, None, ALU.arith_shift_right))
            chained(v.tensor_copy(nb[:], nb_i[:]))
            chained(v.tensor_tensor_scan(end[:], nb[:], zero[:], 0.0, ALU.add, ALU.add))
            chained(v.tensor_tensor(start[:], end[:], nb[:], ALU.subtract))
            chained(v.tensor_scalar(ends[:], end[:], block_no[:, 0:1], None, ALU.is_le))
            total(f[:, 0:1], ends[:])
            chained(v.tensor_scalar(f[:, 0:1], f[:, 0:1], float(E - 1), None, ALU.min))
            chained(v.tensor_scalar(hot[:], io[:], f[:, 0:1], None, ALU.is_equal))
            chained(v.tensor_tensor(tmp[:], hot[:], start[:], ALU.mult))
            total(f[:, 1:2], tmp[:])
            chained(v.tensor_scalar(tmp[:], nb[:], 0.0, None, ALU.is_gt))
            chained(v.tensor_tensor_scan(past[:], tmp[:], zero[:], 0.0, ALU.add, ALU.add))
            chained(v.tensor_tensor(tmp[:], tmp[:], ends[:], ALU.mult))
            total(f[:, 7:8], tmp[:])
            chained(v.tensor_scalar(f[:, 6:7], past[:, E - 1:E], -1.0, None, ALU.add))
            chained(v.tensor_tensor(col[:, RUN:RUN + 1], f[:, 7:8], f[:, 6:7], ALU.min))
            chained(v.tensor_scalar(tmp[:], past[:], block_no[:, 0:1], None, ALU.is_le))
            total(f[:, 8:9], tmp[:])
            chained(v.tensor_scalar(col[:, NTH:NTH + 1], f[:, 8:9], float(E - 1), None, ALU.min))
            chained(v.tensor_tensor(f[:, 4:5], block_no[:], f[:, 1:2], ALU.is_equal))
            chained(v.tensor_tensor(f[:, 5:6], block_no[:], end[:, E - 1:E], ALU.is_lt))
            chained(v.tensor_tensor(f[:, 4:5], f[:, 4:5], f[:, 5:6], ALU.mult))
            chained(v.tensor_tensor(f[:, 5:6], f[:, 7:8], f[:, 6:7], ALU.is_lt))
            chained(v.tensor_tensor(col[:, SPLIT:SPLIT + 1], f[:, 4:5], f[:, 5:6], ALU.mult))
            chained(v.tensor_scalar(f[:, 5:6], f[:, 7:8], 2.0, None, ALU.add))
            chained(v.tensor_tensor(f[:, 5:6], f[:, 5:6], f[:, 6:7], ALU.is_lt))
            chained(v.tensor_tensor(col[:, LOAD:LOAD + 1], f[:, 4:5], f[:, 5:6], ALU.mult))
            chained(v.tensor_tensor(f[:, 6:7], block_no[:], f[:, 1:2], ALU.subtract))
            chained(v.tensor_scalar(f[:, 6:7], f[:, 6:7], float(T // P), float(P), ALU.min, ALU.mult))
            chained(v.scalar_tensor_tensor(out=col[:, ROW:ROW + 1], in0=f[:, 0:1], scalar=float(LIST),
                                           in1=f[:, 6:7], op0=ALU.mult, op1=ALU.add))
            chained(v.tensor_scalar(iters[:], end[:, E - 1:E], float(U_BLK - 1), None, ALU.add))
            chained(v.tensor_scalar(iters[:], iters[:], U_SHIFT, None, ALU.arith_shift_right))
            chained(v.tensor_copy(col[:, ITERS:ITERS + 1], iters[:]))
            planned.by(v.tensor_copy(tab[:], col[:]))
            sl = slots[:].rearrange("p t (s k) -> p t s k", k=TOP)
            chained(v.tensor_copy(row[:].rearrange("p (t k) -> p t k", k=TOP), sl[:, :, 0]))
            chained(v.tensor_tensor(big[:], row[:].unsqueeze(2).to_broadcast([P, NT * TOP, E]),
                                    io[:].unsqueeze(1).to_broadcast([P, NT * TOP, E]), ALU.is_equal))
            chained(v.tensor_tensor(big[:], big[:], start[:].unsqueeze(1).to_broadcast([P, NT * TOP, E]), ALU.mult))
            chained(v.tensor_reduce(row[:], big[:], AX.X, ALU.add))
            chained(v.scalar_tensor_tensor(out=dest[:], in0=row[:].rearrange("p (t k) -> p t k", k=TOP),
                                           scalar=float(P), in1=sl[:, :, 1], op0=ALU.mult, op1=ALU.add))

        @block.sync
        def _(sp):
            sp.wait_ge(planned.sem, 1)
            sp.dma_start(plan_dram, tab[:]).then_inc(out.sem, 16)
            sp.wait_ge(out.sem, 16)
            sp.dma_start(plan[0:1, :], plan_dram.rearrange("(a b) c -> a (b c)", a=1)).then_inc(back.sem, 16)
            sp.wait_ge(back.sem, 16)


def run_experts(nc, plan, lists, u_rows, w_gate, w_up, w_down, y_rows):
    with ExitStack() as ctx:
        def sb(name, shape, dt=F32):
            return ctx.enter_context(nc.sbuf_tensor(name, shape, dt))

        def ps(name, shape):
            return ctx.enter_context(nc.psum_tensor(name, shape, F32))

        U = U_BLK
        NI = NBLK // U

        def sig(name, per=U, base=0, step=1):
            return Signal(ctx, nc, name, per, base, step)

        gu_raw, dn_raw = sb("gu_raw", [P, 2, KD, 2 * F]), sb("dn_raw", [P, 2, FC, D])
        gu_hi, gu_lo = (sb(n, [P, 2, KD, 2 * F], F32R) for n in ("gu_hi", "gu_lo"))
        dn_hi, dn_lo = (sb(n, [P, 2, FC, D], F32R) for n in ("dn_hi", "dn_lo"))
        idx = [sb(f"idx{b}", [P, 1], I32) for b in range(U)]
        xg = [sb(f"xg{b}", [P, D]) for b in range(U)]
        x_hi, x_lo = (sb(n, [P, 2, KD, P], F32R) for n in ("x_hi", "x_lo"))
        act_g, hid = sb("act_g", [P, F]), sb("hid", [P, F])
        h_hi, h_lo = (sb(n, [P, FC, P], F32R) for n in ("h_hi", "h_lo"))
        ys = sb("ys", [P, U, D])
        idn = sb("idn_m", [P, P])
        no_rows = sb("no_rows", [P, D])
        tps = ps("tps_m", [P, KD, P])
        gu = [ps(f"gu{b}", [P, 2 * F]) for b in range(2)]
        hp = ps("hp", [P, FC, P])
        yp = [ps(f"yp{n}", [P, D // 2]) for n in range(2)]

        GU_PARTS, DN_PARTS = 4, FC
        KS = KD // GU_PARTS
        const_ready = sig("const_ready4", 0)
        raw_in = [sig(f"raw_in{q}", 0) for q in range(2)]
        gu_hi_done, gu_lo_done, dn_hi_done, dn_lo_done = (sig(n, 0) for n in ("gu_hi_done", "gu_lo_done",
                                                                              "dn_hi_done", "dn_lo_done"))
        idx_in = [sig(f"idx_in{b}", 1, 1, 16) for b in range(U)]
        gathered = [sig(f"gathered{b}", 1, 1, 16) for b in range(U)]
        turned, x_hi_done, x_lo_done = sig("turned", U, 2), sig("x_hi_done", U, 2), sig("x_lo_done", U, 2)
        gated, silu_done, hid_done = sig("gated_m", U, 1), sig("silu_done"), sig("hid_done")
        h_turned, h_hi_done, h_lo_done = sig("h_turned"), sig("h_hi_done"), sig("h_lo_done")
        down_done = sig("down_done", 2 * U)
        y_taken = [sig(f"y_taken{n}", U, 1) for n in range(2)]
        y_stored = [sig(f"y_stored{b}", 1, 1, 16) for b in range(U)]
        filled = sig("filled", 0)
        begun = sig("begun_m", 0)
        block = ctx.enter_context(nc.Block())
        plan_rows = plan[0:1, :].rearrange("a (b c) -> a b c", c=COLS)
        y_blocks = y_rows.rearrange("(b p) n -> b p n", p=P)
        wg_rows, wu_rows = (w[0].rearrange("e (k p) n -> e p k n", p=P) for w in (w_gate, w_up))
        wd_rows = w_down[0].rearrange("e (c p) n -> e p c n", p=P)

        def planned(eng, blk, c, top, low=0):
            at = bass.ds(blk, 1) if not isinstance(blk, int) else slice(blk, blk + 1)
            return eng.value_load(plan_rows[:, at, c], min_val=low, max_val=top)

        def iterations(eng):
            return planned(eng, 0, ITERS, NI, T * TOP // P // U)

        def part(w, buf, k, n):
            return w[:, bass.ds(buf, 1), k:k + n].rearrange("p one k n -> p (one k) n")

        def row(w, buf, k, cut):
            return w[:, bass.ds(buf, 1), k, cut].rearrange("p one n -> p (one n)")

        @block.sync
        def _(sp):
            def load_index(blk, b):
                start = planned(sp, blk, ROW, E * LIST - P)
                idx_in[b].by(sp.dma_start(idx[b][:], lists[bass.ds(start, P), :]))

            def load_weights(e, q):
                for dst, src in ((gu_raw[:, q, :, 0:F], wg_rows), (gu_raw[:, q, :, F:], wu_rows),
                                 (dn_raw[:, q], wd_rows)):
                    sp.dma_start(dst, src[e]).then_inc(raw_in[q].sem, 16)

            for b in range(2):
                load_index(b, b)
            load_weights(planned(sp, 0, NTH, E - 1), 0)
            for b in range(2, U):
                load_index(b, b)
            load_weights(planned(sp, 1, NTH, E - 1), 1)
            third = planned(sp, 2, NTH, E - 1)
            sp.wait_ge(gu_lo_done.sem, GU_PARTS)
            sp.wait_ge(dn_lo_done.sem, DN_PARTS)
            sp.sem_inc(begun.sem, 1)
            load_weights(third, 0)
            for b in range(U):
                sp.sem_inc(y_stored[b].sem, 16)
            sp.wait_ge(const_ready.sem, 3)
            n_iter = iterations(sp)
            with sp.Fori(0, NI) as g:
                with sp.If(g < n_iter):
                    for b in range(U):
                        gathered[b].wait(sp, g, 0)
                        sp.sem_inc(begun.sem, 1)
                        load_index(g * U + (b + U), b)
                        for n in range(2):
                            y_taken[n].wait(sp, g, b + 1)
                        sp.sem_inc(begun.sem, 1)
                        y_stored[b].by(sp.dma_start(y_blocks[g * U + b], ys[:, b]))
                        load = planned(sp, g * U + b, LOAD, 1)
                        with sp.If(load):
                            run = planned(sp, g * U + b, RUN, E - 4)
                            sp.wait_ge(gu_lo_done.sem, run * GU_PARTS + 2 * GU_PARTS)
                            sp.wait_ge(dn_lo_done.sem, run * DN_PARTS + 2 * DN_PARTS)
                            sp.sem_inc(begun.sem, 1)
                            expert = planned(sp, run + 3, NTH, E - 1)
                            with sp.If(sp.snap(run % 2) == 0):
                                load_weights(expert, 1)
                            with sp.Else():
                                load_weights(expert, 0)
                        with sp.If(g * U + (n_iter * U + b) < NBLK):
                            sp.dma_start(y_blocks[sp.snap((g * U + (n_iter * U + b)) % NBLK)], no_rows[:]
                                         ).then_inc(filled.sem, 16)
                        with sp.Else():
                            sp.sem_inc(filled.sem, 16)
            sp.wait_ge(raw_in[0].sem, 96)
            sp.wait_ge(filled.sem, n_iter * (16 * U))
            for b in range(U):
                sp.wait_ge(y_stored[b].sem, n_iter * 16 + 16)
                sp.wait_ge(idx_in[b].sem, n_iter * 16 + 16)
                sp.sem_inc(begun.sem, 1)

        @block.gpsimd
        def _(pool):
            pool.memset(idn[:], 0.0).then_inc(const_ready.sem, 1)
            pool.wait_ge(const_ready.sem, 1)
            pool.affine_select(out=idn[:], in_=idn[:], compare_op=ALU.not_equal, fill=1.0, base=0,
                               pattern=[[-1, P]], channel_multiplier=1).then_inc(const_ready.sem, 1)
            pool.wait_ge(const_ready.sem, 2)
            pool.memset(no_rows[:], 0.0).then_inc(const_ready.sem, 1)

            def gather(b):
                pool.sem_inc(begun.sem, 1)
                gathered[b].by(pool.indirect_dma_start(xg[b][:], None, u_rows,
                                                       bass.IndirectOffsetOnAxis(ap=idx[b][:, 0:1], axis=0)))

            def split_dn_lo(run, buf):
                for c in range(DN_PARTS):
                    pool.wait_ge(dn_hi_done.sem, run * DN_PARTS + (c + 1))
                    pool.tensor_tensor(part(dn_lo, buf, c, 1), part(dn_raw, buf, c, 1),
                                       part(dn_hi, buf, c, 1).bitcast(F32), ALU.subtract
                                       ).then_inc(dn_lo_done.sem, 1)

            for b in range(U):
                idx_in[b].wait(pool, -1, 1)
                gather(b)
            split_dn_lo(0, 0)
            n_iter = iterations(pool)
            with pool.Fori(0, NI) as g:
                with pool.If(g < n_iter):
                    for b in range(U):
                        idx_in[b].wait(pool, g, 1)
                        turned.wait(pool, g, b - 1)
                        gather(b)
                        split = planned(pool, g * U + b, SPLIT, 1)
                        with pool.If(split):
                            run = planned(pool, g * U + b, RUN, E - 1)
                            split_dn_lo(run + 1, pool.snap((run + 1) % 2, min_val=0, max_val=1))
            for b in range(U):
                pool.wait_ge(gathered[b].sem, n_iter * 16 + 16)
                pool.sem_inc(begun.sem, 1)

        @block.tensor
        def _(pe):
            def turn(g, b):
                gathered[b % U].wait(pe, g, b // U)
                for k in range(KD):
                    ins = pe.transpose(tps[:, k], xg[b % U][:, k * P:(k + 1) * P], idn[:])
                turned.by(ins)

            def gate_up(b, buf, k0):
                for k in range(k0, k0 + KD // 2):
                    ins = product3(pe, gu[b % 2][:], x_hi[:, b % 2, k], x_lo[:, b % 2, k],
                                   row(gu_hi, buf, k, slice(0, 2 * F)), row(gu_lo, buf, k, slice(0, 2 * F)),
                                   k == 0, k == KD - 1)
                return ins

            pe.wait_ge(const_ready.sem, 2)
            turn(0, 0)
            pe.wait_ge(x_lo_done.sem, 1)
            turn(0, 1)
            pe.wait_ge(gu_lo_done.sem, GU_PARTS)
            gate_up(0, 0, 0)
            gated.by(gate_up(0, 0, KD // 2))
            n_iter = iterations(pe)
            with pe.Fori(0, NI) as g:
                with pe.If(g < n_iter):
                    for b in range(U):
                        if b == 0:
                            run = planned(pe, g * U, RUN, E - 1)
                            buf = pe.snap(run % 2, min_val=0, max_val=1)
                        nrun = planned(pe, g * U + (b + 1), RUN, E - 1)
                        nbuf = pe.snap(nrun % 2, min_val=0, max_val=1)
                        pe.wait_ge(gu_lo_done.sem, nrun * GU_PARTS + GU_PARTS)
                        x_lo_done.wait(pe, g, b)
                        gate_up(b + 1, nbuf, 0)
                        hid_done.wait(pe, g, b + 1)
                        for c in range(FC):
                            ins = pe.transpose(hp[:, c], hid[:, c * P:(c + 1) * P], idn[:])
                        h_turned.by(ins)
                        turn(g, b + 2)
                        gated.by(gate_up(b + 1, nbuf, KD // 2))
                        pe.wait_ge(dn_lo_done.sem, run * DN_PARTS + DN_PARTS)
                        h_lo_done.wait(pe, g, b + 1)
                        for n in range(2):
                            y_taken[n].wait(pe, g, b)
                            cut = slice(n * (D // 2), (n + 1) * (D // 2))
                            for c in range(FC):
                                ins = product3(pe, yp[n][:], h_hi[:, c], h_lo[:, c], row(dn_hi, buf, c, cut),
                                               row(dn_lo, buf, c, cut), c == 0, c == FC - 1)
                            down_done.by(ins)
                        run, buf = nrun, nbuf

        @block.scalar
        def _(a):
            def take_x(b):
                x_hi_done.by(a.activation(x_hi[:, b % 2], tps[:], ACT.Copy))

            def split_gu_hi(g, b):
                if b is None:
                    buf = 0
                    a.wait_ge(raw_in[0].sem, 48)
                else:
                    run = planned(a, g * U + b, RUN, E - 1)
                    buf = a.snap((run + 1) % 2, min_val=0, max_val=1)
                    even, odd = (a.snap((run + n) // 2) for n in (1, 2))
                    a.wait_ge(raw_in[0].sem, even * 48 + 48)
                    a.wait_ge(raw_in[1].sem, odd * 48)
                    if b > 0:
                        down_done.wait(a, g, 2 * b)
                    else:
                        y_taken[1].wait(a, g, 0)
                for n in range(GU_PARTS):
                    a.activation(part(gu_hi, buf, n * KS, KS), part(gu_raw, buf, n * KS, KS), ACT.Copy
                                 ).then_inc(gu_hi_done.sem, 1)

            def split_dn_hi(buf):
                for c in range(DN_PARTS):
                    a.activation(part(dn_hi, buf, c, 1), part(dn_raw, buf, c, 1), ACT.Copy).then_inc(dn_hi_done.sem, 1)

            def take_y(g, b):
                down_done.wait(a, g, 2 * b + 1)
                y_stored[b].wait(a, g, 0)
                y_taken[0].by(a.activation(ys[:, b, 0:D // 2], yp[0][:], ACT.Copy))

            for b in range(2):
                a.wait_ge(turned.sem, b + 1)
                take_x(b)
            split_gu_hi(0, None)
            split_dn_hi(0)
            a.sem_inc(y_taken[0].sem, 1)
            n_iter = iterations(a)
            with a.Fori(0, NI) as g:
                with a.If(g < n_iter):
                    for b in range(U):
                        split = planned(a, g * U + b, SPLIT, 1)
                        gated.wait(a, g, b)
                        silu_done.by(a.activation(act_g[:], gu[b % 2][:, 0:F], ACT.Silu))
                        if b > 0:
                            take_y(g, b - 1)
                        with a.If(split):
                            split_gu_hi(g, b)
                        h_turned.wait(a, g, b + 1)
                        h_hi_done.by(a.activation(h_hi[:], hp[:], ACT.Copy))
                        turned.wait(a, g, b + 1)
                        take_x(b)
                        with a.If(split):
                            run = planned(a, g * U + b, RUN, E - 1)
                            split_dn_hi(a.snap((run + 1) % 2, min_val=0, max_val=1))
                        if b == U - 1:
                            take_y(g, b)

        @block.vector
        def _(v):
            def take_x(g, b):
                x_hi_done.wait(v, g, b + 1 - 2)
                x_lo_done.by(v.tensor_tensor(x_lo[:, b % 2], tps[:], x_hi[:, b % 2].bitcast(F32), ALU.subtract))

            def split_gu_lo(run, buf):
                for n in range(GU_PARTS):
                    v.wait_ge(gu_hi_done.sem, run * GU_PARTS + (n + 1))
                    v.tensor_tensor(part(gu_lo, buf, n * KS, KS), part(gu_raw, buf, n * KS, KS),
                                    part(gu_hi, buf, n * KS, KS).bitcast(F32), ALU.subtract
                                    ).then_inc(gu_lo_done.sem, 1)

            def take_y(g, b):
                down_done.wait(v, g, 2 * b + 2)
                y_stored[b].wait(v, g, 0)
                y_taken[1].by(v.tensor_copy(ys[:, b, D // 2:], yp[1][:]))

            for b in range(2):
                take_x(0, b)
            split_gu_lo(0, 0)
            v.sem_inc(y_taken[1].sem, 1)
            n_iter = iterations(v)
            with v.Fori(0, NI) as g:
                with v.If(g < n_iter):
                    for b in range(U):
                        split = planned(v, g * U + b, SPLIT, 1)
                        silu_done.wait(v, g, b + 1)
                        hid_done.by(v.tensor_tensor(hid[:], act_g[:], gu[b % 2][:, F:], ALU.mult))
                        if b > 0:
                            take_y(g, b - 1)
                        with v.If(split):
                            run = planned(v, g * U + b, RUN, E - 1)
                            split_gu_lo(run + 1, v.snap((run + 1) % 2, min_val=0, max_val=1))
                        h_hi_done.wait(v, g, b + 1)
                        h_lo_done.by(v.tensor_tensor(h_lo[:], hp[:], h_hi[:].bitcast(F32), ALU.subtract))
                        take_x(g, b + 2)
                        if b == U - 1:
                            take_y(g, b)


def combine(nc, h_rows, y_rows, slots, dest, final_g, out):
    with ExitStack() as ctx:
        def sb(name, shape, dt=F32):
            return ctx.enter_context(nc.sbuf_tensor(name, shape, dt))

        def sig(name, per=2, base=0, step=1):
            return Signal(ctx, nc, name, per, base, step)

        NBUF = 4
        fg, eps = sb("fg", [P, D]), sb("eps_f", [P, 1])
        ht = [sb(f"hf{b}", [P, D]) for b in range(NBUF)]
        y = [[sb(f"y{k}_{b}", [P, D]) for k in range(TOP)] for b in range(NBUF)]
        at = [sb(f"at_f{b}", [P, TOP], U32) for b in range(NBUF)]
        sq = [sb(f"sq_f{b}", [P, D]) for b in range(2)]
        wt = sb("wt_f", [P, NBUF, TOP])
        r = sb("r_f", [P, NBUF])
        consts_in, const_ready = sig("consts_in5", 0), sig("const_ready5", 0)
        h_in = [sig(f"hf_in{b}", 1, 0, 16) for b in range(NBUF)]
        y_in = [sig(f"yf_in{b}", 1, 0, 32) for b in range(NBUF)]
        index_done = [sig(f"index_done{b}", 1, 0, 1) for b in range(NBUF)]
        squared, rooted = sig("squared_f", NBUF), sig("rooted_f", NBUF)
        summed, scaled = sig("summed_f", NBUF), sig("scaled_f", NBUF, NBUF)
        stored = [sig(f"stored_f{b}", 1, 1, 16) for b in range(NBUF)]
        begun = sig("begun_f", 0)
        STEPS = 3
        step = Chain(ctx, nc, "dve_step5", NBUF * STEPS)
        block = ctx.enter_context(nc.Block())
        h_tiles, out_tiles = (t.rearrange("(t p) n -> t p n", p=P) for t in (h_rows, out))
        NI = NT // NBUF

        @block.sync
        def _(sp):
            sp.dma_start(fg[:], final_g.partition_broadcast(P)).then_inc(consts_in.sem, 16)
            for b in range(NBUF):
                sp.sem_inc(stored[b].sem, 16)
            with sp.Fori(0, NI) as g:
                for b in range(NBUF):
                    stored[b].wait(sp, g, 0)
                    sp.sem_inc(begun.sem, 1)
                    h_in[b].by(sp.dma_start(ht[b][:], h_tiles[g * NBUF + b]))
            for b in range(NBUF):
                sp.wait_ge(stored[b].sem, 16 * (NI + 1))

        @block.gpsimd
        def _(pool):
            pool.memset(eps[:], EPS).then_inc(const_ready.sem, 1)
            with pool.Fori(0, NI) as g:
                for b in range(NBUF):
                    scaled.wait(pool, g, b + 1 - NBUF)
                    index_done[b].by(pool.tensor_copy(at[b][:], dest[:, bass.ds(g * NBUF + b, 1)]
                                                      .rearrange("p one k -> p (one k)")))
                    index_done[b].wait(pool, g, 1)
                    pool.sem_inc(begun.sem, 1)
                    for k in range(TOP):
                        pool.indirect_dma_start(y[b][k][:], None, y_rows,
                                                bass.IndirectOffsetOnAxis(ap=at[b][:, k:k + 1], axis=0)
                                                ).then_inc(y_in[b].sem, 16)

        @block.scalar
        def _(a):
            a.wait_ge(const_ready.sem, 1)
            with a.Fori(0, NI) as g:
                for b in range(NBUF):
                    summed.wait(a, g, b + 1)
                    squared.by(a.activation(sq[b % 2][:], ht[b][:], ACT.Square, accum_out=r[:, b:b + 1]))
                    squared.wait(a, g, b + 1)
                    rooted.by(a.activation(r[:, b:b + 1], r[:, b:b + 1], ACT.Sqrt, bias=eps[:, 0:1], scale=1.0 / D))
                    if b > 0:
                        scaled.wait(a, g, b)
                        stored[b - 1].by(a.dma_start(out_tiles[g * NBUF + (b - 1)], ht[b - 1][:]))
                scaled.wait(a, g, NBUF)
                stored[NBUF - 1].by(a.dma_start(out_tiles[g * NBUF + (NBUF - 1)], ht[NBUF - 1][:]))

        @block.vector
        def _(v):
            def chained(ins):
                step.step(ins)
                step.wait(v)

            v.wait_ge(consts_in.sem, 16)
            v.sem_inc(scaled.sem, NBUF)
            with v.Fori(0, NI) as g:
                step.enter(g)

                def add(b):
                    h_in[b].wait(v, g, 1)
                    y_in[b].wait(v, g, 1)
                    chained(v.tensor_copy(wt[:, b], slots[:, bass.ds(g * NBUF + b, 1), 4:6]
                                          .rearrange("p one k -> p (one k)")))
                    chained(v.scalar_tensor_tensor(out=ht[b][:], in0=y[b][0][:], scalar=wt[:, b, 0:1],
                                                   in1=ht[b][:], op0=ALU.mult, op1=ALU.add))
                    summed.by(v.scalar_tensor_tensor(out=ht[b][:], in0=y[b][1][:], scalar=wt[:, b, 1:2],
                                                     in1=ht[b][:], op0=ALU.mult, op1=ALU.add))

                def scale(b):
                    rooted.wait(v, g, b + 1)
                    chained(v.reciprocal(r[:, b:b + 1], r[:, b:b + 1]))
                    scaled.by(v.scalar_tensor_tensor(out=ht[b][:], in0=ht[b][:], scalar=r[:, b:b + 1], in1=fg[:],
                                                     op0=ALU.mult, op1=ALU.mult))

                for b in range(NBUF):
                    add(b)
                    if b > 0:
                        scale(b - 1)
                scale(NBUF - 1)
                step.leave()


def build(nc, x, out, norm1_g, w_in, conv_w, conv_b, w_rg, b_rg, w_ig, b_ig, lru_lambda, attn_sinks,
          rnn_out_g, attn_out_g, w_out, norm2_g, w_group_router, w_expert_router, w_gate, w_up, w_down, final_g):
    def dram(name, shape, dt=F32):
        return nc.dram_tensor(name, shape, dt).ap()

    mixT = dram("mixT", (2 * RC, P, T))
    h_rows, u_rows = dram("h_rows", (T, D)), dram("u_rows", (T, D))
    lists = dram("lists", (E * LIST, 1), I32)
    plan_dram = dram("plan_dram", (P, COLS), I32)
    y_rows = dram("y_rows", (NBLK * P, D))
    xr, outr = x[0], out[0]
    project_and_mix(nc, xr, norm1_g, w_in, conv_w, conv_b, w_rg, b_rg, w_ig, b_ig, lru_lambda, attn_sinks, mixT)
    with (nc.sbuf_tensor("slots", [P, NT, 3 * TOP], F32) as slots,
          nc.sbuf_tensor("dest", [P, NT, TOP], U32) as dest):
        with (nc.sbuf_tensor("seen_out", [P, E], BF16) as seen,
              nc.sbuf_tensor("plan", [1, P * COLS], I32) as plan):
            project_out(nc, xr, mixT, rnn_out_g, attn_out_g, w_out, norm2_g, w_group_router, w_expert_router,
                        h_rows, u_rows, lists, slots, seen)
            plan_blocks(nc, seen, slots, plan_dram, plan, dest)
            run_experts(nc, plan, lists, u_rows, w_gate, w_up, w_down, y_rows)
        combine(nc, h_rows, y_rows, slots, dest, final_g, outr)


_INS = ['x', 'norm1_g', 'w_in', 'conv_w', 'conv_b', 'w_rg', 'b_rg', 'w_ig', 'b_ig', 'lru_lambda', 'attn_sinks',
        'rnn_out_g', 'attn_out_g', 'w_out', 'norm2_g', 'w_group_router', 'w_expert_router', 'w_gate', 'w_up',
        'w_down', 'final_g']


def kernel(**inputs):
    import concourse.bacc as _bacc
    from concourse.bass_utils import run_bass_kernel_spmd as _run

    nc = _bacc.Bacc("TRN2", target_bir_lowering=False, num_devices=1)
    arrays, aps = {}, {}
    for name in _INS:
        a = np.ascontiguousarray(inputs[name])
        arrays[f"in_{name}"] = a
        aps[name] = nc.dram_tensor(f"in_{name}", a.shape, mybir.dt.from_np(a.dtype), kind="ExternalInput").ap()
    x = aps.pop("x")
    out = nc.dram_tensor("out_dram", (1, T, D), F32, kind="ExternalOutput").ap()
    build(nc, x, out, **aps)
    r = _run(nc, [arrays], core_ids=[0])
    return r.results[0]["out_dram"]
```
